# Optimizing a Trainium2 kernel written in Bass

```python
import math
import jax, jax.numpy as jnp
from jax import lax
import numpy as np

D_MODEL = 1024
BATCH = 1
SEQ = 1024
DEPTH = 1
DEC_BATCH = 8
DEC_SEQ = 1
PAST_LEN = 256
PAGE_SIZE = 128

SSM_INNER = 2 * D_MODEL
SSM_HEAD_DIM = 64
SSM_HEADS = SSM_INNER // SSM_HEAD_DIM
SSM_GROUPS = 4
SSM_STATE = 128
SSM_CONV = 4
SSM_CHUNK = 128
SSM_GN = SSM_GROUPS * SSM_STATE
SSM_CONV_DIM = SSM_INNER + 2 * SSM_GN
ATTN_HEAD_DIM = 64
ATTN_HEADS = D_MODEL // ATTN_HEAD_DIM
ATTN_KV_HEADS = 4
ATTN_WIDTH = ATTN_HEADS * ATTN_HEAD_DIM
IDX_HEADS = 4
IDX_DIM = 64
IDX_WEIGHT_SCALE = IDX_HEADS ** -0.5 * IDX_DIM ** -0.5
TOPK_MAX = 256
Q_BLOCK = 128
ROPE_THETA = 10000.0
FFN_HIDDEN = ((8 * D_MODEL + 3 * 256 - 1) // (3 * 256)) * 256
NORM_EPS = 1e-6
IN_SPLITS = (SSM_INNER, SSM_INNER, SSM_GN, SSM_GN, SSM_HEADS,
             ATTN_WIDTH, ATTN_KV_HEADS * ATTN_HEAD_DIM, ATTN_KV_HEADS * ATTN_HEAD_DIM,
             IDX_HEADS * IDX_DIM, IDX_DIM, IDX_HEADS, D_MODEL, D_MODEL)
IN_DIM = sum(IN_SPLITS)

kernel_name = 'ssd_dsa_gated_hybrid_step'

def split_points(widths):
    pts, acc = [], 0
    for w in widths[:-1]:
        acc += w
        pts.append(acc)
    return pts

def rmsnorm(x, g):
    xf = x.astype(jnp.float32)
    y = xf * lax.rsqrt(jnp.mean(xf * xf, axis=-1, keepdims=True) + NORM_EPS)
    return (y * g.astype(jnp.float32)).astype(x.dtype)

def rope(x, pos):
    half = x.shape[-1] // 2
    inv = ROPE_THETA ** (-jnp.arange(half, dtype=jnp.float32) / half)
    ang = pos.astype(jnp.float32)[:, None] * inv[None, :]
    shape = (1, pos.shape[0]) + (1,) * (x.ndim - 3) + (half,)
    cos = jnp.cos(ang).reshape(shape).astype(x.dtype)
    sin = jnp.sin(ang).reshape(shape).astype(x.dtype)
    x1, x2 = x[..., :half], x[..., half:]
    return jnp.concatenate([x1 * cos - x2 * sin, x2 * cos + x1 * sin], axis=-1)

def causal_conv(xbc, conv_state, w, b):
    L = xbc.shape[1]
    full = jnp.concatenate([conv_state.astype(xbc.dtype), xbc], axis=1)
    out = sum(full[:, i:i + L] * w[i] for i in range(SSM_CONV)) + b
    return jax.nn.silu(out), full[:, -(SSM_CONV - 1):]

def ssd_scan(x, dt, A, Bm, Cm, init):
    b, L = x.shape[:2]
    Q = min(SSM_CHUNK, L)
    nc = -(-L // Q)
    pad = nc * Q - L
    if pad:
        pw = ((0, 0), (0, pad), (0, 0), (0, 0))
        x, Bm, Cm = jnp.pad(x, pw), jnp.pad(Bm, pw), jnp.pad(Cm, pw)
        dt = jnp.pad(dt, ((0, 0), (0, pad), (0, 0)))
    G, R, P, N = SSM_GROUPS, SSM_HEADS // SSM_GROUPS, SSM_HEAD_DIM, SSM_STATE
    x = x.reshape(b, nc, Q, G, R, P)
    dt = dt.reshape(b, nc, Q, G, R)
    Bm = Bm.reshape(b, nc, Q, G, N)
    Cm = Cm.reshape(b, nc, Q, G, N)
    Acs = jnp.cumsum(dt * A.reshape(G, R), axis=2)
    tri = jnp.tril(jnp.ones((Q, Q), dtype=bool))
    seg = Acs[:, :, :, None] - Acs[:, :, None, :]
    decay = jnp.exp(jnp.where(tri[None, None, :, :, None, None], seg, -jnp.inf))
    cb = jnp.einsum('bclgn,bcsgn->bclsg', Cm, Bm)
    m = cb[..., None] * decay * dt[:, :, None]
    y_diag = jnp.einsum('bclsgr,bcsgrp->bclgrp', m, x)
    decay_end = jnp.exp(Acs[:, :, -1:] - Acs)
    states = jnp.einsum('bclgn,bclgrp->bcgrpn', Bm, x * (decay_end * dt)[..., None])
    chunk_decay = jnp.exp(Acs[:, :, -1])

    def step(s, inp):
        st, dec = inp
        return s * dec[..., None, None] + st, s

    final, s_in = lax.scan(step, init.reshape(b, G, R, P, N),
                           (jnp.moveaxis(states, 1, 0), jnp.moveaxis(chunk_decay, 1, 0)))
    s_in = jnp.moveaxis(s_in, 0, 1)
    y_off = jnp.einsum('bclgn,bcgrpn->bclgrp', Cm, s_in) * jnp.exp(Acs)[..., None]
    y = (y_diag + y_off).reshape(b, nc * Q, SSM_HEADS, P)[:, :L]
    return y, final.reshape(b, SSM_HEADS, P, N)

def ssm_branch(z, xs, bm, cm, dtr, ssm_state, dt_bias, a_log, d_skip, norm_g):
    B, L, _ = xs.shape
    f32 = jnp.float32
    xh = xs.astype(f32).reshape(B, L, SSM_HEADS, SSM_HEAD_DIM)
    dt = jax.nn.softplus(dtr.astype(f32) + dt_bias.astype(f32))
    A = -jnp.exp(a_log.astype(f32))
    y, new_state = ssd_scan(xh, dt, A,
                            bm.astype(f32).reshape(B, L, SSM_GROUPS, SSM_STATE),
                            cm.astype(f32).reshape(B, L, SSM_GROUPS, SSM_STATE),
                            ssm_state.astype(f32))
    y = y + d_skip.astype(f32)[:, None] * xh
    y = y.reshape(B, L, SSM_INNER) * jax.nn.silu(z.astype(f32))
    yg = y.reshape(B, L, SSM_GROUPS, SSM_INNER // SSM_GROUPS)
    yg = yg * lax.rsqrt(jnp.mean(yg * yg, axis=-1, keepdims=True) + NORM_EPS)
    y = yg.reshape(B, L, SSM_INNER) * norm_g.astype(f32)
    return y.astype(xs.dtype), new_state.astype(xs.dtype)

def dsa_select(qi, wts, ki, qpos, topk):
    L = ki.shape[1]
    s = jax.nn.relu(jnp.einsum('bqhd,bsd->bqhs', qi.astype(jnp.float32), ki.astype(jnp.float32)))
    score = jnp.einsum('bqhs,bqh->bqs', s, wts.astype(jnp.float32))
    kpos = jnp.arange(L, dtype=jnp.int32)
    score = jnp.where(kpos[None, None, :] <= qpos[None, :, None], score, -jnp.inf)
    _, idx = lax.top_k(score, topk)
    valid = idx <= qpos[None, :, None]
    return idx, valid

def sparse_attend(q, k_sel, v_sel, valid):
    B, Tq = q.shape[:2]
    logits = jnp.einsum('bqgrd,bqkgd->bqgrk', q.astype(jnp.float32),
                        k_sel.astype(jnp.float32)) * (ATTN_HEAD_DIM ** -0.5)
    logits = jnp.where(valid[:, :, None, None, :], logits, -jnp.inf)
    p = jax.nn.softmax(logits, axis=-1)
    out = jnp.einsum('bqgrk,bqkgd->bqgrd', p, v_sel.astype(jnp.float32))
    return out.reshape(B, Tq, ATTN_WIDTH).astype(q.dtype)

def dsa_prompt(q, k, v, qi, ki, wts, pos):
    B, T = q.shape[:2]
    nblk = T // Q_BLOCK
    topk = min(TOPK_MAX, T // 4)
    bidx = jnp.arange(B)[:, None, None]

    def blk(a):
        return jnp.swapaxes(a.reshape((B, nblk, Q_BLOCK) + a.shape[2:]), 0, 1)

    def one_block(args):
        qb, qib, wb, pb = args
        idx, valid = dsa_select(qib, wb, ki, pb, topk)
        return sparse_attend(qb, k[bidx, idx], v[bidx, idx], valid)

    out = lax.map(one_block, (blk(q), blk(qi), blk(wts), pos.reshape(nblk, Q_BLOCK)))
    return jnp.swapaxes(out, 0, 1).reshape(B, T, ATTN_WIDTH)

def dsa_sample(q, k_new, v_new, qi, ki_new, wts, qpos, cache_k, cache_v, cache_kidx, page_table):
    DB, DS = q.shape[:2]
    past = page_table.shape[1] * PAGE_SIZE
    ki_past = cache_kidx[page_table].reshape(DB, past, IDX_DIM).astype(ki_new.dtype)
    ki_all = jnp.concatenate([ki_past, ki_new], axis=1)
    topk = min(TOPK_MAX, (past + DS) // 4)
    idx, valid = dsa_select(qi, wts, ki_all, qpos, topk)
    bidx = jnp.arange(DB)[:, None, None]
    in_past = idx < past
    pidx = jnp.minimum(idx, past - 1)
    phys = page_table[bidx, pidx // PAGE_SIZE]
    off = pidx % PAGE_SIZE
    nidx = jnp.clip(idx - past, 0, DS - 1)

    def gather(cache, new):
        return jnp.where(in_past[..., None, None], cache[phys, off].astype(new.dtype), new[bidx, nidx])

    return sparse_attend(q, gather(cache_k, k_new), gather(cache_v, v_new), valid)

def layer(x, c, pos, conv_state, ssm_state, attend, p):
    B, L, _ = x.shape
    mod = (jax.nn.silu(c) @ p['w_ada'] + p['b_ada'])[:, None, :]
    sh1, sc1, g1, sh2, sc2, g2 = jnp.split(mod, 6, axis=-1)
    h = rmsnorm(x, p['norm1_g']) * (1 + sc1) + sh1
    (z, xs, bm, cm, dtr, q, k, v, qi, ki, wi, gs, ga) = jnp.split(
        h @ p['w_in'], split_points(IN_SPLITS), axis=-1)
    xbc, new_conv = causal_conv(jnp.concatenate([xs, bm, cm], axis=-1), conv_state,
                                p['conv_w'], p['conv_b'])
    xs, bm, cm = jnp.split(xbc, split_points((SSM_INNER, SSM_GN, SSM_GN)), axis=-1)
    y_ssm, new_ssm = ssm_branch(z, xs, bm, cm, dtr, ssm_state, p['dt_bias'], p['a_log'],
                                p['d_skip'], p['ssm_norm_g'])
    R = ATTN_HEADS // ATTN_KV_HEADS
    q = rope(q.reshape(B, L, ATTN_KV_HEADS, R, ATTN_HEAD_DIM), pos)
    k = rope(k.reshape(B, L, ATTN_KV_HEADS, ATTN_HEAD_DIM), pos)
    v = v.reshape(B, L, ATTN_KV_HEADS, ATTN_HEAD_DIM)
    qi = rope(qi.reshape(B, L, IDX_HEADS, IDX_DIM), pos)
    ki = rope(ki, pos)
    y_attn = attend(q, k, v, qi, ki, wi * IDX_WEIGHT_SCALE, pos)
    merged = (jax.nn.sigmoid(gs) * (y_ssm @ p['w_proj_ssm'])
              + jax.nn.sigmoid(ga) * (y_attn @ p['w_proj_attn']))
    x = x + g1 * (merged @ p['w_out'])
    h2 = rmsnorm(x, p['norm2_g']) * (1 + sc2) + sh2
    gate, up = jnp.split(h2 @ p['w_ffn_in'], 2, axis=-1)
    x = x + g2 * ((jax.nn.silu(gate) * up) @ p['w_ffn_out'])
    return x, (k, v, ki, new_conv, new_ssm)

def setup_inputs(seed: int = 0) -> dict:
    key = jax.random.key(seed)
    it = iter(jax.random.split(key, 32))
    nrm = lambda shape, s: jax.random.normal(next(it), shape, jnp.float32) * s
    n_pages = PAST_LEN // PAGE_SIZE
    n_used = DEC_BATCH * n_pages
    n_pool = n_used + max(1, n_used // 4)
    D = D_MODEL
    x_prompt = nrm((BATCH, SEQ, D), 1.0)
    x_sample = nrm((DEC_BATCH, DEC_SEQ, D), 1.0)
    cache_k = nrm((DEPTH, n_pool, PAGE_SIZE, ATTN_KV_HEADS, ATTN_HEAD_DIM), 1.0)
    cache_v = nrm((DEPTH, n_pool, PAGE_SIZE, ATTN_KV_HEADS, ATTN_HEAD_DIM), 1.0)
    cache_kidx = nrm((DEPTH, n_pool, PAGE_SIZE, IDX_DIM), 1.0)
    page_table = jax.random.permutation(next(it), n_pool)[:n_used].reshape(
        DEC_BATCH, n_pages).astype(jnp.int32)
    c_prompt = nrm((BATCH, D), 1.0)
    c_sample = nrm((DEC_BATCH, D), 1.0)
    state_conv = nrm((DEPTH, DEC_BATCH, SSM_CONV - 1, SSM_CONV_DIM), 1.0)
    state_ssm = nrm((DEPTH, DEC_BATCH, SSM_HEADS, SSM_HEAD_DIM, SSM_STATE), 0.3)
    w_ada = nrm((DEPTH, D, 6 * D), 0.5 * D ** -0.5)
    b_ada = nrm((DEPTH, 6 * D), 0.02)
    norm1_g = 1.0 + nrm((DEPTH, D), 0.05)
    w_in = nrm((DEPTH, D, IN_DIM), D ** -0.5)
    conv_w = nrm((DEPTH, SSM_CONV, SSM_CONV_DIM), SSM_CONV ** -0.5)
    conv_b = nrm((DEPTH, SSM_CONV_DIM), 0.02)
    u = jax.random.uniform(next(it), (DEPTH, SSM_HEADS), jnp.float32)
    dt0 = jnp.exp(u * (math.log(0.1) - math.log(0.001)) + math.log(0.001))
    dt_bias = dt0 + jnp.log(-jnp.expm1(-dt0))
    a_log = jnp.log(jax.random.uniform(next(it), (DEPTH, SSM_HEADS), jnp.float32, 1.0, 16.0))
    d_skip = 1.0 + nrm((DEPTH, SSM_HEADS), 0.1)
    ssm_norm_g = 1.0 + nrm((DEPTH, SSM_INNER), 0.05)
    w_proj_ssm = nrm((DEPTH, SSM_INNER, D), SSM_INNER ** -0.5)
    w_proj_attn = nrm((DEPTH, ATTN_WIDTH, D), ATTN_WIDTH ** -0.5)
    w_out = nrm((DEPTH, D, D), D ** -0.5)
    norm2_g = 1.0 + nrm((DEPTH, D), 0.05)
    w_ffn_in = nrm((DEPTH, D, 2 * FFN_HIDDEN), D ** -0.5)
    w_ffn_out = nrm((DEPTH, FFN_HIDDEN, D), FFN_HIDDEN ** -0.5)
    final_g = 1.0 + nrm((D,), 0.05)
    return {'x_prompt': x_prompt, 'x_sample': x_sample, 'cache_k': cache_k, 'cache_v': cache_v,
            'cache_kidx': cache_kidx, 'state_conv': state_conv, 'state_ssm': state_ssm,
            'page_table': page_table, 'c_prompt': c_prompt, 'c_sample': c_sample,
            'w_ada': w_ada, 'b_ada': b_ada, 'norm1_g': norm1_g, 'w_in': w_in,
            'conv_w': conv_w, 'conv_b': conv_b, 'dt_bias': dt_bias, 'a_log': a_log,
            'd_skip': d_skip, 'ssm_norm_g': ssm_norm_g, 'w_proj_ssm': w_proj_ssm,
            'w_proj_attn': w_proj_attn, 'w_out': w_out, 'norm2_g': norm2_g,
            'w_ffn_in': w_ffn_in, 'w_ffn_out': w_ffn_out, 'final_g': final_g}

def reference(x_prompt, x_sample, cache_k, cache_v, cache_kidx, state_conv, state_ssm,
              page_table, c_prompt, c_sample, w_ada, b_ada, norm1_g, w_in, conv_w, conv_b,
              dt_bias, a_log, d_skip, ssm_norm_g, w_proj_ssm, w_proj_attn, w_out, norm2_g,
              w_ffn_in, w_ffn_out, final_g):
    B, T, _ = x_prompt.shape
    DB, DS, _ = x_sample.shape
    past = page_table.shape[1] * PAGE_SIZE
    pos_p = jnp.arange(T, dtype=jnp.int32)
    pos_s = past + jnp.arange(DS, dtype=jnp.int32)
    yp, ys = x_prompt, x_sample
    outs_p, outs_s = [], []
    for l in range(DEPTH):
        p = dict(w_ada=w_ada[l], b_ada=b_ada[l], norm1_g=norm1_g[l], w_in=w_in[l],
                 conv_w=conv_w[l], conv_b=conv_b[l], dt_bias=dt_bias[l], a_log=a_log[l],
                 d_skip=d_skip[l], ssm_norm_g=ssm_norm_g[l], w_proj_ssm=w_proj_ssm[l],
                 w_proj_attn=w_proj_attn[l], w_out=w_out[l], norm2_g=norm2_g[l],
                 w_ffn_in=w_ffn_in[l], w_ffn_out=w_ffn_out[l])
        conv0 = jnp.zeros((B, SSM_CONV - 1, SSM_CONV_DIM), x_prompt.dtype)
        ssm0 = jnp.zeros((B, SSM_HEADS, SSM_HEAD_DIM, SSM_STATE), jnp.float32)
        yp, st_p = layer(yp, c_prompt, pos_p, conv0, ssm0, dsa_prompt, p)

        def attend_s(q, k, v, qi, ki, wts, qpos, l=l):
            return dsa_sample(q, k, v, qi, ki, wts, qpos, cache_k[l], cache_v[l],
                              cache_kidx[l], page_table)

        ys, st_s = layer(ys, c_sample, pos_s, state_conv[l], state_ssm[l], attend_s, p)
        outs_p.append(st_p)
        outs_s.append(st_s)

    def stack(outs, i):
        return jnp.stack([o[i] for o in outs], axis=0)

    y_prompt = rmsnorm(yp, final_g)
    y_sample = rmsnorm(ys, final_g)
    k_prompt, v_prompt, kidx_prompt = stack(outs_p, 0), stack(outs_p, 1), stack(outs_p, 2)
    conv_prompt, ssm_prompt = stack(outs_p, 3), stack(outs_p, 4)
    k_sample, v_sample, kidx_sample = stack(outs_s, 0), stack(outs_s, 1), stack(outs_s, 2)
    conv_sample, ssm_sample = stack(outs_s, 3), stack(outs_s, 4)
    return (y_prompt, y_sample, k_prompt, v_prompt, kidx_prompt, conv_prompt, ssm_prompt,
            k_sample, v_sample, kidx_sample, conv_sample, ssm_sample)


_drawn_inputs = setup_inputs


def setup_inputs(seed=0):
    import zlib

    import numpy as np

    out = dict(_drawn_inputs(seed))
    spreads = {}
    factors = {'d_skip': 5.62, 'ssm_norm_g': 7.196, 'norm2_g': 4.096}
    for name, (base, spread) in spreads.items():
        noise = np.random.default_rng([zlib.crc32(name.encode()), seed]).standard_normal(out[name].shape)
        drawn = base * np.exp(spread * noise) if base else spread * noise
        out[name] = __import__('jax').numpy.asarray(drawn.astype(out[name].dtype))
    for name, factor in factors.items():
        out[name] = (out[name] * factor).astype(out[name].dtype)
    return out
```

```python
from contextlib import ExitStack

import concourse.bass as bass
from concourse import mybir

F32 = mybir.dt.float32
I32 = mybir.dt.int32
BF16 = mybir.dt.bfloat16
ALU = mybir.AluOpType
ACT = mybir.ActivationFunctionType
AX = mybir.AxisListType

P = 128
D = 1024
SEQ, DEC = 1024, 8
NT = SEQ + DEC
TT = SEQ // P
KB = D // P
TC, CW = 3, NT // 3
EPS = 1e-6
INNER, HEADS, HD, GROUPS, NST, CONV = 2048, 32, 64, 4, 128, 4
GW = INNER // GROUPS
GH = HEADS // GROUPS
XBC = INNER + 2 * GROUPS * NST
AH, KVH = 16, 4
IH = 4
PAST, PAGE = 256, 128
NPAGE = PAST // PAGE
SKEYS = PAST + 1
TOPK = min(256, SEQ // 4)
STOPK = min(256, SKEYS // 4)
FFN = 2816
FB = FFN // P
C_Z, C_X, C_B, C_C, C_DT = 0, 2048, 4096, 4608, 5120
C_Q, C_K, C_V, C_QI, C_KI, C_WI, C_GS, C_GA = 5152, 6176, 6432, 6688, 6944, 7008, 7012, 8036
IDX_SCALE = IH ** -0.5 * HD ** -0.5
ATT_SCALE = HD ** -0.5
FAR = -3.0e38
OFF = -1.0e30
SLAB = 2048
RING = 4


def rows_of(t):
    return P if t < TT else DEC


class Chip:
    pass


def weight_slabs(A):
    slabs, span = [], {}

    def cols(w, c0, n):
        return w[0, :, c0:c0 + n].rearrange("(k p) n -> p k n", p=P)

    def k8(at, n=256):
        return lambda s: s.rearrange("p (k n) -> p k n", k=KB)[:, :, at:at + n]

    def add(name, *parts):
        span.setdefault(name, [len(slabs), 0])
        slabs.append(list(parts))
        span[name][1] = len(slabs)

    for i in range(24):
        add("ada", (k8(0), cols(A["w_ada"], 256 * i, 256)))
    add("qkv", (k8(0, 32), cols(A["w_in"], C_DT, 32)), (k8(32, 68), cols(A["w_in"], C_KI, 68)))
    add("qkv", (k8(0), cols(A["w_in"], C_QI, 256)))
    add("qkv", (k8(0), cols(A["w_in"], C_K, 256)))
    add("qkv", (k8(0), cols(A["w_in"], C_V, 256)))
    for i in range(4):
        add("qkv", (k8(0), cols(A["w_in"], C_Q + 256 * i, 256)))
    for c in (C_GS, C_GA):
        for i in range(4):
            add("gates", (k8(0), cols(A["w_in"], c + 256 * i, 256)))
    for g in range(GROUPS):
        n = f"g{g}"
        for i in range(2):
            add(n, (k8(0), cols(A["w_in"], C_X + GW * g + 256 * i, 256)))
        add(n, (k8(0, P), cols(A["w_in"], C_B + P * g, P)), (k8(P, P), cols(A["w_in"], C_C + P * g, P)))
        for i in range(2):
            add(n, (k8(0), cols(A["w_in"], C_Z + GW * g + 256 * i, 256)))
    for i in range(4):
        add("merge", (k8(0), cols(A["w_proj_attn"], 256 * i, 256)))
        for j in range(2 * i, 2 * i + 2):
            add("merge", (lambda s: s.rearrange("p (k n) -> p k n", k=2 * KB),
                          A["w_proj_ssm"][0, :, P * j:P * j + P].rearrange("(k p) n -> p k n", p=P)))
    for i in range(4):
        add("out", (k8(0), cols(A["w_out"], 256 * i, 256)))
    for f in range(FB):
        add("ffn", (k8(0, P), cols(A["w_ffn_in"], P * f, P)), (k8(P, P), cols(A["w_ffn_in"], FFN + P * f, P)))
    return slabs, span


def ring_landed(K, n):
    return K.landed[n % RING], 16 * sum(len(K.slabs[m]) for m in range(n % RING, n + 1, RING))


def ring_load(K, eng, stage, used):
    first, last = K.span[stage]
    for n in range(first + RING, min(last + RING, len(K.slabs))):
        eng.wait_ge(*used(n - RING - first))
        for place, src in K.slabs[n]:
            eng.dma_start(place(K.ring[:, n % RING, :]), src).then_inc(K.landed[n % RING], 16)


def slab_of(K, n, k=KB):
    return K.ring[:, n % RING, :].rearrange("p (k n) -> p k n", k=k)


def modulation(K):
    nc, A, ps = K.nc, K.A, K.ps
    first, last = K.span["ada"]
    with ExitStack() as ctx:
        def sb(name, shape):
            return ctx.enter_context(nc.sbuf_tensor(name, shape, F32))
        c_rows = sb("c_rows", [9, D])
        c_silu = sb("c_silu", [9, D])
        cT = sb("cT", [P, KB, 9])
        mod = sb("mod", [9, 6 * D])
        vec_rows = sb("vec_rows", [P, 2, P])
        gate_sb = sb("gate_sb", [P, 4, D])
        c_in, vec_in, mod_b = K.sem("c_in"), K.sem("vec_in"), K.sem("mod_bias_in")
        silu_done, cT_ps, cT_done = K.sem("c_silu_done"), K.sem("cT_in_psum"), K.sem("cT_done")
        vec_ps = K.sem("vec_in_psum")
        prod, summed = K.sem("mod_product"), K.sem("mod_summed")
        modT_ps, modT_done = K.sem("modT_in_psum"), K.sem("modT_done")
        step = K.sem("mod_vector_step")
        gate_ps, gate_done, gate_out = K.sem("gate_in_psum"), K.sem("gate_done"), K.sem("gate_stored")
        block = ctx.enter_context(nc.Block())

        @block.sync
        def _(sp):
            sp.dma_start(c_rows[0:1, :], A["c_prompt"]).then_inc(c_in, 16)
            sp.dma_start(c_rows[1:9, :], A["c_sample"]).then_inc(c_in, 16)
            sp.dma_start(K.ident[:], A["k_ident"]).then_inc(K.ident_in, 16)
            for n in range(RING):
                for place, src in K.slabs[n]:
                    sp.dma_start(place(K.ring[:, n, :]), src).then_inc(K.landed[n], 16)
            sp.dma_start(mod[:, :], A["b_ada"][0].partition_broadcast(9)).then_inc(mod_b, 16)
            rows = ((0, 0, A["conv_w"][0].rearrange("i (b p) -> (i b) p", p=P), 96),
                    (0, 96, A["conv_b"][0].rearrange("(b p) -> b p", p=P), 24),
                    (1, 0, A["norm1_g"][0].rearrange("(b p) -> b p", p=P), 8),
                    (1, 8, A["norm2_g"][0].rearrange("(b p) -> b p", p=P), 8),
                    (1, 16, A["ssm_norm_g"][0].rearrange("(b p) -> b p", p=P), 16))
            for part, r0, src, n in rows:
                sp.dma_start(vec_rows[r0:r0 + n, part, :], src).then_inc(vec_in, 16)
            for dst, name in ((K.le, "k_le"), (K.gt, "k_gt"), (K.ones, "k_ones"), (K.diag_off, "k_diag_off"),
                              (K.cos, "k_cos"), (K.sin, "k_sin")):
                sp.dma_start(dst[:], A[name]).then_inc(K.const_in, 16)
            for i, name in enumerate(("dt_bias", "a_log", "d_skip")):
                sp.dma_start(K.heads_row[:, i, :], A[name][0].partition_broadcast(P)).then_inc(K.const_in, 16)
                sp.dma_start(K.heads_col[:, i:i + 1], A[name][0].unsqueeze(1)).then_inc(K.const_in, 16)
            ring_load(K, sp, "ada", lambda i: (prod, i + 1))
            sp.wait_ge(gate_done, 4)
            for b in range(4):
                r = P if b % 2 == 0 else DEC
                sp.dma_start(A["s_gates"][b, 0:r, :], gate_sb[0:r, b, :]).then_inc(gate_out, 16)
            sp.wait_ge(gate_out, 64)

        @block.scalar
        def _(act):
            act.wait_ge(c_in, 32)
            nc.scalar.activation(c_silu[:], c_rows[:], ACT.Silu).then_inc(silu_done, 1)
            for b in range(4):
                act.wait_ge(gate_ps, b + 1)
                for h in range(2):
                    cp = nc.scalar.copy(gate_sb[0:P if b % 2 == 0 else DEC, b, 512 * h:512 * h + 512],
                                        ps[0:P if b % 2 == 0 else DEC, 2 + h, :])
                cp.then_inc(gate_done, 1)

        @block.tensor
        def _(pe):
            pe.wait_ge(K.ident_in, 16)
            pe.wait_ge(silu_done, 1)
            for k in range(KB):
                mm = nc.tensor.transpose(ps[:, 7, 9 * k:9 * k + 9], c_silu[:, P * k:P * k + P], K.ident[0:9, 0:9])
            mm.then_inc(cT_ps, 1)
            pe.wait_ge(cT_done, 1)
            for n in range(first, last):
                i = n - first
                pe.wait_ge(*ring_landed(K, n))
                if i >= 2:
                    pe.wait_ge(summed, i - 1)
                for k in range(KB):
                    mm = nc.tensor.matmul(ps[0:9, i % 2, 0:256], cT[:, k, :], slab_of(K, n)[:, k, :],
                                          start=(k == 0), stop=(k == KB - 1))
                mm.then_inc(prod, 1)
            pe.wait_ge(vec_in, 80)
            nc.tensor.transpose(ps[:, 4, 0:120], vec_rows[0:120, 0, :], K.ident[0:120, 0:120])
            nc.tensor.transpose(ps[:, 4, 120:152], vec_rows[0:32, 1, :], K.ident[0:32, 0:32]).then_inc(vec_ps, 1)
            pe.wait_ge(summed, last - first)
            for a, part in enumerate((0, 1, 3, 4)):
                for k in range(KB):
                    mm = nc.tensor.transpose(ps[:, 5, (8 * a + k) * 9:(8 * a + k) * 9 + 9],
                                             mod[:, D * part + P * k:D * part + P * k + P], K.ident[0:9, 0:9])
            mm.then_inc(modT_ps, 1)
            for b in range(4):
                if b:
                    pe.wait_ge(gate_done, b)
                base = D * (2 if b < 2 else 5)
                who = K.ident[0:9, 0:1].to_broadcast([9, P]) if b % 2 == 0 else K.ident[0:9, 1:9]
                for h in range(2):
                    mm = nc.tensor.matmul(ps[0:P if b % 2 == 0 else DEC, 2 + h, :], who,
                                          mod[:, base + 512 * h:base + 512 * h + 512], start=True, stop=True)
                mm.then_inc(gate_ps, 1)

        @block.vector
        def _(dve):
            dve.wait_ge(cT_ps, 1)
            nc.vector.tensor_copy(cT[:].rearrange("p k s -> p (k s)"), ps[:, 7, 0:72]).then_inc(cT_done, 1)
            dve.wait_ge(mod_b, 16)
            for i in range(last - first):
                dve.wait_ge(prod, i + 1)
                nc.vector.tensor_tensor(mod[:, 256 * i:256 * i + 256], ps[0:9, i % 2, 0:256],
                                        mod[:, 256 * i:256 * i + 256], ALU.add).then_inc(summed, 1)
            dve.wait_ge(vec_ps, 1)
            nc.vector.tensor_copy(K.vecs[:], ps[:, 4, 0:152]).then_inc(step, 1)
            dve.wait_ge(modT_ps, 1)
            nc.vector.tensor_copy(K.modT[:].rearrange("p a k s -> p (a k s)"), ps[:, 5, 0:288]).then_inc(step, 1)
            dve.wait_ge(step, 2)
            for a in range(2):
                sc = K.modT[:, 2 * a + 1, :, :]
                nc.vector.tensor_scalar(sc, sc, 1.0, None, ALU.add).then_inc(step, 1)
                dve.wait_ge(step, 3 + 2 * a)
                g = K.vecs[:, 120 + 8 * a:128 + 8 * a].unsqueeze(2).to_broadcast([P, KB, 9])
                nc.vector.tensor_tensor(sc, sc, g, ALU.mult).then_inc(step, 1)
                dve.wait_ge(step, 4 + 2 * a)


def norm_stage(K, tag, which, hT, source):
    nc, ps = K.nc, K.ps
    with ExitStack() as ctx:
        def sb(name, shape):
            return ctx.enter_context(nc.sbuf_tensor(tag + name, shape, F32))
        x = sb("x", [P, 3, D])
        xn = sb("xn", [P, 2, D])
        sq = sb("sq", [P, D])
        stat = sb("stat", [P, 4, 9])
        x_in = [K.sem(f"{tag}x_in{i}") for i in range(3)]
        squared, mean, root, inv = K.sem(tag + "squared"), K.sem(tag + "mean"), K.sem(tag + "root"), K.sem(tag + "inv")
        scaled, turned, moved = K.sem(tag + "scaled"), K.sem(tag + "turned"), K.sem(tag + "moved")
        extra = K.sem(tag + "sample_scaled")
        block = ctx.enter_context(nc.Block())

        @block.sync
        def _(sp):
            for t in range(9):
                if t >= 3:
                    sp.wait_ge(scaled, t - 2)
                    sp.wait_ge(squared, t - 2)
                sp.dma_start(x[0:rows_of(t), t % 3, :], source(t)).then_inc(x_in[t % 3], 16)

        @block.scalar
        def _(act):
            def square(t):
                r = rows_of(t)
                act.wait_ge(x_in[t % 3], 16 * (t // 3 + 1))
                if t:
                    act.wait_ge(squared, t)
                nc.scalar.activation(sq[0:r, :], x[0:r, t % 3, :], ACT.Square,
                                     accum_out=stat[0:r, 0, t:t + 1]).then_inc(squared, 1)
                act.wait_ge(mean, t + 1)
                nc.scalar.activation(stat[0:r, 2, t:t + 1], stat[0:r, 1, t:t + 1], ACT.Sqrt).then_inc(root, 1)

            def move(t):
                for h in range(2):
                    act.wait_ge(turned, 2 * t + h + 1)
                    for j in range(4):
                        k = 4 * h + j
                        mv = nc.scalar.activation(hT[:, k, P * t:P * t + P], ps[:, 2 * (t % 2) + h, P * j:P * j + P],
                                                  ACT.Identity, bias=K.modT[:, 2 * which, k, 0:1],
                                                  scale=K.modT[:, 2 * which + 1, k, 0:1])
                    mv.then_inc(moved, 1)

            square(0)
            for t in range(TT):
                square(t + 1)
                move(t)

        @block.vector
        def _(dve):
            for t in range(9):
                r = rows_of(t)
                dve.wait_ge(squared, t + 1)
                nc.vector.tensor_scalar(stat[0:r, 1, t:t + 1], stat[0:r, 0, t:t + 1], 1.0 / D, EPS,
                                        ALU.mult, ALU.add).then_inc(mean, 1)
                dve.wait_ge(root, t + 1)
                nc.vector.reciprocal(stat[0:r, 3, t:t + 1], stat[0:r, 2, t:t + 1]).then_inc(inv, 1)
                dve.wait_ge(inv, t + 1)
                if t >= 2:
                    dve.wait_ge(turned, 2 * (t - 1))
                nc.vector.tensor_scalar(xn[0:r, t % 2, :], x[0:r, t % 3, :], stat[0:r, 3, t:t + 1], None,
                                        ALU.mult).then_inc(scaled, 1)
            dve.wait_ge(turned, 2 * TT + 1)
            hs = hT[:, :, SEQ:NT]
            nc.vector.tensor_tensor(hs, ps[:, 4, 0:64].rearrange("p (k s) -> p k s", k=KB),
                                    K.modT[:, 2 * which + 1, :, 1:9], ALU.mult).then_inc(extra, 1)
            dve.wait_ge(extra, 1)
            nc.vector.tensor_tensor(hs, hs, K.modT[:, 2 * which, :, 1:9], ALU.add).then_inc(extra, 1)

        @block.tensor
        def _(pe):
            for t in range(9):
                pe.wait_ge(scaled, t + 1)
                if t == TT:
                    for k in range(KB):
                        mm = nc.tensor.transpose(ps[:, 4, 8 * k:8 * k + 8], xn[0:DEC, t % 2, P * k:P * k + P],
                                                 K.ident[0:DEC, 0:DEC])
                    mm.then_inc(turned, 1)
                    break
                for h in range(2):
                    if t >= 2:
                        pe.wait_ge(moved, 2 * (t - 2) + h + 1)
                    for j in range(4):
                        k = 4 * h + j
                        mm = nc.tensor.transpose(ps[:, 2 * (t % 2) + h, P * j:P * j + P],
                                                 xn[:, t % 2, P * k:P * k + P], K.ident[:])
                    mm.then_inc(turned, 1)


def project(K, hT, T):
    nc, A, ps = K.nc, K.A, K.ps
    first, last = K.span["qkv"]
    n_slabs = last - first
    SMALL, QI, KK, V, Q0 = 0, 1, 2, 3, 4
    with ExitStack() as ctx:
        def sb(name, shape):
            return ctx.enter_context(nc.sbuf_tensor(name, shape, F32))
        stg = sb("stg", [P, 2, 9, 256])
        rot = sb("rot", [P, 2, 9, 256])
        tmp = sb("tmp", [P, 2, 256])
        gemm, out_of_ps = K.sem("qkv_in_psum"), K.sem("qkv_rows")
        t_a, t_b, rotated = K.sem("rope_cos_part"), K.sem("rope_sin_part"), K.sem("roped_tiles")
        dtT_ps, kept = K.sem("dtT_in_psum"), K.sem("sample_rows_kept")
        turned, moved = K.sem("qk_turned"), K.sem("qk_moved")
        ki_stored, k_stored, v_stored = (K.store_sem(n) for n in ("ki_stored", "k_stored", "v_stored"))
        block = ctx.enter_context(nc.Block())

        rope_cols = [(32, 1), (0, 4), (0, 4), None] + [(0, 4)] * 4
        roped_before = [9 * sum(1 for c in rope_cols[:s] if c) for s in range(n_slabs + 1)]

        def turns(s):
            r, lo, hi = rot[:, s % 2], slice(0, HD), slice(HD, P)
            if s == SMALL:
                return [(lambda t: r[:, t, 32:96], HD, [(lo, T.kiT[lo, :]), (lo, T.kiT[hi, :])])]
            if s == KK:
                return [(lambda t, j=j: r[:, t, P * j:P * j + P], P,
                         [(lo, T.kT[lo, 2 * j, :]), (lo, T.kT[hi, 2 * j, :]),
                          (hi, T.kT[lo, 2 * j + 1, :]), (hi, T.kT[hi, 2 * j + 1, :])]) for j in range(2)]
            if s == V:
                return []
            full = slice(0, P)
            return [(lambda t, j=j: r[:, t, P * j:P * j + P], P,
                     [(full, T.qiT[:, j, :] if s == QI else T.qT[:, 2 * (s - Q0) + j, 0:SEQ])]) for j in range(2)]

        units = [(s, src, w, dst, h) for s in range(n_slabs) for src, w, dst in turns(s) for h in range(2)]
        units_before = [sum(1 for u in units if u[0] < s) for s in range(n_slabs + 1)]

        @block.sync
        def _(sp):
            ring_load(K, sp, "qkv", lambda i: (gemm, 9 * i + 9) if i else (dtT_ps, 1))

        @block.gpsimd
        def _(pool):
            pool.wait_ge(rotated, roped_before[SMALL + 1])
            r = rot[:, SMALL % 2]
            pool.dma_start(A["kidx_prompt"][0, 0].rearrange("(t p) d -> p t d", p=P), r[:, 0:TT, 32:96]).then_inc(ki_stored, 16)
            pool.dma_start(A["kidx_sample"][0, :, 0], r[0:DEC, TT, 32:96]).then_inc(ki_stored, 16)
            pool.wait_ge(rotated, roped_before[KK + 1])
            r = rot[:, KK % 2]
            pool.dma_start(A["k_prompt"][0, 0].rearrange("(t p) g d -> p t (g d)", p=P), r[:, 0:TT, :]).then_inc(k_stored, 16)
            pool.dma_start(A["k_sample"][0, :, 0].rearrange("b g d -> b (g d)"), r[0:DEC, TT, :]).then_inc(k_stored, 16)
            pool.wait_ge(out_of_ps, 9 * (V + 1))
            pool.dma_start(A["v_prompt"][0, 0].rearrange("(t p) g d -> p t (g d)", p=P), T.v[:, 0:TT, :]).then_inc(v_stored, 16)
            pool.dma_start(A["v_sample"][0, :, 0].rearrange("b g d -> b (g d)"), T.v[0:DEC, TT, :]).then_inc(v_stored, 16)
            for done in (ki_stored, k_stored, v_stored):
                pool.wait_ge(done, 32)

        @block.scalar
        def _(act):
            def rows(s):
                for t in range(9):
                    r, n = rows_of(t), 100 if s == SMALL else 256
                    act.wait_ge(gemm, 9 * s + t + 1)
                    if s >= 2 and t == 0:
                        act.wait_ge(kept, roped_before[s - 1] // 9)
                    dst = T.v[0:r, t, :] if s == V else stg[0:r, s % 2, t, 0:n]
                    nc.scalar.copy(dst, ps[0:r, (9 * s + t) % 4, 0:n]).then_inc(out_of_ps, 1)

            def turn_moves(s):
                for u in range(units_before[s], units_before[s + 1]):
                    _, _, _, places, h = units[u]
                    act.wait_ge(turned, u + 1)
                    for rows, dst in places:
                        mv = nc.scalar.copy(dst[:, 512 * h:512 * h + 512], ps[rows, 4 + u % 3, :])
                    mv.then_inc(moved, 1)

            rows(0)
            for s in range(1, n_slabs):
                rows(s)
                turn_moves(s - 1)
            turn_moves(n_slabs - 1)

        @block.vector
        def _(dve):
            m = 0
            dve.wait_ge(K.const_in, 16 * 12)
            for s in range(n_slabs):
                if rope_cols[s] is None:
                    continue
                c0, nh = rope_cols[s]
                w = HD * nh
                if s == QI + 1:
                    dve.wait_ge(ki_stored, 32)
                if s == Q0:
                    dve.wait_ge(k_stored, 32)
                if s >= 2:
                    dve.wait_ge(turned, units_before[s - 1])
                for t in range(9):
                    r = rows_of(t)
                    dve.wait_ge(out_of_ps, 9 * s + t + 1)
                    x = stg[0:r, s % 2, t, c0:c0 + w].rearrange("p (h d) -> p h d", d=HD)
                    o = rot[0:r, s % 2, t, c0:c0 + w].rearrange("p (h d) -> p h d", d=HD)
                    b = tmp[0:r, m % 2, 0:w].rearrange("p (h d) -> p h d", d=HD)
                    hh = HD // 2
                    cos = K.cos[0:r, t, :].unsqueeze(1).to_broadcast([r, nh, HD])
                    sin = K.sin[0:r, t, :].unsqueeze(1)
                    nc.vector.tensor_tensor(b[:, :, 0:hh], x[:, :, hh:HD], sin[:, :, 0:hh].to_broadcast([r, nh, hh]), ALU.mult)
                    nc.vector.tensor_tensor(b[:, :, hh:HD], x[:, :, 0:hh], sin[:, :, hh:HD].to_broadcast([r, nh, hh]),
                                            ALU.mult).then_inc(t_b, 1)
                    nc.vector.tensor_tensor(o, x, cos, ALU.mult).then_inc(t_a, 1)
                    m += 1
                    dve.wait_ge(t_b, m)
                    dve.wait_ge(t_a, m)
                    nc.vector.tensor_tensor(o, o, b, ALU.add).then_inc(rotated, 1)
                dve.wait_ge(rotated, m)
                if s == SMALL:
                    nc.vector.tensor_copy(T.dt_raw[:], stg[:, 0, 0:TT, 0:32])
                    nc.vector.tensor_scalar(T.wi[:, 0:TT, :], stg[:, 0, 0:TT, 96:100], IDX_SCALE, None, ALU.mult)
                    nc.vector.tensor_scalar(T.wi[0:DEC, TT, :], stg[0:DEC, 0, TT, 96:100], IDX_SCALE, None, ALU.mult)
                    nc.vector.tensor_copy(T.ki_s[:], rot[0:DEC, 0, TT, 32:96]).then_inc(kept, 1)
                elif s == QI:
                    nc.vector.tensor_copy(T.qi_s[:], rot[0:DEC, 1, TT, :]).then_inc(kept, 1)
                elif s == KK:
                    nc.vector.tensor_copy(T.k_s[:], rot[0:DEC, 0, TT, :]).then_inc(kept, 1)
                else:
                    nc.vector.tensor_copy(T.q_s[:, 256 * (s - Q0):256 * (s - Q0) + 256],
                                          rot[0:DEC, s % 2, TT, :]).then_inc(kept, 1)
            dve.wait_ge(dtT_ps, 1)
            nc.vector.tensor_copy(T.dtT_raw[:], ps[0:32, 7, 0:DEC])

        @block.tensor
        def _(pe):
            def gemm_slab(s):
                n = first + s
                w = slab_of(K, n)
                width = 100 if s == SMALL else 256
                pe.wait_ge(*ring_landed(K, n))
                for t in range(9):
                    r = rows_of(t)
                    if 9 * s + t >= 4:
                        pe.wait_ge(out_of_ps, 9 * s + t - 3)
                    for k in range(KB):
                        mm = nc.tensor.matmul(ps[0:r, (9 * s + t) % 4, 0:width], hT[:, k, P * t:P * t + r], w[:, k, 0:width],
                                              start=(k == 0), stop=(k == KB - 1))
                    mm.then_inc(gemm, 1)

            def turn_slab(s):
                for u in range(units_before[s], units_before[s + 1]):
                    _, src, w, _, h = units[u]
                    if u >= 3:
                        pe.wait_ge(moved, u - 2)
                    for j in range(4):
                        t = 4 * h + j
                        pe.wait_ge(rotated, roped_before[s] + t + 1)
                        mm = nc.tensor.transpose(ps[0:w, 4 + u % 3, P * j:P * j + P], src(t), K.ident[:])
                    mm.then_inc(turned, 1)

            gemm_slab(0)
            w = slab_of(K, first)
            for k in range(KB):
                mm = nc.tensor.matmul(ps[0:HEADS, 7, 0:DEC], w[:, k, 0:HEADS], hT[:, k, SEQ:NT],
                                      start=(k == 0), stop=(k == KB - 1))
            mm.then_inc(dtT_ps, 1)
            for s in range(1, n_slabs):
                gemm_slab(s)
                turn_slab(s - 1)
            turn_slab(n_slabs - 1)


BIAS_AT = [P * i * (i + 1) // 2 for i in range(TT + 1)]


def select(K, hT, T):
    nc, A, ps = K.nc, K.A, K.ps
    first, last = K.span["gates"]
    with ExitStack() as ctx:
        def sb(name, shape):
            return ctx.enter_context(nc.sbuf_tensor(name, shape, F32))
        relu = sb("relu", [P, IH, SEQ])
        score, work, eq, cum = (sb(n, [P, SEQ]) for n in ("score", "work", "eq", "cum"))
        top8, count = sb("top8", [P, 2, 8]), sb("count", [P, 2])
        sig = sb("sig", [P, 2, NT])
        gemm, sig_done, sig_out = K.sem("gate_sums"), K.sem("gate_sigmoids"), [K.store_sem(f"gate_out{i}") for i in range(2)]
        idx_ps, relu_done, relu_used = K.sem("index_in_psum"), K.sem("index_relus"), K.sem("index_relus_used")
        step = K.sem("select_step")
        block = ctx.enter_context(nc.Block())

        groups = [(n, fb, c) for n in range(last - first) for fb in range(2) for c in range(TC)]
        units = [(i, h) for i in range(2, TT) for h in range(IH)]
        order, g = [], 0
        for i in range(2, TT):
            order += [("index", IH * (i - 2) + h) for h in range(IH)]
            take = len(groups) - g if i == TT - 1 else 8
            order += [("gate", g + j) for j in range(take)]
            g += take

        @block.sync
        def _(sp):
            ring_load(K, sp, "gates", lambda i: (gemm, 2 * TC * (i + 1)))

        @block.gpsimd
        def _(pool):
            for b in range(2 * KB):
                pool.wait_ge(sig_done, TC * (b + 1))
                pool.dma_start(A["s_sig"][b], sig[:, b % 2, :]).then_inc(sig_out[b % 2], 16)
            pool.wait_ge(sig_out[0], 16 * KB)
            pool.wait_ge(sig_out[1], 16 * KB)

        @block.tensor
        def _(pe):
            for kind, u in order:
                if kind == "index":
                    i, h = units[u]
                    if u >= 2:
                        pe.wait_ge(relu_done, u - 1)
                    rows = slice(HD * (h % 2), HD * (h % 2) + HD)
                    for c0 in range(0, P * (i + 1), 512):
                        n = min(512, P * (i + 1) - c0)
                        mm = nc.tensor.matmul(ps[:, 4 + 2 * (u % 2) + c0 // 512, 0:n],
                                              T.qiT[rows, h // 2, P * i:P * i + P], T.kiT[rows, c0:c0 + n],
                                              start=True, stop=True)
                    mm.then_inc(idx_ps, 1)
                else:
                    n, fb, c = groups[u]
                    if fb == 0 and c == 0:
                        pe.wait_ge(*ring_landed(K, first + n))
                    if u >= 4:
                        pe.wait_ge(sig_done, u - 3)
                    w = slab_of(K, first + n)
                    for k in range(KB):
                        mm = nc.tensor.matmul(ps[:, u % 4, 0:CW], w[:, k, P * fb:P * fb + P],
                                              hT[:, k, CW * c:CW * c + CW], start=(k == 0), stop=(k == KB - 1))
                    mm.then_inc(gemm, 1)

        @block.scalar
        def _(act):
            for kind, u in order:
                if kind == "index":
                    i, h = units[u]
                    L = P * (i + 1)
                    act.wait_ge(idx_ps, u + 1)
                    if u >= IH:
                        act.wait_ge(relu_used, u - IH + 1)
                    nc.scalar.activation(relu[:, h, 0:L], ps[:, 4 + 2 * (u % 2):6 + 2 * (u % 2), :]
                                         .rearrange("p a n -> p (a n)")[:, 0:L], ACT.Relu).then_inc(relu_done, 1)
                else:
                    n, fb, c = groups[u]
                    b = 2 * n + fb
                    act.wait_ge(gemm, u + 1)
                    if c == 0 and b >= 2:
                        act.wait_ge(sig_out[b % 2], 16 * (b // 2))
                    nc.scalar.activation(sig[:, b % 2, CW * c:CW * c + CW], ps[:, u % 4, 0:CW],
                                         ACT.Sigmoid).then_inc(sig_done, 1)

        @block.vector
        def _(dve):
            n = [0]

            def link(ins):
                n[0] += 1
                ins.then_inc(step, 1)
                dve.wait_ge(step, n[0])

            v = nc.vector
            link(v.tensor_copy(T.bias[:, 0:P], K.diag_off[:]))
            link(v.memset(T.bias[:, P:2 * P], 0.0))
            link(v.tensor_copy(T.bias[:, 2 * P:3 * P], K.diag_off[:]))
            for i in range(2, TT):
                L = P * (i + 1)
                sc, wk, e, cu = score[:, 0:L], work[:, 0:L], eq[:, 0:L], cum[:, 0:L]
                for h in range(IH):
                    dve.wait_ge(relu_done, IH * (i - 2) + h + 1)
                    w = T.wi[:, i, h:h + 1]
                    dst = sc if h % 2 else cu
                    src = cu if h % 2 else sc
                    if h == 0:
                        v.tensor_scalar(dst, relu[:, h, 0:L], w, None, ALU.mult).then_inc(relu_used, 1)
                    else:
                        v.scalar_tensor_tensor(dst, relu[:, h, 0:L], w, src, ALU.mult, ALU.add).then_inc(relu_used, 1)
                    dve.wait_ge(relu_used, IH * (i - 2) + h + 1)
                link(v.tensor_tensor(sc[:, L - P:L], sc[:, L - P:L], K.diag_off[:], ALU.add))
                cur = sc
                for r in range(TOPK // 8):
                    m8 = top8[:, r % 2, :]
                    link(v.max(m8, cur))
                    if r < TOPK // 8 - 1:
                        link(v.match_replace(wk, m8, cur, FAR))
                        cur = wk
                thr = m8[:, 7:8]
                link(v.tensor_scalar(wk, sc, thr, None, ALU.is_gt, ALU.add, accum_out=count[:, 0:1]))
                link(v.tensor_scalar(count[:, 1:2], count[:, 0:1], -1.0, float(TOPK), ALU.mult, ALU.add))
                link(v.tensor_scalar(e, sc, thr, None, ALU.is_equal))
                link(v.tensor_tensor_scan(cu, K.ones[:, 0:1].to_broadcast([P, L]), e, 0.0, ALU.mult, ALU.add))
                link(v.scalar_tensor_tensor(cu, cu, count[:, 1:2], e, ALU.is_le, ALU.mult))
                link(v.scalar_tensor_tensor(wk, wk, -1.0, cu, ALU.add, ALU.add))
                link(v.tensor_scalar(T.bias[:, BIAS_AT[i]:BIAS_AT[i] + L], wk, -OFF, None, ALU.mult))


def attend(K, T):
    nc, ps = K.nc, K.ps
    with ExitStack() as ctx:
        def sb(name, shape):
            return ctx.enter_context(nc.sbuf_tensor(name, shape, F32))
        prob = sb("prob", [P, 2, SEQ])
        probT = sb("probT", [P, 2, SEQ])
        y = sb("y", [P, 2, D])
        top, nbias, total, inv = (sb(n, [P, 2]) for n in ("top", "nbias", "total", "inv"))
        qk, logits, nb = K.sem("qk_in_psum"), K.sem("logits_done"), K.sem("neg_max_done")
        probs, t_ps, t_moved = K.sem("probs_done"), K.sem("probT_in_psum"), K.sem("probT_done")
        o_ps, inv_done, o_done = K.sem("pv_in_psum"), K.sem("inv_done"), K.sem("y_head_done")
        y_ps, y_moved = K.sem("yT_in_psum"), K.sem("yT_done")
        block = ctx.enter_context(nc.Block())
        N = TT * AH

        def tile(n):
            return n // AH

        def turn_groups(n):
            return sum(1 if i < 4 else 2 for i in range(tile(n))) * AH + (n % AH) * (1 if tile(n) < 4 else 2)

        events, seen = [], {}
        for n in range(N + 1):
            if n < N:
                for q in range(turn_groups(n), turn_groups(n + 1) if n + 1 < N else turn_groups(n) + 2):
                    events.append(("prob", q, n))
            if n % AH == 2 and n > AH or n == N:
                i = (n - 1) // AH if n == N else tile(n) - 1
                events += [("y", 2 * i, i), ("y", 2 * i + 1, i)]
        for e, (kind, q, _) in enumerate(events):
            seen[kind, q] = e

        def bank_free(eng, e):
            if e >= 2:
                kind, q, _ = events[e - 2]
                eng.wait_ge(t_moved if kind == "prob" else y_moved, q + 1)

        @block.tensor
        def _(pe):
            def qk_unit(n):
                i, h = tile(n), n % AH
                rows = slice(HD * (h % 2), HD * (h % 2) + HD)
                if n >= 2:
                    pe.wait_ge(logits, n - 1)
                for c0 in range(0, P * (i + 1), 512):
                    w = min(512, P * (i + 1) - c0)
                    mm = nc.tensor.matmul(ps[:, 2 * (n % 2) + c0 // 512, 0:w], T.qT[rows, h // 2, P * i:P * i + P],
                                          T.kT[rows, h // (AH // KVH), c0:c0 + w], start=True, stop=True)
                mm.then_inc(qk, 1)

            def turn(n):
                i = tile(n)
                pe.wait_ge(probs, n + 1)
                for q in range(turn_groups(n), turn_groups(n) + (1 if i < 4 else 2)):
                    e = seen["prob", q]
                    bank_free(pe, e)
                    b0 = 4 * (q - turn_groups(n))
                    for b in range(b0, min(b0 + 4, i + 1)):
                        mm = nc.tensor.transpose(ps[:, 4 + e % 2, P * (b - b0):P * (b - b0) + P],
                                                 prob[:, n % 2, P * b:P * b + P], K.ident[:])
                    mm.then_inc(t_ps, 1)

            def pv(n):
                i, h = tile(n), n % AH
                g = h // (AH // KVH)
                pe.wait_ge(t_moved, turn_groups(n) + (1 if i < 4 else 2))
                if n >= 2:
                    pe.wait_ge(o_done, n - 1)
                for b in range(i + 1):
                    mm = nc.tensor.matmul(ps[:, 6 + n % 2, 0:HD], probT[:, n % 2, P * b:P * b + P],
                                          T.v[:, b, HD * g:HD * g + HD], start=(b == 0), stop=(b == i))
                mm.then_inc(o_ps, 1)

            def turn_y(i):
                pe.wait_ge(o_done, AH * (i + 1))
                for half in range(2):
                    e = seen["y", 2 * i + half]
                    bank_free(pe, e)
                    for j in range(4):
                        b = 4 * half + j
                        mm = nc.tensor.transpose(ps[:, 4 + e % 2, P * j:P * j + P], y[:, i % 2, P * b:P * b + P],
                                                 K.ident[:])
                    mm.then_inc(y_ps, 1)

            qk_unit(0)
            for n in range(N):
                if n + 1 < N:
                    qk_unit(n + 1)
                if n:
                    pv(n - 1)
                turn(n)
                if n % AH == 2 and n > AH:
                    turn_y(tile(n) - 1)
            pv(N - 1)
            turn_y(TT - 1)

        @block.vector
        def _(dve):
            def logit(n):
                i = tile(n)
                L = P * (i + 1)
                dve.wait_ge(qk, n + 1)
                if n >= 2:
                    dve.wait_ge(t_ps, turn_groups(n - 1))
                nc.vector.tensor_tensor_reduce(
                    out=prob[:, n % 2, 0:L], in0=ps[:, 2 * (n % 2):2 * (n % 2) + 2, :].rearrange("p a n -> p (a n)")[:, 0:L],
                    in1=T.bias[:, BIAS_AT[i]:BIAS_AT[i] + L], scale=1.0, scalar=FAR, op0=ALU.add, op1=ALU.max,
                    accum_out=top[:, n % 2:n % 2 + 1]).then_inc(logits, 1)
                dve.wait_ge(logits, n + 1)
                nc.vector.tensor_scalar(nbias[:, n % 2:n % 2 + 1], top[:, n % 2:n % 2 + 1], -ATT_SCALE, None,
                                        ALU.mult).then_inc(nb, 1)

            def head(n):
                i, h = tile(n), n % AH
                dve.wait_ge(probs, n + 1)
                nc.vector.reciprocal(inv[:, n % 2:n % 2 + 1], total[:, n % 2:n % 2 + 1]).then_inc(inv_done, 1)
                dve.wait_ge(inv_done, n + 1)
                dve.wait_ge(o_ps, n + 1)
                if h == 0 and i >= 2:
                    dve.wait_ge(y_ps, 2 * (i - 1))
                nc.vector.tensor_scalar(y[:, i % 2, HD * h:HD * h + HD], ps[:, 6 + n % 2, 0:HD], inv[:, n % 2:n % 2 + 1],
                                        None, ALU.mult).then_inc(o_done, 1)

            for n in range(N + 2):
                if n < N:
                    logit(n)
                if n >= 2:
                    head(n - 2)

        @block.scalar
        def _(act):
            e = 0

            def move(upto):
                nonlocal e
                while e < upto:
                    kind, q, n = events[e]
                    if kind == "prob":
                        i = tile(n)
                        b0 = 4 * (q - turn_groups(n))
                        w = P * (min(b0 + 4, i + 1) - b0)
                        act.wait_ge(t_ps, q + 1)
                        if n >= 2:
                            act.wait_ge(o_ps, n - 1)
                        nc.scalar.copy(probT[:, n % 2, P * b0:P * b0 + w], ps[:, 4 + e % 2, 0:w]).then_inc(t_moved, 1)
                    else:
                        act.wait_ge(y_ps, q + 1)
                        half = q % 2
                        nc.scalar.copy(T.qT[:, 4 * half:4 * half + 4, P * n:P * n + P],
                                       ps[:, 4 + e % 2, :].rearrange("p (b t) -> p b t", b=4)).then_inc(y_moved, 1)
                    e += 1

            def exp(n):
                L = P * (tile(n) + 1)
                act.wait_ge(nb, n + 1)
                if n >= 2:
                    act.wait_ge(inv_done, n - 1)
                nc.scalar.activation(prob[:, n % 2, 0:L], prob[:, n % 2, 0:L], ACT.Exp, bias=nbias[:, n % 2:n % 2 + 1],
                                     scale=ATT_SCALE, accum_out=total[:, n % 2:n % 2 + 1]).then_inc(probs, 1)

            exp(0)
            for n in range(1, N):
                exp(n)
                move(seen["prob", turn_groups(n)])
            move(len(events))


def attend_samples(K, T):
    nc, A, ps = K.nc, K.A, K.ps
    KP = 2
    with ExitStack() as ctx:
        def sb(name, shape, dt=F32):
            return ctx.enter_context(nc.sbuf_tensor(name, shape, dt))
        pages = sb("pages", [1, DEC * NPAGE], I32)
        kpage, vpage = sb("kpage", [P, DEC, NPAGE, 256]), sb("vpage", [P, DEC, NPAGE, 256])
        ipage = sb("ipage", [P, DEC, NPAGE, HD])
        q_r = sb("q_r", [DEC, D])
        skT = sb("skT", [P, DEC, KP, SKEYS])
        sqx = sb("sqx", [P, 2320])
        siT, sqiT = sb("siT", [HD, DEC, SKEYS]), sb("sqiT", [HD, DEC, IH])
        swx = sb("swx", [IH, 9 * DEC])
        srelu = sb("srelu", [IH, 2, SKEYS])
        who, whoT = sb("who", [DEC, P]), sb("whoT", [P, DEC])
        ssc, swk, seq_, scu, sbias = (sb(n, [DEC, SKEYS]) for n in ("ssc", "swk", "seq", "scu", "sbias"))
        s8, scount = sb("s8", [DEC, 8]), sb("scount", [DEC, 2])
        sp_, sdiag = sb("sprob", [P, SKEYS]), sb("sdiag", [P, P])
        spT, snew = sb("spT", [P, NPAGE, P]), sb("snew", [DEC, P])
        stat = sb("sstat", [P, 4])
        table_in, who_in = K.sem("page_table_in"), K.sem("who_in")
        i_in, k_in, v_in = K.sem("index_pages_in"), K.sem("key_pages_in"), K.sem("value_pages_in")
        step = K.sem("sample_step")
        pe_small, pe_idx, pe_key, pe_rel = K.sem("small_turned"), K.sem("ipages_turned"), K.sem("kpages_turned"), K.sem("srelu_in_psum")
        idx_moved, key_moved, rel_done = K.sem("siT_done"), K.sem("skT_done"), K.sem("srelu_done")
        pe_score, pe_logit, exp_done, pe_pT, pe_out = (K.sem(n) for n in (
            "sscore_in_psum", "slogits_in_psum", "sprobs_done", "sprobsT_in_psum", "sout_in_psum"))
        max_done, y_done, y_out = K.sem("smax_done"), K.sem("sample_y_done"), K.sem("y_att_stored")
        ready, biased, diag_done, pT_done = K.sem("small_done"), K.sem("sbias_done"), K.sem("sdiag_done"), K.sem("spT_done")
        block = ctx.enter_context(nc.Block())

        @block.sync
        def _(sp):
            sp.dma_start(pages[:], A["page_table"].rearrange("b j -> (b j)").unsqueeze(0)).then_inc(table_in, 16)
            sp.dma_start(who[:], A["k_who"]).then_inc(who_in, 16)
            sp.dma_start(A["s_att"].rearrange("k p n -> p k n")[:, :, 0:SEQ], T.qT[:, :, 0:SEQ]).then_inc(y_out, 16)
            sp.wait_ge(table_in, 16)
            for cache, dst, done in (("cache_kidx", ipage, i_in), ("cache_k", kpage, k_in), ("cache_v", vpage, v_in)):
                n_pool = A[cache].shape[1]
                for b in range(DEC):
                    for j in range(NPAGE):
                        at = sp.value_load(pages[0:1, NPAGE * b + j:NPAGE * b + j + 1], min_val=0, max_val=n_pool - 1)
                        src = A[cache][0, bass.ds(at, 1)]
                        src = src.rearrange("a t d -> (a t) d" if cache == "cache_kidx" else "a t g d -> (a t) (g d)")
                        sp.dma_start(dst[:, b, j, :], src).then_inc(done, 16)
            sp.wait_ge(y_done, 1)
            sp.dma_start(A["s_att"].rearrange("k p n -> p k n")[:, :, SEQ:NT], T.qT[:, :, SEQ:NT]).then_inc(y_out, 16)
            sp.wait_ge(y_out, 32)

        @block.tensor
        def _(pe):
            tr, mm = nc.tensor.transpose, nc.tensor.matmul
            i8, i4 = K.ident[0:DEC, 0:DEC], K.ident[0:DEC, 0:DEC]
            pe.wait_ge(step, 1)
            pe.wait_ge(who_in, 16)
            for m in range(KB):
                tr(ps[:, 0, DEC * m:DEC * m + DEC], q_r[:, P * m:P * m + P], i8)
            for p in range(KP):
                tr(ps[:, 0, 64 + DEC * p:72 + DEC * p], T.k_s[:, P * p:P * p + P], i8)
            tr(ps[0:HD, 0, 80:88], T.ki_s[:], i8)
            for h in range(IH):
                tr(ps[0:HD, 0, 88 + DEC * h:96 + DEC * h], T.qi_s[:, HD * h:HD * h + HD], i8)
            tr(ps[0:IH, 0, 120:128], T.wi[0:DEC, TT, :], i4)
            tr(ps[:, 0, 128:136], who[:], i8).then_inc(pe_small, 1)
            pe.wait_ge(i_in, 16 * DEC * NPAGE)
            for a in range(4):
                if a >= 2:
                    pe.wait_ge(idx_moved, a - 1)
                for b in range(2):
                    for j in range(NPAGE):
                        m = tr(ps[0:HD, 1 + a % 2, 256 * b + P * j:256 * b + P * j + P], ipage[:, 2 * a + b, j, :], K.ident[:])
                m.then_inc(pe_idx, 1)
            pe.wait_ge(ready, 1)
            pe.wait_ge(idx_moved, 4)
            for b in range(DEC + 1):
                if b < DEC:
                    if b >= 2:
                        pe.wait_ge(rel_done, b - 1)
                    mm(ps[0:IH, 3 + b % 2, 0:SKEYS], sqiT[:, b, :], siT[:, b, :], start=True, stop=True).then_inc(pe_rel, 1)
                if b:
                    pe.wait_ge(rel_done, b)
                    mm(ps[0:DEC, 5, 0:SKEYS], swx[:, DEC * (b - 1):DEC * b], srelu[:, (b - 1) % 2, :],
                       start=(b == 1), stop=(b == DEC)).then_inc(pe_score, 1)
            pe.wait_ge(k_in, 16 * DEC * NPAGE)
            for b in range(DEC):
                if b >= 2:
                    pe.wait_ge(key_moved, b - 1)
                for p in range(KP):
                    for j in range(NPAGE):
                        m = tr(ps[:, 6 + b % 2, 256 * p + P * j:256 * p + P * j + P], kpage[:, b, j, P * p:P * p + P], K.ident[:])
                m.then_inc(pe_key, 1)
            pe.wait_ge(key_moved, DEC)
            pe.wait_ge(biased, 1)
            mm(ps[:, 3, 0:SKEYS], who[:], sbias[:], start=True, stop=False)
            for b in range(DEC):
                for p in range(KP):
                    last = b == DEC - 1 and p == KP - 1
                    m = mm(ps[:, 3, 0:SKEYS], sqx[:, 256 * b + P * p:256 * b + P * p + P], skT[:, b, p, :],
                           start=False, stop=last)
            m.then_inc(pe_logit, 1)
            pe.wait_ge(diag_done, 1)
            for j in range(NPAGE):
                tr(ps[:, 4, P * j:P * j + P], sp_[:, P * j:P * j + P], K.ident[:])
            mm(ps[0:DEC, 5, 0:P], whoT[:], sdiag[:], start=True, stop=True).then_inc(pe_pT, 1)
            pe.wait_ge(pT_done, 1)
            pe.wait_ge(v_in, 16 * DEC * NPAGE)
            for p in range(KP):
                mm(ps[:, 6 + p, 0:P], T.v[0:DEC, TT, P * p:P * p + P], snew[:], start=True, stop=False)
                for b in range(DEC):
                    for j in range(NPAGE):
                        m = mm(ps[:, 6 + p, AH * b:AH * b + AH], vpage[:, b, j, P * p:P * p + P],
                               spT[:, j, AH * b:AH * b + AH], start=False, stop=(b == DEC - 1 and j == NPAGE - 1))
            m.then_inc(pe_out, 1)

        @block.scalar
        def _(act):
            for a in range(4):
                act.wait_ge(pe_idx, a + 1)
                nc.scalar.copy(siT[:, 2 * a:2 * a + 2, 0:PAST], ps[0:HD, 1 + a % 2, :]
                               .rearrange("p (b s) -> p b s", b=2)).then_inc(idx_moved, 1)
            for b in range(DEC):
                act.wait_ge(pe_rel, b + 1)
                if b >= 2:
                    act.wait_ge(pe_score, b - 1)
                nc.scalar.activation(srelu[:, b % 2, :], ps[0:IH, 3 + b % 2, 0:SKEYS], ACT.Relu).then_inc(rel_done, 1)
            for b in range(DEC):
                act.wait_ge(pe_key, b + 1)
                nc.scalar.copy(skT[:, b, :, 0:PAST], ps[:, 6 + b % 2, :]
                               .rearrange("p (k s) -> p k s", k=KP)).then_inc(key_moved, 1)
            act.wait_ge(max_done, 1)
            nc.scalar.activation(sp_[:], sp_[:], ACT.Exp, bias=stat[:, 1:2], scale=ATT_SCALE,
                                 accum_out=stat[:, 2:3]).then_inc(exp_done, 1)

        @block.vector
        def _(dve):
            n = [0]
            v = nc.vector

            def link(ins):
                n[0] += 1
                ins.then_inc(step, 1)
                dve.wait_ge(step, n[0])

            gq = AH // KVH
            for p in range(KP):
                src = T.q_s[:, 512 * p:512 * p + 512].rearrange("b (g r d) -> b r g d", g=2, r=gq)
                c = v.tensor_copy(q_r[:, 512 * p:512 * p + 512].rearrange("b (r g d) -> b r g d", r=gq, g=2), src)
            link(c)
            link(v.memset(sqx[:], 0.0))
            link(v.memset(swx[:], 0.0))
            dve.wait_ge(pe_small, 1)
            for p in range(KP):
                for g in range(2):
                    off = P * p + gq * (2 * p + g)
                    rows = slice(HD * g, HD * g + HD)
                    v.tensor_copy(sqx[rows, off:off + 272 * DEC].rearrange("p (b x) -> p b x", x=272)[:, :, 0:gq],
                                  ps[rows, 0, 32 * p:32 * p + 32].rearrange("p (r b) -> p b r", b=DEC))
            for p in range(KP):
                v.tensor_copy(skT[:, :, p, PAST], ps[:, 0, 64 + DEC * p:72 + DEC * p])
            v.tensor_copy(siT[:, :, PAST], ps[0:HD, 0, 80:88])
            v.tensor_copy(sqiT[:], ps[0:HD, 0, 88:120].rearrange("p (h b) -> p b h", h=IH))
            v.tensor_copy(swx[:].rearrange("p (b x) -> p b x", x=9)[:, :, 0], ps[0:IH, 0, 120:128])
            v.tensor_copy(whoT[:], ps[:, 0, 128:136]).then_inc(ready, 1)
            dve.wait_ge(pe_score, DEC)
            link(v.tensor_copy(ssc[:], ps[0:DEC, 5, 0:SKEYS]))
            cur = ssc
            for r in range(STOPK // 8):
                link(v.max(s8[:], cur[:]))
                if r < STOPK // 8 - 1:
                    link(v.match_replace(swk[:], s8[:], cur[:], FAR))
                    cur = swk
            thr = s8[:, 7:8]
            link(v.tensor_scalar(swk[:], ssc[:], thr, None, ALU.is_gt, ALU.add, accum_out=scount[:, 0:1]))
            link(v.tensor_scalar(scount[:, 1:2], scount[:, 0:1], -1.0, float(STOPK), ALU.mult, ALU.add))
            link(v.tensor_scalar(seq_[:], ssc[:], thr, None, ALU.is_equal))
            link(v.tensor_tensor_scan(scu[:], K.ones[0:DEC, 0:1].to_broadcast([DEC, SKEYS]), seq_[:], 0.0, ALU.mult, ALU.add))
            link(v.scalar_tensor_tensor(scu[:], scu[:], scount[:, 1:2], seq_[:], ALU.is_le, ALU.mult))
            link(v.scalar_tensor_tensor(swk[:], swk[:], -1.0, scu[:], ALU.add, ALU.add))
            v.tensor_scalar(sbias[:], swk[:], -OFF, None, ALU.mult).then_inc(biased, 1)
            dve.wait_ge(pe_logit, 1)
            link(v.tensor_copy(sp_[:], ps[:, 3, 0:SKEYS]))
            link(v.reduce_max(stat[:, 0:1], sp_[:], AX.X))
            v.tensor_scalar(stat[:, 1:2], stat[:, 0:1], -ATT_SCALE, None, ALU.mult).then_inc(max_done, 1)
            dve.wait_ge(exp_done, 1)
            link(v.reciprocal(stat[:, 3:4], stat[:, 2:3]))
            link(v.tensor_scalar(sp_[:], sp_[:], stat[:, 3:4], None, ALU.mult))
            v.tensor_scalar(sdiag[:], K.ident[:], sp_[:, PAST:SKEYS], None, ALU.mult).then_inc(diag_done, 1)
            dve.wait_ge(pe_pT, 1)
            v.tensor_copy(snew[:], ps[0:DEC, 5, 0:P])
            v.tensor_copy(spT[:].rearrange("p j h -> p (j h)"), ps[:, 4, 0:NPAGE * P]).then_inc(pT_done, 1)
            dve.wait_ge(pe_out, 1)
            for p in range(KP):
                for g in range(2):
                    for odd in range(2):
                        kv = 2 * p + g
                        src = ps[HD * g:HD * g + HD, 6 + p, 0:P].rearrange("p (b k a o) -> p k a o b", k=KVH, a=2, o=2)
                        c = v.tensor_copy(T.qT[HD * odd:HD * odd + HD, 2 * kv:2 * kv + 2, SEQ:NT], src[:, kv, :, odd, :])
            c.then_inc(y_done, 1)


def steps(K, S):
    nc, A, ps = K.nc, K.A, K.ps
    NC = TT * HEADS
    W = NC + DEC
    with ExitStack() as ctx:
        def sb(name, shape):
            return ctx.enter_context(nc.sbuf_tensor(name, shape, F32))
        u, e, z, t, p = (sb("dt_" + n, [P, W]) for n in "uezts")
        a_row, a_col = sb("a_row", [P, HEADS]), sb("a_col", [HEADS, 1])
        head_x = sb("head_x", [HEADS, INNER])
        spread = sb("spread", [HEADS, 17])
        d_end = sb("d_end", [P, NC])
        head_in, step = K.sem("head_in"), K.sem("dt_step")
        arg_ready, exp_done, a_done = K.sem("dt_arg"), K.sem("dt_exp"), K.sem("a_exp")
        dta_done, sums, decays = K.sem("dta_done"), K.sem("decay_sums"), K.sem("decays_done")
        sdec_arg, sdec, sp_ready, spread_ps = K.sem("sdecay_arg"), K.sem("sdecay_done"), K.sem("spread_ready"), K.sem("spread_in_psum")
        block = ctx.enter_context(nc.Block())

        @block.sync
        def _(sp):
            sp.dma_start(head_x[:], A["k_head"]).then_inc(head_in, 16)

        @block.scalar
        def _(act):
            nc.scalar.activation(a_row[:], K.heads_row[:, 1, :], ACT.Exp).then_inc(a_done, 1)
            nc.scalar.activation(a_col[:], K.heads_col[:, 1:2], ACT.Exp).then_inc(a_done, 1)
            act.wait_ge(arg_ready, 1)
            nc.scalar.activation(e[:], e[:], ACT.Exp).then_inc(exp_done, 1)
            act.wait_ge(sdec_arg, 1)
            nc.scalar.activation(spread[:, 0:DEC], spread[:, 0:DEC], ACT.Exp).then_inc(sdec, 1)
            act.wait_ge(sums, 1)
            for bank, dst in ((0, S.e_acs[:].rearrange("p c h -> p (c h)")), (1, d_end[:]),
                              (2, S.c_dec[:].rearrange("p c h -> p (c h)"))):
                nc.scalar.activation(dst, ps[:, bank, 0:NC], ACT.Exp).then_inc(decays, 1)

        @block.tensor
        def _(pe):
            pe.wait_ge(dta_done, 1)
            dta = S.dta[:].rearrange("p c h -> p (c h)")
            nc.tensor.matmul(ps[:, 0, 0:NC], K.le[:], dta, start=True, stop=True)
            nc.tensor.matmul(ps[:, 1, 0:NC], K.gt[:], dta, start=True, stop=True)
            nc.tensor.matmul(ps[:, 2, 0:NC], K.ones[:], dta, start=True, stop=True).then_inc(sums, 1)
            pe.wait_ge(sp_ready, 1)
            pe.wait_ge(head_in, 16)
            for b in range(INNER // P):
                mm = nc.tensor.matmul(ps[:, 3, 17 * b:17 * b + 17], head_x[:, P * b:P * b + P], spread[:],
                                      start=True, stop=True)
            mm.then_inc(spread_ps, 1)

        @block.vector
        def _(dve):
            n = [0]
            v = nc.vector

            def link(ins):
                n[0] += 1
                ins.then_inc(step, 1)
                dve.wait_ge(step, n[0])

            link(v.memset(u[:, NC:W], 0.0))
            link(v.tensor_tensor(u[:, 0:NC].rearrange("p (c h) -> p c h", h=HEADS), K.dt_raw[:],
                                 K.heads_row[:, 0, :].unsqueeze(1).to_broadcast([P, TT, HEADS]), ALU.add))
            link(v.tensor_scalar(u[0:HEADS, NC:W], K.dtT_raw[:], K.heads_col[:, 0:1], None, ALU.add))
            v.scalar_tensor_tensor(e[:], u[:], -1.0, u[:], ALU.mult, ALU.min).then_inc(arg_ready, 1)
            dve.wait_ge(exp_done, 1)
            link(v.tensor_scalar(t[:], e[:], 2.0, None, ALU.add))
            link(v.reciprocal(t[:], t[:]))
            link(v.tensor_tensor(z[:], e[:], t[:], ALU.mult))
            link(v.tensor_tensor(t[:], z[:], z[:], ALU.mult))
            link(v.tensor_scalar(p[:], t[:], 1.0 / 15.0, None, ALU.mult))
            for k in (13, 11, 9, 7, 5, 3):
                link(v.scalar_tensor_tensor(p[:], p[:], 1.0 / k, t[:], ALU.add, ALU.mult))
            link(v.scalar_tensor_tensor(z[:], p[:], 1.0, z[:], ALU.add, ALU.mult))
            link(v.tensor_scalar(u[:], u[:], 0.0, None, ALU.max))
            link(v.scalar_tensor_tensor(u[:], z[:], 2.0, u[:], ALU.mult, ALU.add))
            dve.wait_ge(a_done, 2)
            dt3 = u[:, 0:NC].rearrange("p (c h) -> p c h", h=HEADS)
            link(v.tensor_copy(S.dt[:], dt3))
            link(v.tensor_scalar(a_row[:], a_row[:], -1.0, None, ALU.mult))
            v.tensor_tensor(S.dta[:], dt3, a_row[:].unsqueeze(1).to_broadcast([P, TT, HEADS]), ALU.mult).then_inc(dta_done, 1)
            link(v.tensor_scalar(a_col[:], a_col[:], -1.0, None, ALU.mult))
            link(v.tensor_copy(spread[:, DEC:2 * DEC], u[0:HEADS, NC:W]))
            link(v.tensor_copy(spread[:, 16:17], K.heads_col[:, 2:3]))
            v.tensor_scalar(spread[:, 0:DEC], u[0:HEADS, NC:W], a_col[:], None, ALU.mult).then_inc(sdec_arg, 1)
            dve.wait_ge(sdec, 1)
            link(v.tensor_copy(a_col[:], a_col[:]))
            v.tensor_copy(a_col[:], K.heads_col[:, 0:1]).then_inc(sp_ready, 1)
            dve.wait_ge(decays, 3)
            link(v.tensor_tensor(S.ddt[:].rearrange("p c h -> p (c h)"), d_end[:], u[:, 0:NC], ALU.mult))
            dve.wait_ge(spread_ps, 1)
            link(v.tensor_copy(S.hx[:].rearrange("p b s -> p (b s)"), ps[:, 3, 0:17 * 16]))


def ssm(K, hT, S):
    nc, A, ps = K.nc, K.A, K.ps
    first = K.span["g0"][0]
    FBS = 6
    PW = CONV - 1 + NT
    with ExitStack() as ctx:
        def sb(name, shape):
            return ctx.enter_context(nc.sbuf_tensor(name, shape, F32))
        pre = sb("pre", [P, 2, PW])
        post = sb("post", [P, FBS, SEQ])
        z = sb("z", [P, TT, GW])
        tail = sb("tail", [P, FBS, 11])
        tail_rows = sb("tail_rows", [11, FBS, P])
        st_rows = sb("st_rows", [DEC * 3, FBS, P])
        wg = sb("wg", [P, 5, FBS])
        cx, ct = sb("cx", [P, FBS, DEC]), sb("ct", [P, FBS, DEC])
        zs, xdt_s = sb("zs", [P, 4, DEC]), sb("xdt_s", [P, 4, DEC])
        bc_diag = sb("bc_diag", [P, 2, 4, P])
        stt = sb("stt", [P, 4, 4, NST])
        tmp = sb("stmp", [P, 4, 4, NST])
        ysum = sb("ysum", [P, 4, DEC])
        ysq, yrs = sb("ysq", [P, 4, DEC]), sb("yrs", [P, DEC])
        cbm = sb("cbm", [P, 2, P])
        btok = sb("btok", [P, 2, P])
        seg = sb("seg", [P, GH, P])
        m = sb("m", [P, 2, GH, P])
        xt, xdt, xw, xd = sb("xt", [P, GW]), sb("xdt", [P, 2, GW]), sb("xw", [P, 2, GW]), sb("xd", [P, 2, GW])
        y, ysq2 = sb("ssm_y", [P, 2, GW]), sb("ssm_ysq", [P, GW])
        state = sb("state", [P, GW])
        yT = sb("ssm_yT", [P, 2, 4, P])
        stat = sb("ssm_stat", [P, 4, 2])
        fin = sb("fin", [P, 4, P])

        gemm, pre_done, conv_done, post_done = K.sem("xbc_sums"), K.sem("pre_done"), K.sem("conv_done"), K.sem("post_done")
        conv_step, tails = K.sem("conv_step"), K.sem("tails_kept")
        z_ps, z_done, zs_ps, zs_done = K.sem("z_sums"), K.sem("z_done"), K.sem("zs_sums"), K.sem("zs_done")
        st_in, st_used = K.store_sem("conv_state_in"), K.sem("conv_state_turned")
        rows_ps, rows_done, rows_out = K.sem("tail_rows_in_psum"), K.sem("tail_rows_done"), K.store_sem("tail_rows_stored")
        cs_sum, cs_done = K.sem("sample_conv_sum"), K.sem("sample_conv_done")
        diag, bc_ps, bc_used = K.sem("bc_diag_done"), K.sem("bc_in_psum"), K.sem("bc_used")
        s_in, s_dec, s_new, s_out = K.store_sem("states_in"), K.sem("states_decayed"), K.sem("states_new"), K.store_sem("states_stored")
        sstep, ysq_done, yss_ps, yroot, yrooted = (K.sem(n) for n in (
            "sample_ssm_step", "ysq_done", "ysq_summed", "yroot_arg", "yroot_done"))
        seg_in, seg_ps, m_exp, m_done = K.sem("seg_in"), K.sem("seg_in_psum"), K.sem("m_exp"), K.sem("m_done")
        bcb_ps, cb_done, xt_ps, xt_done = K.sem("cb_b_in_psum"), K.sem("cb_b_done"), K.sem("xt_in_psum"), K.sem("xt_done")
        xdt_done, xw_done, xd_done = K.sem("xdt_done"), K.sem("xw_done"), K.sem("xd_done")
        yd_ps, yo_ps, sp_ps = K.sem("ydiag_in_psum"), K.sem("yoff_in_psum"), K.sem("state_in_psum")
        yo_done, s_scaled, s_done, yd_done = K.sem("yoff_done"), K.sem("state_decayed"), K.sem("state_done"), K.sem("ydiag_done")
        ystep, ygated, ysquared, ymean, yroot2, ynormed = (K.sem(n) for n in (
            "y_step", "y_gated", "y_squared", "y_mean", "y_root", "y_normed"))
        yT_ps, yT_done, yT_out = K.sem("ssm_yT_in_psum"), K.sem("ssm_yT_done"), [K.store_sem(f"ssm_yT_stored{i}") for i in range(2)]
        fin_ps, fin_done, fin_out = K.sem("final_in_psum"), K.sem("final_done"), K.store_sem("final_stored")
        old_out = K.store_sem("old_conv_rows_stored")
        block = ctx.enter_context(nc.Block())

        def feature(g, f):
            return 4 * g + f if f < 4 else (16 + g if f == 4 else 20 + g)

        def slab(g, i):
            return first + 5 * g + i

        @block.sync
        def _(sp):
            for g in range(GROUPS):
                for i in range(5):
                    n = slab(g, i) + RING
                    if n < len(K.slabs):
                        if i < 3:
                            sp.wait_ge(gemm, 18 * g + 6 * (i + 1))
                        else:
                            sp.wait_ge(zs_ps, 2 * g + i - 2)
                        for place, src in K.slabs[n]:
                            sp.dma_start(place(K.ring[:, n % RING, :]), src).then_inc(K.landed[n % RING], 16)

        @block.gpsimd
        def _(pool):
            v = nc.gpsimd
            v.memset(pre[:, :, 0:CONV - 1], 0.0).then_inc(conv_step, 1)
            pool.dma_start(A["conv_sample"][0, :, 0:2, :], A["state_conv"][0, :, 1:3, :]).then_inc(old_out, 16)

            def rows_in(g):
                for f in range(FBS):
                    c = P * feature(g, f)
                    pool.dma_start(st_rows[:, f, :], A["state_conv"][0, :, :, c:c + P].rearrange("b j c -> (b j) c"))\
                        .then_inc(st_in, 16)

            def states(g, q, name):
                heads = A[name][0, 4 * q:4 * q + 4, GH * g:GH * g + GH]
                return heads.rearrange("b h p n -> b (h p) n").rearrange("b (k q) n -> q b k n", q=P)

            def store(g, c):
                pool.wait_ge(yT_done, TT * g + c + 1)
                pool.dma_start(A["s_ssm"].rearrange("k p n -> p k n")[:, 4 * g:4 * g + 4, P * c:P * c + P],
                               yT[:, c % 2]).then_inc(yT_out[c % 2], 16)

            rows_in(0)
            for g in range(GROUPS):
                for q in range(2):
                    h = 2 * g + q
                    if h:
                        pool.wait_ge(s_out, 16 * 4 * h)
                        pool.wait_ge(bc_used, h)
                    for b in range(4):
                        pool.dma_start(stt[:, b], states(g, q, "state_ssm")[:, b]).then_inc(s_in, 16)
                    pool.wait_ge(cs_done, g + 1)
                    if h:
                        pool.wait_ge(bc_ps, 2 * h)
                    for k in range(2):
                        v.tensor_tensor(bc_diag[:, k], K.ident[:].unsqueeze(1).to_broadcast([P, 4, P]),
                                        cx[:, 4 + k, 4 * q:4 * q + 4].unsqueeze(2).to_broadcast([P, 4, P]), ALU.mult)\
                            .then_inc(diag, 1)
                    pool.wait_ge(s_in, 16 * 4 * (h + 1))
                    for b in range(4):
                        d = v.tensor_tensor(stt[:, b], stt[:, b],
                                            S.hx[:, 4 * g:4 * g + 4, 4 * q + b].unsqueeze(2).to_broadcast([P, 4, NST]),
                                            ALU.mult)
                    d.then_inc(s_dec, 1)
                    if q == 0:
                        pool.wait_ge(rows_done, 2 * (g + 1))
                        for f in range(FBS):
                            c = P * feature(g, f)
                            pool.dma_start(A["conv_prompt"][0, 0, :, c:c + P], tail_rows[0:3, f, :]).then_inc(rows_out, 16)
                            pool.dma_start(A["conv_sample"][0, :, 2, c:c + P], tail_rows[3:11, f, :]).then_inc(rows_out, 16)
                        if g + 1 < GROUPS:
                            pool.wait_ge(st_used, g + 1)
                            rows_in(g + 1)
                    pool.wait_ge(s_new, h + 1)
                    for b in range(4):
                        pool.dma_start(states(g, q, "ssm_sample")[:, b], stt[:, b]).then_inc(s_out, 16)
                for c in range(TT):
                    n = TT * g + c
                    if n:
                        pool.wait_ge(seg_ps, n)
                    v.tensor_tensor(seg[:], K.le[:].unsqueeze(1).to_broadcast([P, GH, P]),
                                    S.dta[:, c, GH * g:GH * g + GH].unsqueeze(2).to_broadcast([P, GH, P]), ALU.mult)\
                        .then_inc(seg_in, 1)
                    pool.wait_ge(xt_done, n + 1)
                    if n >= 2:
                        pool.wait_ge(sp_ps, n - 1)
                        pool.wait_ge(yd_done, 2 * (n - 1))
                    xh = xt[:].rearrange("p (h d) -> p h d", d=HD)

                    def per_head(vec):
                        return vec.unsqueeze(2).to_broadcast([P, GH, HD])
                    v.tensor_tensor(xw[:, c % 2].rearrange("p (h d) -> p h d", d=HD), xh,
                                    per_head(S.ddt[:, c, GH * g:GH * g + GH]), ALU.mult).then_inc(xw_done, 1)
                    v.tensor_tensor(xd[:, c % 2].rearrange("p (h d) -> p h d", d=HD), xh,
                                    per_head(K.heads_row[:, 2, GH * g:GH * g + GH]), ALU.mult).then_inc(xd_done, 1)
                    if c >= 2:
                        store(g, c - 2)
                store(g, TT - 2)
                store(g, TT - 1)
                pool.wait_ge(fin_done, g + 1)
                pool.dma_start(A["ssm_prompt"][0, 0].rearrange("h p n -> (h p) n")[GW * g:GW * g + GW]
                               .rearrange("(k q) n -> q k n", q=P), fin[:]).then_inc(fin_out, 16)
            pool.wait_ge(s_out, 16 * 8 * GROUPS)
            pool.wait_ge(rows_out, 16 * 2 * FBS * GROUPS)
            for i in range(2):
                pool.wait_ge(yT_out[i], 8 * TT * GROUPS)
            pool.wait_ge(fin_out, 16 * GROUPS)
            pool.wait_ge(old_out, 16)

        @block.tensor
        def _(pe):
            tr, mm = nc.tensor.transpose, nc.tensor.matmul

            def front(g, c):
                n = TT * g + c
                cols = slice(P * c, P * c + P)
                if c == 0:
                    pe.wait_ge(post_done, FBS * (g + 1))
                if n:
                    pe.wait_ge(cb_done, 2 * n)
                tr(ps[:, 0, P:2 * P], post[:, 4, cols], K.ident[:])
                mm(ps[:, 0, 0:P], post[:, 4, cols], post[:, 5, cols], start=True, stop=True).then_inc(bcb_ps, 1)
                if n:
                    pe.wait_ge(xt_done, n)
                    pe.wait_ge(xdt_done, n)
                for j in range(4):
                    t = tr(ps[:, 3, P * j:P * j + P], post[:, j, cols], K.ident[:])
                t.then_inc(xt_ps, 1)
                pe.wait_ge(seg_in, n + 1)
                if n:
                    pe.wait_ge(m_exp, n)
                for half in range(2):
                    s = mm(ps[:, 1 + half, :], K.gt[:], seg[:, 4 * half:4 * half + 4, :].rearrange("p h l -> p (h l)"),
                           start=True, stop=True)
                s.then_inc(seg_ps, 1)

            def back(g, c):
                n = TT * g + c
                cols = slice(P * c, P * c + P)
                pe.wait_ge(m_done, n + 1)
                pe.wait_ge(xdt_done, n + 1)
                if n:
                    pe.wait_ge(yd_done, 2 * n)
                for r in range(GH):
                    d = mm(ps[:, 5, HD * r:HD * r + HD], m[:, c % 2, r, :], xdt[:, c % 2, HD * r:HD * r + HD],
                           start=True, stop=True)
                d.then_inc(yd_ps, 1)
                if c:
                    pe.wait_ge(s_done, n)
                    if n > 1:
                        pe.wait_ge(yo_done, n - g - 1)
                    mm(ps[:, 4, :], post[:, 5, cols], state[:], start=True, stop=True).then_inc(yo_ps, 1)
                pe.wait_ge(xw_done, n + 1)
                pe.wait_ge(cb_done, 2 * n + 2)
                if n:
                    pe.wait_ge(s_done, n)
                mm(ps[:, 6, :], btok[:, c % 2, :], xw[:, c % 2, :], start=True, stop=True).then_inc(sp_ps, 1)

            def turn(g, c):
                n = TT * g + c
                pe.wait_ge(ynormed, n + 1)
                if n:
                    pe.wait_ge(yT_done, n)
                for j in range(4):
                    t = tr(ps[:, 7, P * j:P * j + P], y[:, c % 2, P * j:P * j + P], K.ident[:])
                t.then_inc(yT_ps, 1)

            for g in range(GROUPS):
                if g:
                    pe.wait_ge(yT_done, TT * g)
                    pe.wait_ge(fin_done, g)
                for f in range(FBS):
                    if f % 2 == 0:
                        pe.wait_ge(*ring_landed(K, slab(g, f // 2)))
                    w = slab_of(K, slab(g, f // 2))
                    for c in range(TC):
                        u = 18 * g + 3 * f + c
                        if u >= 4:
                            pe.wait_ge(pre_done, u - 3)
                        for k in range(KB):
                            a = mm(ps[:, 4 + u % 4, 0:CW], w[:, k, P * (f % 2):P * (f % 2) + P],
                                   hT[:, k, CW * c:CW * c + CW], start=(k == 0), stop=(k == KB - 1))
                        a.then_inc(gemm, 1)
                for i in range(2):
                    n = slab(g, 3 + i)
                    pe.wait_ge(*ring_landed(K, n))
                    w = slab_of(K, n)
                    for t in range(TT):
                        u = 16 * g + 8 * i + t
                        if u >= 4:
                            pe.wait_ge(z_done, u - 3)
                        if g and i == 0 and t < 4:
                            pe.wait_ge(m_exp, TT * g)
                            pe.wait_ge(cb_done, 2 * TT * g)
                            pe.wait_ge(xdt_done, TT * g)
                        for k in range(KB):
                            a = mm(ps[:, u % 4, 0:256], hT[:, k, P * t:P * t + P], w[:, k, :],
                                   start=(k == 0), stop=(k == KB - 1))
                        a.then_inc(z_ps, 1)
                    if i == 0:
                        pe.wait_ge(pre_done, 18 * (g + 1))
                    for fb in range(2):
                        for k in range(KB):
                            a = mm(ps[:, 4, DEC * (2 * i + fb):DEC * (2 * i + fb) + DEC], w[:, k, P * fb:P * fb + P],
                                   hT[:, k, SEQ:NT], start=(k == 0), stop=(k == KB - 1))
                    a.then_inc(zs_ps, 1)
                    if i == 0:
                        pe.wait_ge(st_in, 16 * FBS * (g + 1))
                        for f in range(FBS):
                            t = tr(ps[:, 5, 24 * f:24 * f + 24], st_rows[:, f, :], K.ident[0:24, 0:24])
                        t.then_inc(st_used, 1)
                        pe.wait_ge(tails, FBS * (g + 1))
                        for f in range(FBS):
                            t = tr(ps[0:11, 6 + f // 3, P * (f % 3):P * (f % 3) + P], tail[:, f, :], K.ident[:])
                        t.then_inc(rows_ps, 1)
                for q in range(2):
                    h = 2 * g + q
                    pe.wait_ge(diag, 2 * h + 2)
                    if q == 0:
                        pe.wait_ge(rows_done, 2 * (g + 1))
                    else:
                        pe.wait_ge(bc_used, h)
                    for k in range(2):
                        mm(ps[:, 6 + k, :], K.ones[:], bc_diag[:, k].rearrange("p b n -> p (b n)"),
                           start=True, stop=True).then_inc(bc_ps, 1)
                pe.wait_ge(ysq_done, g + 1)
                for j in range(4):
                    a = mm(ps[:, 5, 0:DEC], K.ones[:], ysq[:, j, :], start=(j == 0), stop=(j == 3))
                a.then_inc(yss_ps, 1)
                pe.wait_ge(z_done, 16 * (g + 1))
                pe.wait_ge(zs_done, g + 1)
                pe.wait_ge(bc_used, 2 * (g + 1))
                pe.wait_ge(yroot, g + 1)
                front(g, 0)
                for c in range(TT):
                    if c + 1 < TT:
                        front(g, c + 1)
                    back(g, c)
                    if c:
                        turn(g, c - 1)
                turn(g, TT - 1)
                pe.wait_ge(s_done, TT * (g + 1))
                for j in range(4):
                    t = tr(ps[:, 4, P * j:P * j + P], state[:, P * j:P * j + P], K.ident[:])
                t.then_inc(fin_ps, 1)

        @block.scalar
        def _(act):
            a = nc.scalar
            for g in range(GROUPS):
                def silu(f):
                    act.wait_ge(conv_done, FBS * g + f + 1)
                    a.activation(post[:, f, :], post[:, f, :], ACT.Silu).then_inc(post_done, 1)
                for f in range(FBS):
                    for c in range(TC):
                        u = 18 * g + 3 * f + c
                        act.wait_ge(gemm, u + 1)
                        if c == 0 and FBS * g + f >= 2:
                            act.wait_ge(conv_done, FBS * g + f - 1)
                            act.wait_ge(tails, FBS * g + f - 1)
                        a.copy(pre[:, f % 2, CONV - 1 + CW * c:CONV - 1 + CW * c + CW], ps[:, 4 + u % 4, 0:CW])\
                            .then_inc(pre_done, 1)
                    if f:
                        silu(f - 1)
                silu(FBS - 1)

                def z_rows(i):
                    for t in range(TT):
                        u = 16 * g + 8 * i + t
                        act.wait_ge(z_ps, u + 1)
                        if g and i == 0 and t == 0:
                            act.wait_ge(ygated, TT * g)
                        a.activation(z[:, t, 256 * i:256 * i + 256], ps[:, u % 4, 0:256], ACT.Silu).then_inc(z_done, 1)
                z_rows(0)
                act.wait_ge(rows_ps, g + 1)
                if g:
                    act.wait_ge(rows_out, 16 * 2 * FBS * g)
                for half in range(2):
                    a.copy(tail_rows[:, 3 * half:3 * half + 3, :].rearrange("p f c -> p (f c)"),
                           ps[0:11, 6 + half, 0:3 * P]).then_inc(rows_done, 1)
                act.wait_ge(cs_sum, g + 1)
                a.activation(cx[:], ct[:], ACT.Silu).then_inc(cs_done, 1)
                z_rows(1)
                act.wait_ge(zs_ps, 2 * g + 2)
                a.activation(zs[:].rearrange("p b s -> p (b s)"), ps[:, 4, 0:4 * DEC], ACT.Silu).then_inc(zs_done, 1)
                act.wait_ge(yroot, g + 1)
                a.activation(yrs[:], yrs[:], ACT.Sqrt).then_inc(yrooted, 1)

                def decay(c):
                    n = TT * g + c
                    act.wait_ge(xt_ps, n + 1)
                    if n:
                        act.wait_ge(xd_done, n)
                    a.copy(xt[:], ps[:, 3, :]).then_inc(xt_done, 1)
                    act.wait_ge(seg_ps, n + 1)
                    if n >= 2:
                        act.wait_ge(yd_ps, n - 1)
                    a.activation(m[:, c % 2].rearrange("p h l -> p (h l)"), ps[:, 1:3, :].rearrange("p a n -> p (a n)"),
                                 ACT.Exp).then_inc(m_exp, 1)

                def norm(c):
                    n = TT * g + c
                    act.wait_ge(ygated, n + 1)
                    if n:
                        act.wait_ge(ysquared, n)
                    a.activation(ysq2[:], y[:, c % 2, :], ACT.Square, accum_out=stat[:, 0, c % 2:c % 2 + 1])\
                        .then_inc(ysquared, 1)
                    act.wait_ge(ymean, n + 1)
                    a.activation(stat[:, 2, c % 2:c % 2 + 1], stat[:, 1, c % 2:c % 2 + 1], ACT.Sqrt).then_inc(yroot2, 1)

                def out(c):
                    n = TT * g + c
                    act.wait_ge(yT_ps, n + 1)
                    if n >= 2:
                        act.wait_ge(yT_out[c % 2], 16 * (n // 2))
                    for j in range(4):
                        k = 136 + 4 * g + j
                        o = a.activation(yT[:, c % 2, j, :], ps[:, 7, P * j:P * j + P], ACT.Copy, scale=K.vecs[:, k:k + 1])
                    o.then_inc(yT_done, 1)

                decay(0)
                for c in range(TT):
                    if c + 1 < TT:
                        decay(c + 1)
                    norm(c)
                    if c:
                        out(c - 1)
                out(TT - 1)
                act.wait_ge(fin_ps, g + 1)
                if g:
                    act.wait_ge(fin_out, 16 * g)
                a.copy(fin[:].rearrange("p k n -> p (k n)"), ps[:, 4, :]).then_inc(fin_done, 1)

        @block.vector
        def _(dve):
            v = nc.vector
            nconv, nss, ny = [0], [0], [0]

            def link(ins, sem, count):
                count[0] += 1
                ins.then_inc(sem, 1)
                dve.wait_ge(sem, count[0])

            nconv[0] = 1
            for g in range(GROUPS):
                for f in range(FBS):
                    b = feature(g, f)
                    src = pre[:, f % 2, :]
                    dve.wait_ge(pre_done, 18 * g + 3 * f + 3)
                    if g == 0 and f == 0:
                        dve.wait_ge(conv_step, 1)
                    if g and f == 0:
                        dve.wait_ge(yT_done, TT * g)
                        dve.wait_ge(st_used, g)
                        dve.wait_ge(rows_ps, g)
                    v.tensor_copy(tail[:, f, :], src[:, SEQ:PW]).then_inc(tails, 1)
                    link(v.tensor_scalar(post[:, f, :], src[:, 0:SEQ], K.vecs[:, b:b + 1], K.vecs[:, 96 + b:97 + b],
                                         ALU.mult, ALU.add), conv_step, nconv)
                    for i in range(1, CONV):
                        ins = v.scalar_tensor_tensor(post[:, f, :], src[:, i:i + SEQ], K.vecs[:, 24 * i + b:24 * i + b + 1],
                                                     post[:, f, :], ALU.mult, ALU.add)
                        if i < CONV - 1:
                            link(ins, conv_step, nconv)
                        else:
                            ins.then_inc(conv_done, 1)
                allv = K.vecs[:, 0:120].rearrange("p (i b) -> p i b", b=24)
                v.tensor_copy(wg[:, :, 0:4], allv[:, :, 4 * g:4 * g + 4])
                v.tensor_copy(wg[:, :, 4:5], allv[:, :, 16 + g:17 + g])
                link(v.tensor_copy(wg[:, :, 5:6], allv[:, :, 20 + g:21 + g]), sstep, nss)
                dve.wait_ge(st_used, g + 1)
                dve.wait_ge(tails, FBS * (g + 1))
                if g:
                    dve.wait_ge(cs_done, g)

                def tap(i):
                    return wg[:, i, :].unsqueeze(2).to_broadcast([P, FBS, DEC])
                old = ps[:, 5, 0:24 * FBS].rearrange("p (f b j) -> p f b j", f=FBS, j=3)
                link(v.tensor_tensor(ct[:], tail[:, :, 3:11], tap(3), ALU.mult), sstep, nss)
                link(v.tensor_tensor(ct[:], ct[:], tap(4), ALU.add), sstep, nss)
                for i in range(3):
                    w8 = tmp[:, 0, 0, 0:FBS * DEC].rearrange("p (f b) -> p f b", f=FBS)
                    link(v.tensor_tensor(w8, old[:, :, :, i], tap(i), ALU.mult), sstep, nss)
                    ins = v.tensor_tensor(ct[:], ct[:], w8, ALU.add)
                    if i < 2:
                        link(ins, sstep, nss)
                    else:
                        ins.then_inc(cs_sum, 1)
                dve.wait_ge(cs_done, g + 1)
                hx = S.hx[:, 4 * g:4 * g + 4, :]
                link(v.tensor_tensor(xdt_s[:], cx[:, 0:4, :], hx[:, :, 8:16], ALU.mult), sstep, nss)
                for q in range(2):
                    h = 2 * g + q
                    dve.wait_ge(bc_ps, 2 * h + 2)
                    for b in range(4):
                        bb = ps[:, 6, P * b:P * b + P].unsqueeze(1).to_broadcast([P, 4, NST])
                        t = v.tensor_tensor(tmp[:, b], bb, xdt_s[:, :, 4 * q + b].unsqueeze(2).to_broadcast([P, 4, NST]), ALU.mult)
                    link(t, sstep, nss)
                    dve.wait_ge(s_dec, h + 1)
                    v.tensor_tensor(stt[:], stt[:], tmp[:], ALU.add).then_inc(s_new, 1)
                    dve.wait_ge(s_new, h + 1)
                    for b in range(4):
                        cc = ps[:, 7, P * b:P * b + P].unsqueeze(1).to_broadcast([P, 4, NST])
                        t = v.tensor_tensor(tmp[:, b], cc, stt[:, b], ALU.mult)
                    t.then_inc(bc_used, 1)
                    dve.wait_ge(bc_used, h + 1)
                    link(v.tensor_reduce(ysum[:, :, 4 * q:4 * q + 4].rearrange("p k b -> p b k"), tmp[:], AX.X, ALU.add),
                         sstep, nss)
                link(v.tensor_tensor(xdt_s[:], cx[:, 0:4, :], hx[:, :, 16:17].to_broadcast([P, 4, DEC]), ALU.mult), sstep, nss)
                link(v.tensor_tensor(ysum[:], ysum[:], xdt_s[:], ALU.add), sstep, nss)
                dve.wait_ge(zs_done, g + 1)
                link(v.tensor_tensor(ysum[:], ysum[:], zs[:], ALU.mult), sstep, nss)
                v.tensor_tensor(ysq[:], ysum[:], ysum[:], ALU.mult).then_inc(ysq_done, 1)
                dve.wait_ge(yss_ps, g + 1)
                v.tensor_scalar(yrs[:], ps[:, 5, 0:DEC], 1.0 / GW, EPS, ALU.mult, ALU.add).then_inc(yroot, 1)
                dve.wait_ge(yrooted, g + 1)
                link(v.reciprocal(yrs[:], yrs[:]), sstep, nss)
                link(v.tensor_tensor(ysum[:], ysum[:], yrs[:].unsqueeze(1).to_broadcast([P, 4, DEC]), ALU.mult), sstep, nss)
                ng = K.vecs[:, 136 + 4 * g:140 + 4 * g].unsqueeze(2).to_broadcast([P, 4, DEC])
                link(v.tensor_tensor(S.ysT[:, 4 * g:4 * g + 4, :], ysum[:], ng, ALU.mult), sstep, nss)

                def heads(vec):
                    return vec.unsqueeze(2).to_broadcast([P, GH, HD])

                def front(c):
                    n = TT * g + c
                    dve.wait_ge(bcb_ps, n + 1)
                    if n >= 2:
                        dve.wait_ge(sp_ps, n - 1)
                    v.tensor_tensor(cbm[:, c % 2, :], ps[:, 0, 0:P], K.le[:], ALU.mult).then_inc(cb_done, 1)
                    v.tensor_copy(btok[:, c % 2, :], ps[:, 0, P:2 * P]).then_inc(cb_done, 1)
                    dve.wait_ge(xt_ps, n + 1)
                    dve.wait_ge(xt_done, n + 1)
                    if n >= 2:
                        dve.wait_ge(yd_ps, n - 1)
                    v.tensor_tensor(xdt[:, c % 2, :].rearrange("p (h d) -> p h d", d=HD),
                                    ps[:, 3, :].rearrange("p (h d) -> p h d", d=HD),
                                    heads(S.dt[:, c, GH * g:GH * g + GH]), ALU.mult).then_inc(xdt_done, 1)
                    dve.wait_ge(m_exp, n + 1)
                    dve.wait_ge(cb_done, 2 * n + 2)
                    v.tensor_tensor(m[:, c % 2], m[:, c % 2], cbm[:, c % 2, :].unsqueeze(1).to_broadcast([P, GH, P]),
                                    ALU.mult).then_inc(m_done, 1)

                def back(c):
                    n = TT * g + c
                    yc = y[:, c % 2, :]
                    yh = yc.rearrange("p (h d) -> p h d", d=HD)
                    dve.wait_ge(yd_ps, n + 1)
                    dve.wait_ge(xd_done, n + 1)
                    if n >= 2:
                        dve.wait_ge(yT_ps, n - 1)
                    v.tensor_tensor(yc, ps[:, 5, :], xd[:, c % 2, :], ALU.add).then_inc(yd_done, 2)
                    if c:
                        t = tmp[:, 0].rearrange("p k n -> p (k n)")
                        dve.wait_ge(yo_ps, n - g)
                        v.tensor_tensor(t.rearrange("p (h d) -> p h d", d=HD), ps[:, 4, :].rearrange("p (h d) -> p h d", d=HD),
                                        heads(S.e_acs[:, c, GH * g:GH * g + GH]), ALU.mult).then_inc(yo_done, 1)
                        dve.wait_ge(yo_done, n - g)
                        dve.wait_ge(yd_done, 2 * (n + 1))
                        link(v.tensor_tensor(yc, yc, t, ALU.add), ystep, ny)
                    else:
                        dve.wait_ge(yd_done, 2 * (n + 1))
                    v.tensor_tensor(yc, yc, z[:, c, :], ALU.mult).then_inc(ygated, 1)
                    dve.wait_ge(sp_ps, n + 1)
                    if c == 0:
                        if g:
                            dve.wait_ge(fin_ps, g)
                        v.tensor_copy(state[:], ps[:, 6, :]).then_inc(s_done, 1)
                    else:
                        sh = state[:].rearrange("p (h d) -> p h d", d=HD)
                        dve.wait_ge(s_done, n)
                        v.tensor_tensor(sh, sh, heads(S.c_dec[:, c, GH * g:GH * g + GH]), ALU.mult).then_inc(s_scaled, 1)
                        dve.wait_ge(s_scaled, n - g)
                        v.tensor_tensor(state[:], state[:], ps[:, 6, :], ALU.add).then_inc(s_done, 1)
                    i = c % 2
                    dve.wait_ge(ysquared, n + 1)
                    v.tensor_scalar(stat[:, 1, i:i + 1], stat[:, 0, i:i + 1], 1.0 / GW, EPS, ALU.mult, ALU.add).then_inc(ymean, 1)

                def scale(c):
                    n = TT * g + c
                    i = c % 2
                    dve.wait_ge(yroot2, n + 1)
                    link(v.reciprocal(stat[:, 3, i:i + 1], stat[:, 2, i:i + 1]), ystep, ny)
                    v.tensor_scalar(y[:, i, :], y[:, i, :], stat[:, 3, i:i + 1], None, ALU.mult).then_inc(ynormed, 1)

                front(0)
                for c in range(TT):
                    if c + 1 < TT:
                        front(c + 1)
                    back(c)
                    scale(c)


def merge(K, merged):
    nc, A, ps = K.nc, K.A, K.ps
    first = K.span["merge"][0]
    with ExitStack() as ctx:
        def sb(name, shape):
            return ctx.enter_context(nc.sbuf_tensor(name, shape, F32))
        yT = sb("m_yT", [P, 2 * KB, NT])
        aT = sb("m_aT", [P, KB, NT])
        sig = sb("m_sig", [P, 2, 2, NT])
        part = sb("m_part", [P, 2, CW])
        att_in, ssm_in = K.sem("m_att_in"), K.sem("m_ssm_in")
        sig_in = [K.store_sem(f"m_sig_in{i}") for i in range(2)]
        samples, gemm, part_done, merged_done = K.sem("m_samples"), K.sem("m_sums"), K.sem("m_part"), K.sem("m_done")
        block = ctx.enter_context(nc.Block())
        units = []
        for i in range(KB // 2):
            units += [("att", 3 * i, 2 * i + j, j, c) for j in range(2) for c in range(TC)]
            for j in range(2):
                units += [("ssm", 3 * i + 1 + j, 2 * i + j, 0, c) for c in range(TC)]

        @block.sync
        def _(sp):
            sp.dma_start(aT[:], A["s_att"].rearrange("k p n -> p k n")).then_inc(att_in, 16)
            sp.dma_start(yT[:, :, 0:SEQ], A["s_ssm"].rearrange("k p n -> p k n")).then_inc(ssm_in, 16)
            ring_load(K, sp, "merge", lambda i: (gemm, 12 * (i // 3) + (6, 9, 12)[i % 3]))

        @block.gpsimd
        def _(pool):
            for b in range(KB):
                if b >= 2:
                    pool.wait_ge(merged_done, TC * (b - 1))
                for w in range(2):
                    pool.dma_start(sig[:, b % 2, w, :], A["s_sig"][KB * w + b]).then_inc(sig_in[b % 2], 16)

        @block.tensor
        def _(pe):
            pe.wait_ge(att_in, 16)
            slab = -1
            for u, (kind, s, b, j, c) in enumerate(units):
                if s != slab:
                    pe.wait_ge(*ring_landed(K, first + s))
                    slab = s
                if u == 6:
                    pe.wait_ge(ssm_in, 16)
                    pe.wait_ge(samples, 1)
                if u >= 8:
                    pe.wait_ge(part_done, u - 7)
                src, nk = (aT, KB) if kind == "att" else (yT, 2 * KB)
                w = slab_of(K, first + s, nk)
                for k in range(nk):
                    mm = nc.tensor.matmul(ps[:, u % 8, 0:CW], w[:, k, P * j:P * j + P], src[:, k, CW * c:CW * c + CW],
                                          start=(k == 0), stop=(k == nk - 1))
                mm.then_inc(gemm, 1)

        @block.vector
        def _(dve):
            v = nc.vector
            v.tensor_copy(yT[:, :, SEQ:NT], K.ysT[:]).then_inc(samples, 1)
            n_ssm = 0
            for u, (kind, s, b, j, c) in enumerate(units):
                cols = slice(CW * c, CW * c + CW)
                dve.wait_ge(gemm, u + 1)
                if c == 0 and kind == "att":
                    dve.wait_ge(sig_in[b % 2], 32 * (b // 2 + 1))
                if kind == "att":
                    v.tensor_tensor(merged[:, b, cols], ps[:, u % 8, 0:CW], sig[:, b % 2, 1, cols], ALU.mult).then_inc(part_done, 1)
                else:
                    v.tensor_tensor(part[:, n_ssm % 2, :], ps[:, u % 8, 0:CW], sig[:, b % 2, 0, cols], ALU.mult)\
                        .then_inc(part_done, 1)
                    dve.wait_ge(part_done, u + 1)
                    v.tensor_tensor(merged[:, b, cols], merged[:, b, cols], part[:, n_ssm % 2, :], ALU.add).then_inc(merged_done, 1)
                    n_ssm += 1


def project_out(K, merged, source):
    nc, A, ps = K.nc, K.A, K.ps
    first = K.span["out"][0]
    with ExitStack() as ctx:
        def sb(name, shape):
            return ctx.enter_context(nc.sbuf_tensor(name, shape, F32))
        x = sb("o_x", [P, 9, D])
        gate = sb("o_gate", [P, 2, D])
        part = sb("o_part", [P, 2, 256])
        x_in, gate_in, gemm = K.sem("o_x_in"), K.sem("o_gate_in"), K.sem("o_sums")
        part_done, added, out = K.sem("o_part_done"), K.sem("o_added"), K.store_sem("o_stored")
        block = ctx.enter_context(nc.Block())

        @block.sync
        def _(sp):
            for b in range(2):
                r = P if b == 0 else DEC
                sp.dma_start(gate[0:r, b, :], A["s_gates"][b, 0:r, :]).then_inc(gate_in, 16)
            for t in range(9):
                sp.dma_start(x[0:rows_of(t), t, :], source(t)).then_inc(x_in, 16)
            ring_load(K, sp, "out", lambda i: (gemm, 9 * (i + 1)))

        @block.gpsimd
        def _(pool):
            for t in range(9):
                pool.wait_ge(added, 27 + t + 1)
                pool.dma_start(A["s_x1"][P * t:P * t + rows_of(t), :], x[0:rows_of(t), t, :]).then_inc(out, 16)
            pool.wait_ge(out, 16 * 9)

        @block.tensor
        def _(pe):
            for s in range(4):
                w = slab_of(K, first + s)
                pe.wait_ge(*ring_landed(K, first + s))
                for t in range(9):
                    r, u = rows_of(t), 9 * s + t
                    if u >= 8:
                        pe.wait_ge(part_done, u - 7)
                    for k in range(KB):
                        mm = nc.tensor.matmul(ps[0:r, u % 8, 0:256], merged[:, k, P * t:P * t + r], w[:, k, :],
                                              start=(k == 0), stop=(k == KB - 1))
                    mm.then_inc(gemm, 1)

        @block.vector
        def _(dve):
            v = nc.vector
            dve.wait_ge(gate_in, 32)
            dve.wait_ge(x_in, 16 * 9)
            for s in range(4):
                for t in range(9):
                    r, u = rows_of(t), 9 * s + t
                    cols = slice(256 * s, 256 * s + 256)
                    dve.wait_ge(gemm, u + 1)
                    v.tensor_tensor(part[0:r, u % 2, :], ps[0:r, u % 8, 0:256], gate[0:r, t // TT, cols], ALU.mult)\
                        .then_inc(part_done, 1)
                    dve.wait_ge(part_done, u + 1)
                    v.tensor_tensor(x[0:r, t, cols], x[0:r, t, cols], part[0:r, u % 2, :], ALU.add).then_inc(added, 1)


def ffn_in(K, hT, act_T):
    nc, ps = K.nc, K.ps
    first = K.span["ffn"][0]
    with ExitStack() as ctx:
        gate = ctx.enter_context(nc.sbuf_tensor("f_gate", [P, 3, CW], F32))
        gemm, silu, done = K.sem("f_sums"), K.sem("f_silu"), K.sem("f_done")
        block = ctx.enter_context(nc.Block())

        @block.sync
        def _(sp):
            ring_load(K, sp, "ffn", lambda i: (gemm, TC * (i + 1)))

        @block.tensor
        def _(pe):
            for s in range(FB):
                pe.wait_ge(*ring_landed(K, first + s))
                w = slab_of(K, first + s)
                for c in range(TC):
                    u = TC * s + c
                    if u >= 4:
                        pe.wait_ge(silu, u - 3)
                        pe.wait_ge(done, u - 3)
                    for h in range(2):
                        for k in range(KB):
                            mm = nc.tensor.matmul(ps[:, 2 * (u % 4) + h, 0:CW], w[:, k, P * h:P * h + P],
                                                  hT[:, k, CW * c:CW * c + CW], start=(k == 0), stop=(k == KB - 1))
                    mm.then_inc(gemm, 1)

        @block.scalar
        def _(act):
            for u in range(FB * TC):
                act.wait_ge(gemm, u + 1)
                if u >= 3:
                    act.wait_ge(done, u - 2)
                nc.scalar.activation(gate[:, u % 3, :], ps[:, 2 * (u % 4), 0:CW], ACT.Silu).then_inc(silu, 1)

        @block.vector
        def _(dve):
            for u in range(FB * TC):
                c = u % TC
                dve.wait_ge(silu, u + 1)
                nc.vector.tensor_tensor(act_T[:, u // TC, CW * c:CW * c + CW], ps[:, 2 * (u % 4) + 1, 0:CW],
                                        gate[:, u % 3, :], ALU.mult).then_inc(done, 1)


def ffn_out(K, act_T):
    nc, A, ps = K.nc, K.A, K.ps
    CS = 8
    SW = D // CS
    with ExitStack() as ctx:
        def sb(name, shape):
            return ctx.enter_context(nc.sbuf_tensor(name, shape, F32))
        own = sb("w2", [P, FB, SW])
        flat = K.ring[:].rearrange("p a b -> p (a b)")
        w = [flat[:, FB * SW * i:FB * SW * (i + 1)].rearrange("p (k n) -> p k n", n=SW) for i in range(2)] + [own[:]]
        x = sb("x2", [P, 9, D])
        gate = sb("gate2", [P, 2, D])
        fg = sb("final_g", [P, D])
        part = sb("part2", [P, 2, SW])
        sq = sb("sq2", [P, D])
        stat = sb("stat2", [P, 4, 9])
        w_in = [K.sem(f"w2_in{i}") for i in range(3)]
        x_in, gate_in, g_in = K.sem("x1_in"), K.sem("gate2_in"), K.sem("final_g_in")
        gemm, part_done, added = K.sem("sums2"), K.sem("part2_done"), K.sem("added2")
        squared, mean, root, inv, scaled, done = (K.sem(n) for n in ("squared2", "mean2", "root2", "inv2", "scaled2", "y_done"))
        out = K.store_sem("y_stored")
        block = ctx.enter_context(nc.Block())

        @block.sync
        def _(sp):
            for s in range(CS):
                if s >= 3:
                    sp.wait_ge(gemm, 9 * (s - 2))
                sp.dma_start(w[s % 3], A["w_ffn_out"][0, :, SW * s:SW * s + SW].rearrange("(k p) n -> p k n", p=P))\
                    .then_inc(w_in[s % 3], 16)
                if s == 1:
                    for b in range(2):
                        r = P if b == 0 else DEC
                        sp.dma_start(gate[0:r, b, :], A["s_gates"][2 + b, 0:r, :]).then_inc(gate_in, 16)
                    for t in range(9):
                        sp.dma_start(x[0:rows_of(t), t, :], A["s_x1"][P * t:P * t + rows_of(t), :]).then_inc(x_in, 16)
                    sp.dma_start(fg[:], A["final_g"].partition_broadcast(P)).then_inc(g_in, 16)
            for t in range(9):
                sp.wait_ge(done, t + 1)
                dst = A["y_prompt"][0, P * t:P * t + P, :] if t < TT else A["y_sample"][:, 0, :]
                sp.dma_start(dst, x[0:rows_of(t), t, :]).then_inc(out, 16)
            sp.wait_ge(out, 16 * 9)

        @block.tensor
        def _(pe):
            for s in range(CS):
                pe.wait_ge(w_in[s % 3], 16 * (s // 3 + 1))
                for t in range(9):
                    r, u = rows_of(t), 9 * s + t
                    if u >= 8:
                        pe.wait_ge(part_done, u - 7)
                    for k in range(FB):
                        mm = nc.tensor.matmul(ps[0:r, u % 8, 0:SW], act_T[:, k, P * t:P * t + r], w[s % 3][:, k, :],
                                              start=(k == 0), stop=(k == FB - 1))
                    mm.then_inc(gemm, 1)

        @block.scalar
        def _(act):
            for t in range(9):
                r = rows_of(t)
                act.wait_ge(added, 9 * (CS - 1) + t + 1)
                if t:
                    act.wait_ge(squared, t)
                nc.scalar.activation(sq[0:r, :], x[0:r, t, :], ACT.Square, accum_out=stat[0:r, 0, t:t + 1]).then_inc(squared, 1)
                act.wait_ge(mean, t + 1)
                nc.scalar.activation(stat[0:r, 2, t:t + 1], stat[0:r, 1, t:t + 1], ACT.Sqrt).then_inc(root, 1)

        @block.vector
        def _(dve):
            v = nc.vector
            dve.wait_ge(gate_in, 32)
            dve.wait_ge(x_in, 16 * 9)
            dve.wait_ge(g_in, 16)

            def final(t):
                r = rows_of(t)
                dve.wait_ge(squared, t + 1)
                v.tensor_scalar(stat[0:r, 1, t:t + 1], stat[0:r, 0, t:t + 1], 1.0 / D, EPS, ALU.mult, ALU.add).then_inc(mean, 1)
                dve.wait_ge(root, t + 1)
                v.reciprocal(stat[0:r, 3, t:t + 1], stat[0:r, 2, t:t + 1]).then_inc(inv, 1)
                dve.wait_ge(inv, t + 1)
                v.scalar_tensor_tensor(x[0:r, t, :], x[0:r, t, :], stat[0:r, 3, t:t + 1], fg[0:r, :],
                                       ALU.mult, ALU.mult).then_inc(done, 1)

            for s in range(CS):
                for t in range(9):
                    r, u = rows_of(t), 9 * s + t
                    cols = slice(SW * s, SW * s + SW)
                    dve.wait_ge(gemm, u + 1)
                    v.tensor_tensor(part[0:r, u % 2, :], ps[0:r, u % 8, 0:SW], gate[0:r, t // TT, cols], ALU.mult)\
                        .then_inc(part_done, 1)
                    dve.wait_ge(part_done, u + 1)
                    v.tensor_tensor(x[0:r, t, cols], x[0:r, t, cols], part[0:r, u % 2, :], ALU.add).then_inc(added, 1)
                    if s == CS - 1 and t:
                        final(t - 1)
            final(8)


def program(nc, A):
    K = Chip()
    K.nc, K.A = nc, A
    K.slabs, K.span = weight_slabs(A)
    A["s_sig"] = nc.dram_tensor("s_sig", (2 * KB, P, NT), F32, kind="Internal").ap()
    A["s_att"] = nc.dram_tensor("s_att", (KB, P, NT), F32, kind="Internal").ap()
    A["s_ssm"] = nc.dram_tensor("s_ssm", (2 * KB, P, SEQ), F32, kind="Internal").ap()
    A["s_x1"] = nc.dram_tensor("s_x1", (NT, D), F32, kind="Internal").ap()
    A["s_gates"] = nc.dram_tensor("s_gates", (4, P, D), F32, kind="Internal").ap()
    with ExitStack() as ctx:
        def sb(name, shape, into=None):
            return (into or ctx).enter_context(nc.sbuf_tensor(name, shape, F32))
        K.lent = []
        kept = lambda name: ctx.enter_context(nc.semaphore(name))

        def lend(name):
            K.lent.append(nc.alloc_semaphore(name=name))
            return K.lent[-1]

        def retire():
            with nc.Block() as block:
                @block.sync
                def _(sp):
                    for s in K.lent:
                        sp.sem_clear(s)
            for s in reversed(K.lent):
                nc.release_semaphore(s)
            K.lent = []

        K.sem = lend
        stores = {n: kept(n) for n in (
            "ki_stored", "k_stored", "v_stored", "tail_rows_stored", "states_stored", "final_stored",
            "old_conv_rows_stored", "y_stored", "gate_out0", "gate_out1", "conv_state_in", "states_in",
            "ssm_yT_stored0", "ssm_yT_stored1", "m_sig_in0", "m_sig_in1", "o_stored")}
        K.store_sem = stores.__getitem__
        K.ps = ctx.enter_context(nc.psum_tensor("ps", [P, 8, 512], F32))
        K.ring = sb("ring", [P, RING, SLAB])
        K.landed = [kept(f"slab_landed{i}") for i in range(RING)]
        K.ident_in, K.const_in = kept("ident_in"), kept("const_in")
        K.ident, K.le, K.gt, K.ones, K.diag_off = (sb(n, [P, P]) for n in ("ident", "le", "gt", "ones", "diag_off"))
        K.cos, K.sin = sb("cos", [P, TT + 1, HD]), sb("sin", [P, TT + 1, HD])
        K.heads_row, K.heads_col = sb("heads_row", [P, 3, HEADS]), sb("heads_col", [HEADS, 3])
        K.vecs = sb("vecs", [P, 152])
        K.modT = sb("modT", [P, 4, KB, 9])
        K.dt_raw, K.dtT_raw = sb("dt_raw", [P, TT, HEADS]), sb("dtT_raw", [HEADS, DEC])
        K.ysT = sb("ysT", [P, INNER // P, DEC])
        modulation(K)
        xp, xs = A["x_prompt"][0], A["x_sample"][:, 0]

        def x_tile(t):
            return xp[P * t:P * t + P, :] if t < TT else xs

        with ExitStack() as first:
            hT = sb("hT", [P, KB, NT], first)
            norm_stage(K, "n1", 0, hT, x_tile)
            with ExitStack() as att:
                T = Chip()
                T.qT = sb("qT", [P, KB, NT], att)
                T.v = sb("v", [P, TT + 1, KVH * HD], att)
                T.wi = sb("wi", [P, TT + 1, IH], att)
                T.q_s, T.k_s = sb("q_s", [DEC, D], att), sb("k_s", [DEC, KVH * HD], att)
                T.qi_s, T.ki_s = sb("qi_s", [DEC, IH * HD], att), sb("ki_s", [DEC, HD], att)
                T.dt_raw, T.dtT_raw = K.dt_raw, K.dtT_raw
                with ExitStack() as keys:
                    T.kT, T.kiT = sb("kT", [P, KVH, SEQ], keys), sb("kiT", [P, SEQ], keys)
                    T.qiT = sb("qiT", [P, 2, SEQ], keys)
                    T.bias = keys.enter_context(nc.sbuf_tensor("sel_bias", [P, BIAS_AT[TT]], BF16))
                    project(K, hT, T)
                    select(K, hT, T)
                    attend(K, T)
                attend_samples(K, T)
            retire()
            with ExitStack() as rec:
                S = Chip()
                S.dt, S.dta, S.ddt, S.e_acs, S.c_dec = (sb("s_" + n, [P, TT, HEADS], rec) for n in ("dt", "dta", "ddt", "e", "c"))
                S.hx = sb("s_hx", [P, INNER // P, 17], rec)
                S.ysT = K.ysT
                steps(K, S)
                ssm(K, hT, S)
            retire()
        with ExitStack() as mix:
            merged = sb("merged", [P, KB, NT], mix)
            merge(K, merged)
            project_out(K, merged, x_tile)
        with ExitStack() as mlp:
            act_T = sb("act_T", [P, FB, NT], mlp)
            with ExitStack() as second:
                hT = sb("hT2", [P, KB, NT], second)
                norm_stage(K, "n2", 1, hT, lambda t: A["s_x1"][P * t:P * t + rows_of(t), :])
                ffn_in(K, hT, act_T)
            ffn_out(K, act_T)


_INS = ["x_prompt", "x_sample", "cache_k", "cache_v", "cache_kidx", "state_conv", "state_ssm", "page_table",
        "c_prompt", "c_sample", "w_ada", "b_ada", "norm1_g", "w_in", "conv_w", "conv_b", "dt_bias", "a_log",
        "d_skip", "ssm_norm_g", "w_proj_ssm", "w_proj_attn", "w_out", "norm2_g", "w_ffn_in", "w_ffn_out", "final_g"]
_OUTS = [("y_prompt", (1, SEQ, D)), ("y_sample", (DEC, 1, D)),
         ("k_prompt", (1, 1, SEQ, KVH, HD)), ("v_prompt", (1, 1, SEQ, KVH, HD)), ("kidx_prompt", (1, 1, SEQ, HD)),
         ("conv_prompt", (1, 1, CONV - 1, XBC)), ("ssm_prompt", (1, 1, HEADS, HD, NST)),
         ("k_sample", (1, DEC, 1, KVH, HD)), ("v_sample", (1, DEC, 1, KVH, HD)), ("kidx_sample", (1, DEC, 1, HD)),
         ("conv_sample", (1, DEC, CONV - 1, XBC)), ("ssm_sample", (1, DEC, HEADS, HD, NST))]


def shape_constants():
    import numpy as np
    i = np.arange(P)
    f = np.float32
    half = HD // 2
    inv = f(10000.0) ** (-np.arange(half, dtype=f) / f(half))
    pos = np.concatenate([np.arange(SEQ), np.full(P, PAST)]).astype(f)
    ang = (pos[:, None] * inv[None, :]).astype(f)
    cos, sin = np.cos(ang).astype(f), np.sin(ang).astype(f)
    tiled = lambda a: np.ascontiguousarray(a.reshape(TT + 1, P, HD).transpose(1, 0, 2))
    return {
        "k_ident": np.eye(P, dtype=f),
        "k_le": (i[:, None] <= i[None, :]).astype(f),
        "k_gt": (i[:, None] > i[None, :]).astype(f),
        "k_ones": np.ones((P, P), f),
        "k_diag_off": np.where(i[None, :] <= i[:, None], f(0), f(OFF)).astype(f),
        "k_diag_far": np.where(i[None, :] <= i[:, None], f(0), f(FAR)).astype(f),
        "k_cos": tiled(np.concatenate([cos, cos], 1)),
        "k_sin": tiled(np.concatenate([-sin, sin], 1)),
        "k_head": (np.arange(HEADS)[:, None] == np.arange(INNER)[None, :] // HD).astype(f),
        "k_who": (np.arange(DEC)[:, None] == i[None, :] // AH).astype(f),
    }


def kernel(**inputs):
    import numpy as _np
    import concourse.bacc as _bacc
    from concourse import mybir as _mybir
    from concourse.bass_utils import run_bass_kernel_spmd as _run

    nc = _bacc.Bacc("TRN2", target_bir_lowering=False, num_devices=1)
    arrays, A = {}, {}
    given = {n: _np.ascontiguousarray(inputs[n]) for n in _INS}
    given.update(shape_constants())
    for name, a in given.items():
        arrays[f"in_{name}"] = a
        A[name] = nc.dram_tensor(f"in_{name}", a.shape, _mybir.dt.from_np(a.dtype), kind="ExternalInput").ap()
    for name, shape in _OUTS:
        A[name] = nc.dram_tensor(f"out_{name}", shape, F32, kind="ExternalOutput").ap()
    program(nc, A)
    r = _run(nc, [arrays], core_ids=[0])
    return tuple(r.results[0][f"out_{name}"] for name, _ in _OUTS)
```

```python
from contextlib import ExitStack

import concourse.bass as bass
from concourse import mybir

F32 = mybir.dt.float32
F32R = mybir.dt.float32r
I32 = mybir.dt.int32
BF16 = mybir.dt.bfloat16
ALU = mybir.AluOpType
ACT = mybir.ActivationFunctionType
AX = mybir.AxisListType

P = 128
D = 1024
SEQ, DEC = 1024, 8
NT = SEQ + DEC
TT = SEQ // P
KB = D // P
TC, CW = 3, NT // 3
EPS = 1e-6
INNER, HEADS, HD, GROUPS, NST, CONV = 2048, 32, 64, 4, 128, 4
GW = INNER // GROUPS
GH = HEADS // GROUPS
XBC = INNER + 2 * GROUPS * NST
AH, KVH = 16, 4
IH = 4
PAST, PAGE = 256, 128
NPAGE = PAST // PAGE
SKEYS = PAST + 1
TOPK = min(256, SEQ // 4)
STOPK = min(256, SKEYS // 4)
FFN = 2816
FB = FFN // P
C_Z, C_X, C_B, C_C, C_DT = 0, 2048, 4096, 4608, 5120
C_Q, C_K, C_V, C_QI, C_KI, C_WI, C_GS, C_GA = 5152, 6176, 6432, 6688, 6944, 7008, 7012, 8036
IDX_SCALE = IH ** -0.5 * HD ** -0.5
ATT_SCALE = HD ** -0.5
FAR = -3.0e38
OFF = -1.0e30
SLAB = 2048
RING = 4


def rows_of(t):
    return P if t < TT else DEC


class Chip:
    pass


def weight_slabs(A):
    slabs, span = [], {}

    def cols(w, c0, n):
        return w[0, :, c0:c0 + n].rearrange("(k p) n -> p k n", p=P)

    def k8(at, n=256):
        return lambda s: s.rearrange("p (k n) -> p k n", k=KB)[:, :, at:at + n]

    def add(name, *parts):
        span.setdefault(name, [len(slabs), 0])
        slabs.append(list(parts))
        span[name][1] = len(slabs)

    for i in range(24):
        add("ada", (k8(0), cols(A["w_ada"], 256 * i, 256)))
    add("qkv", (k8(0, 32), cols(A["w_in"], C_DT, 32)), (k8(32, 68), cols(A["w_in"], C_KI, 68)))
    add("qkv", (k8(0), cols(A["w_in"], C_QI, 256)))
    add("qkv", (k8(0), cols(A["w_in"], C_K, 256)))
    add("qkv", (k8(0), cols(A["w_in"], C_V, 256)))
    for i in range(4):
        add("qkv", (k8(0), cols(A["w_in"], C_Q + 256 * i, 256)))
    for c in (C_GS, C_GA):
        for i in range(4):
            add("gates", (k8(0), cols(A["w_in"], c + 256 * i, 256)))
    for g in range(GROUPS):
        n = f"g{g}"
        for i in range(2):
            add(n, (k8(0), cols(A["w_in"], C_X + GW * g + 256 * i, 256)))
        add(n, (k8(0, P), cols(A["w_in"], C_B + P * g, P)), (k8(P, P), cols(A["w_in"], C_C + P * g, P)))
        for i in range(2):
            add(n, (k8(0), cols(A["w_in"], C_Z + GW * g + 256 * i, 256)))
    return slabs, span


def ring_landed(K, n):
    return K.landed[n % RING], 16 * sum(len(K.slabs[m]) for m in range(n % RING, n + 1, RING))


def ring_load(K, eng, stage, used):
    first, last = K.span[stage]
    for n in range(first + RING, min(last + RING, len(K.slabs))):
        eng.wait_ge(*used(n - RING - first))
        for place, src in K.slabs[n]:
            eng.dma_start(place(K.ring[:, n % RING, :]), src).then_inc(K.landed[n % RING], 16)


def slab_of(K, n, k=KB):
    return K.ring[:, n % RING, :].rearrange("p (k n) -> p k n", k=k)


def modulation(K):
    nc, A, ps = K.nc, K.A, K.ps
    first, last = K.span["ada"]
    with ExitStack() as ctx:
        def sb(name, shape):
            return ctx.enter_context(nc.sbuf_tensor(name, shape, F32))
        c_rows = sb("c_rows", [9, D])
        c_silu = sb("c_silu", [9, D])
        cT = sb("cT", [P, KB, 9])
        mod = sb("mod", [9, 6 * D])
        vec_rows = sb("vec_rows", [P, 2, P])
        gate_sb = sb("gate_sb", [P, 4, D])
        c_in, vec_in, mod_b = K.sem("c_in"), K.sem("vec_in"), K.sem("mod_bias_in")
        silu_done, cT_ps, cT_done = K.sem("c_silu_done"), K.sem("cT_in_psum"), K.sem("cT_done")
        vec_ps = K.sem("vec_in_psum")
        prod, summed = K.sem("mod_product"), K.sem("mod_summed")
        modT_ps, modT_done = K.sem("modT_in_psum"), K.sem("modT_done")
        step = K.sem("mod_vector_step")
        gate_ps, gate_done, gate_out = K.sem("gate_in_psum"), K.sem("gate_done"), K.sem("gate_stored")
        block = ctx.enter_context(nc.Block())

        @block.sync
        def _(sp):
            sp.dma_start(c_rows[0:1, :], A["c_prompt"]).then_inc(c_in, 16)
            sp.dma_start(c_rows[1:9, :], A["c_sample"]).then_inc(c_in, 16)
            sp.dma_start(K.ident[:], A["k_ident"]).then_inc(K.ident_in, 16)
            for n in range(RING):
                for place, src in K.slabs[n]:
                    sp.dma_start(place(K.ring[:, n, :]), src).then_inc(K.landed[n], 16)
            sp.dma_start(mod[:, :], A["b_ada"][0].partition_broadcast(9)).then_inc(mod_b, 16)
            rows = ((0, 0, A["conv_w"][0].rearrange("i (b p) -> (i b) p", p=P), 96),
                    (0, 96, A["conv_b"][0].rearrange("(b p) -> b p", p=P), 24),
                    (1, 0, A["norm1_g"][0].rearrange("(b p) -> b p", p=P), 8),
                    (1, 8, A["norm2_g"][0].rearrange("(b p) -> b p", p=P), 8),
                    (1, 16, A["ssm_norm_g"][0].rearrange("(b p) -> b p", p=P), 16))
            for part, r0, src, n in rows:
                sp.dma_start(vec_rows[r0:r0 + n, part, :], src).then_inc(vec_in, 16)
            for dst, name in ((K.le, "k_le"), (K.gt, "k_gt"), (K.ones, "k_ones"), (K.diag_off, "k_diag_off"),
                              (K.cos, "k_cos"), (K.sin, "k_sin")):
                sp.dma_start(dst[:], A[name]).then_inc(K.const_in, 16)
            for i, name in enumerate(("dt_bias", "a_log", "d_skip")):
                sp.dma_start(K.heads_row[:, i, :], A[name][0].partition_broadcast(P)).then_inc(K.const_in, 16)
                sp.dma_start(K.heads_col[:, i:i + 1], A[name][0].unsqueeze(1)).then_inc(K.const_in, 16)
            ring_load(K, sp, "ada", lambda i: (prod, i + 1))
            sp.wait_ge(gate_done, 4)
            for b in range(4):
                r = P if b % 2 == 0 else DEC
                sp.dma_start(A["s_gates"][b, 0:r, :], gate_sb[0:r, b, :]).then_inc(gate_out, 16)
            sp.wait_ge(gate_out, 64)

        @block.scalar
        def _(act):
            act.wait_ge(c_in, 32)
            nc.scalar.activation(c_silu[:], c_rows[:], ACT.Silu).then_inc(silu_done, 1)
            for b in range(4):
                act.wait_ge(gate_ps, b + 1)
                for h in range(2):
                    cp = nc.scalar.copy(gate_sb[0:P if b % 2 == 0 else DEC, b, 512 * h:512 * h + 512],
                                        ps[0:P if b % 2 == 0 else DEC, 2 + h, :])
                cp.then_inc(gate_done, 1)

        @block.tensor
        def _(pe):
            pe.wait_ge(K.ident_in, 16)
            pe.wait_ge(silu_done, 1)
            for k in range(KB):
                mm = nc.tensor.transpose(ps[:, 7, 9 * k:9 * k + 9], c_silu[:, P * k:P * k + P], K.ident[0:9, 0:9])
            mm.then_inc(cT_ps, 1)
            pe.wait_ge(cT_done, 1)
            for n in range(first, last):
                i = n - first
                pe.wait_ge(*ring_landed(K, n))
                if i >= 2:
                    pe.wait_ge(summed, i - 1)
                for k in range(KB):
                    mm = nc.tensor.matmul(ps[0:9, i % 2, 0:256], cT[:, k, :], slab_of(K, n)[:, k, :],
                                          start=(k == 0), stop=(k == KB - 1))
                mm.then_inc(prod, 1)
            pe.wait_ge(vec_in, 80)
            nc.tensor.transpose(ps[:, 4, 0:120], vec_rows[0:120, 0, :], K.ident[0:120, 0:120])
            nc.tensor.transpose(ps[:, 4, 120:152], vec_rows[0:32, 1, :], K.ident[0:32, 0:32]).then_inc(vec_ps, 1)
            pe.wait_ge(summed, last - first)
            for a, part in enumerate((0, 1, 3, 4)):
                for k in range(KB):
                    mm = nc.tensor.transpose(ps[:, 5, (8 * a + k) * 9:(8 * a + k) * 9 + 9],
                                             mod[:, D * part + P * k:D * part + P * k + P], K.ident[0:9, 0:9])
            mm.then_inc(modT_ps, 1)
            for b in range(4):
                if b:
                    pe.wait_ge(gate_done, b)
                base = D * (2 if b < 2 else 5)
                who = K.ident[0:9, 0:1].to_broadcast([9, P]) if b % 2 == 0 else K.ident[0:9, 1:9]
                for h in range(2):
                    mm = nc.tensor.matmul(ps[0:P if b % 2 == 0 else DEC, 2 + h, :], who,
                                          mod[:, base + 512 * h:base + 512 * h + 512], start=True, stop=True)
                mm.then_inc(gate_ps, 1)

        @block.vector
        def _(dve):
            dve.wait_ge(cT_ps, 1)
            nc.vector.tensor_copy(cT[:].rearrange("p k s -> p (k s)"), ps[:, 7, 0:72]).then_inc(cT_done, 1)
            dve.wait_ge(mod_b, 16)
            for i in range(last - first):
                dve.wait_ge(prod, i + 1)
                nc.vector.tensor_tensor(mod[:, 256 * i:256 * i + 256], ps[0:9, i % 2, 0:256],
                                        mod[:, 256 * i:256 * i + 256], ALU.add).then_inc(summed, 1)
            dve.wait_ge(vec_ps, 1)
            nc.vector.tensor_copy(K.vecs[:], ps[:, 4, 0:152]).then_inc(step, 1)
            dve.wait_ge(modT_ps, 1)
            nc.vector.tensor_copy(K.modT[:].rearrange("p a k s -> p (a k s)"), ps[:, 5, 0:288]).then_inc(step, 1)
            dve.wait_ge(step, 2)
            for a in range(2):
                sc = K.modT[:, 2 * a + 1, :, :]
                nc.vector.tensor_scalar(sc, sc, 1.0, None, ALU.add).then_inc(step, 1)
                dve.wait_ge(step, 3 + 2 * a)
                g = K.vecs[:, 120 + 8 * a:128 + 8 * a].unsqueeze(2).to_broadcast([P, KB, 9])
                nc.vector.tensor_tensor(sc, sc, g, ALU.mult).then_inc(step, 1)
                dve.wait_ge(step, 4 + 2 * a)


def norm_stage(K, tag, which, hT, source):
    nc, ps = K.nc, K.ps
    with ExitStack() as ctx:
        def sb(name, shape):
            return ctx.enter_context(nc.sbuf_tensor(tag + name, shape, F32))
        x = sb("x", [P, 3, D])
        xn = sb("xn", [P, 2, D])
        sq = sb("sq", [P, D])
        stat = sb("stat", [P, 4, 9])
        x_in = [K.sem(f"{tag}x_in{i}") for i in range(3)]
        squared, mean, root, inv = K.sem(tag + "squared"), K.sem(tag + "mean"), K.sem(tag + "root"), K.sem(tag + "inv")
        scaled, turned, moved = K.sem(tag + "scaled"), K.sem(tag + "turned"), K.sem(tag + "moved")
        extra = K.sem(tag + "sample_scaled")
        block = ctx.enter_context(nc.Block())

        @block.sync
        def _(sp):
            for t in range(9):
                if t >= 3:
                    sp.wait_ge(scaled, t - 2)
                    sp.wait_ge(squared, t - 2)
                sp.dma_start(x[0:rows_of(t), t % 3, :], source(t)).then_inc(x_in[t % 3], 16)

        @block.scalar
        def _(act):
            def square(t):
                r = rows_of(t)
                act.wait_ge(x_in[t % 3], 16 * (t // 3 + 1))
                if t:
                    act.wait_ge(squared, t)
                nc.scalar.activation(sq[0:r, :], x[0:r, t % 3, :], ACT.Square,
                                     accum_out=stat[0:r, 0, t:t + 1]).then_inc(squared, 1)
                act.wait_ge(mean, t + 1)
                nc.scalar.activation(stat[0:r, 2, t:t + 1], stat[0:r, 1, t:t + 1], ACT.Sqrt).then_inc(root, 1)

            def move(t):
                for h in range(2):
                    act.wait_ge(turned, 2 * t + h + 1)
                    for j in range(4):
                        k = 4 * h + j
                        mv = nc.scalar.activation(hT[:, k, P * t:P * t + P], ps[:, 2 * (t % 2) + h, P * j:P * j + P],
                                                  ACT.Identity, bias=K.modT[:, 2 * which, k, 0:1],
                                                  scale=K.modT[:, 2 * which + 1, k, 0:1])
                    mv.then_inc(moved, 1)

            square(0)
            for t in range(TT):
                square(t + 1)
                move(t)

        @block.vector
        def _(dve):
            for t in range(9):
                r = rows_of(t)
                dve.wait_ge(squared, t + 1)
                nc.vector.tensor_scalar(stat[0:r, 1, t:t + 1], stat[0:r, 0, t:t + 1], 1.0 / D, EPS,
                                        ALU.mult, ALU.add).then_inc(mean, 1)
                dve.wait_ge(root, t + 1)
                nc.vector.reciprocal(stat[0:r, 3, t:t + 1], stat[0:r, 2, t:t + 1]).then_inc(inv, 1)
                dve.wait_ge(inv, t + 1)
                if t >= 2:
                    dve.wait_ge(turned, 2 * (t - 1))
                nc.vector.tensor_scalar(xn[0:r, t % 2, :], x[0:r, t % 3, :], stat[0:r, 3, t:t + 1], None,
                                        ALU.mult).then_inc(scaled, 1)
            dve.wait_ge(turned, 2 * TT + 1)
            hs = hT[:, :, SEQ:NT]
            nc.vector.tensor_tensor(hs, ps[:, 4, 0:64].rearrange("p (k s) -> p k s", k=KB),
                                    K.modT[:, 2 * which + 1, :, 1:9], ALU.mult).then_inc(extra, 1)
            dve.wait_ge(extra, 1)
            nc.vector.tensor_tensor(hs, hs, K.modT[:, 2 * which, :, 1:9], ALU.add).then_inc(extra, 1)

        @block.tensor
        def _(pe):
            for t in range(9):
                pe.wait_ge(scaled, t + 1)
                if t == TT:
                    for k in range(KB):
                        mm = nc.tensor.transpose(ps[:, 4, 8 * k:8 * k + 8], xn[0:DEC, t % 2, P * k:P * k + P],
                                                 K.ident[0:DEC, 0:DEC])
                    mm.then_inc(turned, 1)
                    break
                for h in range(2):
                    if t >= 2:
                        pe.wait_ge(moved, 2 * (t - 2) + h + 1)
                    for j in range(4):
                        k = 4 * h + j
                        mm = nc.tensor.transpose(ps[:, 2 * (t % 2) + h, P * j:P * j + P],
                                                 xn[:, t % 2, P * k:P * k + P], K.ident[:])
                    mm.then_inc(turned, 1)


def project(K, hT, T):
    nc, A, ps = K.nc, K.A, K.ps
    first, last = K.span["qkv"]
    n_slabs = last - first
    SMALL, QI, KK, V, Q0 = 0, 1, 2, 3, 4
    with ExitStack() as ctx:
        def sb(name, shape):
            return ctx.enter_context(nc.sbuf_tensor(name, shape, F32))
        stg = sb("stg", [P, 2, 9, 256])
        rot = sb("rot", [P, 2, 9, 256])
        tmp = sb("tmp", [P, 2, 256])
        gemm, out_of_ps = K.sem("qkv_in_psum"), K.sem("qkv_rows")
        t_a, t_b, rotated = K.sem("rope_cos_part"), K.sem("rope_sin_part"), K.sem("roped_tiles")
        dtT_ps, kept = K.sem("dtT_in_psum"), K.sem("sample_rows_kept")
        turned, moved = K.sem("qk_turned"), K.sem("qk_moved")
        ki_stored, k_stored, v_stored = (K.store_sem(n) for n in ("ki_stored", "k_stored", "v_stored"))
        block = ctx.enter_context(nc.Block())

        rope_cols = [(32, 1), (0, 4), (0, 4), None] + [(0, 4)] * 4
        roped_before = [9 * sum(1 for c in rope_cols[:s] if c) for s in range(n_slabs + 1)]

        def turns(s):
            r, lo, hi = rot[:, s % 2], slice(0, HD), slice(HD, P)
            if s == SMALL:
                return [(lambda t: r[:, t, 32:96], HD, [(lo, T.kiT[lo, :]), (lo, T.kiT[hi, :])])]
            if s == KK:
                return [(lambda t, j=j: r[:, t, P * j:P * j + P], P,
                         [(lo, T.kT[lo, 2 * j, :]), (lo, T.kT[hi, 2 * j, :]),
                          (hi, T.kT[lo, 2 * j + 1, :]), (hi, T.kT[hi, 2 * j + 1, :])]) for j in range(2)]
            if s == V:
                return []
            full = slice(0, P)
            return [(lambda t, j=j: r[:, t, P * j:P * j + P], P,
                     [(full, T.qiT[:, j, :] if s == QI else T.qT[:, 2 * (s - Q0) + j, 0:SEQ])]) for j in range(2)]

        units = [(s, src, w, dst, h) for s in range(n_slabs) for src, w, dst in turns(s) for h in range(2)]
        units_before = [sum(1 for u in units if u[0] < s) for s in range(n_slabs + 1)]

        @block.sync
        def _(sp):
            ring_load(K, sp, "qkv", lambda i: (gemm, 9 * i + 9) if i else (dtT_ps, 1))

        @block.gpsimd
        def _(pool):
            pool.wait_ge(rotated, roped_before[SMALL + 1])
            r = rot[:, SMALL % 2]
            pool.dma_start(A["kidx_prompt"][0, 0].rearrange("(t p) d -> p t d", p=P), r[:, 0:TT, 32:96]).then_inc(ki_stored, 16)
            pool.dma_start(A["kidx_sample"][0, :, 0], r[0:DEC, TT, 32:96]).then_inc(ki_stored, 16)
            pool.wait_ge(rotated, roped_before[KK + 1])
            r = rot[:, KK % 2]
            pool.dma_start(A["k_prompt"][0, 0].rearrange("(t p) g d -> p t (g d)", p=P), r[:, 0:TT, :]).then_inc(k_stored, 16)
            pool.dma_start(A["k_sample"][0, :, 0].rearrange("b g d -> b (g d)"), r[0:DEC, TT, :]).then_inc(k_stored, 16)
            pool.wait_ge(out_of_ps, 9 * (V + 1))
            pool.dma_start(A["v_prompt"][0, 0].rearrange("(t p) g d -> p t (g d)", p=P), T.v[:, 0:TT, :]).then_inc(v_stored, 16)
            pool.dma_start(A["v_sample"][0, :, 0].rearrange("b g d -> b (g d)"), T.v[0:DEC, TT, :]).then_inc(v_stored, 16)
            for done in (ki_stored, k_stored, v_stored):
                pool.wait_ge(done, 32)

        @block.scalar
        def _(act):
            def rows(s):
                for t in range(9):
                    r, n = rows_of(t), 100 if s == SMALL else 256
                    act.wait_ge(gemm, 9 * s + t + 1)
                    if s >= 2 and t == 0:
                        act.wait_ge(kept, roped_before[s - 1] // 9)
                    dst = T.v[0:r, t, :] if s == V else stg[0:r, s % 2, t, 0:n]
                    nc.scalar.copy(dst, ps[0:r, (9 * s + t) % 4, 0:n]).then_inc(out_of_ps, 1)

            def turn_moves(s):
                for u in range(units_before[s], units_before[s + 1]):
                    _, _, _, places, h = units[u]
                    act.wait_ge(turned, u + 1)
                    for rows, dst in places:
                        mv = nc.scalar.copy(dst[:, 512 * h:512 * h + 512], ps[rows, 4 + u % 3, :])
                    mv.then_inc(moved, 1)

            rows(0)
            for s in range(1, n_slabs):
                rows(s)
                turn_moves(s - 1)
            turn_moves(n_slabs - 1)

        @block.vector
        def _(dve):
            m = 0
            dve.wait_ge(K.const_in, 16 * 12)
            for s in range(n_slabs):
                if rope_cols[s] is None:
                    continue
                c0, nh = rope_cols[s]
                w = HD * nh
                if s == QI + 1:
                    dve.wait_ge(ki_stored, 32)
                if s == Q0:
                    dve.wait_ge(k_stored, 32)
                if s >= 2:
                    dve.wait_ge(turned, units_before[s - 1])
                for t in range(9):
                    r = rows_of(t)
                    dve.wait_ge(out_of_ps, 9 * s + t + 1)
                    x = stg[0:r, s % 2, t, c0:c0 + w].rearrange("p (h d) -> p h d", d=HD)
                    o = rot[0:r, s % 2, t, c0:c0 + w].rearrange("p (h d) -> p h d", d=HD)
                    b = tmp[0:r, m % 2, 0:w].rearrange("p (h d) -> p h d", d=HD)
                    hh = HD // 2
                    cos = K.cos[0:r, t, :].unsqueeze(1).to_broadcast([r, nh, HD])
                    sin = K.sin[0:r, t, :].unsqueeze(1)
                    nc.vector.tensor_tensor(b[:, :, 0:hh], x[:, :, hh:HD], sin[:, :, 0:hh].to_broadcast([r, nh, hh]), ALU.mult)
                    nc.vector.tensor_tensor(b[:, :, hh:HD], x[:, :, 0:hh], sin[:, :, hh:HD].to_broadcast([r, nh, hh]),
                                            ALU.mult).then_inc(t_b, 1)
                    nc.vector.tensor_tensor(o, x, cos, ALU.mult).then_inc(t_a, 1)
                    m += 1
                    dve.wait_ge(t_b, m)
                    dve.wait_ge(t_a, m)
                    nc.vector.tensor_tensor(o, o, b, ALU.add).then_inc(rotated, 1)
                dve.wait_ge(rotated, m)
                if s == SMALL:
                    nc.vector.tensor_copy(T.dt_raw[:], stg[:, 0, 0:TT, 0:32])
                    nc.vector.tensor_scalar(T.wi[:, 0:TT, :], stg[:, 0, 0:TT, 96:100], IDX_SCALE, None, ALU.mult)
                    nc.vector.tensor_scalar(T.wi[0:DEC, TT, :], stg[0:DEC, 0, TT, 96:100], IDX_SCALE, None, ALU.mult)
                    nc.vector.tensor_copy(T.ki_s[:], rot[0:DEC, 0, TT, 32:96]).then_inc(kept, 1)
                elif s == QI:
                    nc.vector.tensor_copy(T.qi_s[:], rot[0:DEC, 1, TT, :]).then_inc(kept, 1)
                elif s == KK:
                    nc.vector.tensor_copy(T.k_s[:], rot[0:DEC, 0, TT, :]).then_inc(kept, 1)
                else:
                    nc.vector.tensor_copy(T.q_s[:, 256 * (s - Q0):256 * (s - Q0) + 256],
                                          rot[0:DEC, s % 2, TT, :]).then_inc(kept, 1)
            dve.wait_ge(dtT_ps, 1)
            nc.vector.tensor_copy(T.dtT_raw[:], ps[0:32, 7, 0:DEC])

        @block.tensor
        def _(pe):
            def gemm_slab(s):
                n = first + s
                w = slab_of(K, n)
                width = 100 if s == SMALL else 256
                pe.wait_ge(*ring_landed(K, n))
                for t in range(9):
                    r = rows_of(t)
                    if 9 * s + t >= 4:
                        pe.wait_ge(out_of_ps, 9 * s + t - 3)
                    for k in range(KB):
                        mm = nc.tensor.matmul(ps[0:r, (9 * s + t) % 4, 0:width], hT[:, k, P * t:P * t + r], w[:, k, 0:width],
                                              start=(k == 0), stop=(k == KB - 1))
                    mm.then_inc(gemm, 1)

            def turn_slab(s):
                for u in range(units_before[s], units_before[s + 1]):
                    _, src, w, _, h = units[u]
                    if u >= 3:
                        pe.wait_ge(moved, u - 2)
                    for j in range(4):
                        t = 4 * h + j
                        pe.wait_ge(rotated, roped_before[s] + t + 1)
                        mm = nc.tensor.transpose(ps[0:w, 4 + u % 3, P * j:P * j + P], src(t), K.ident[:])
                    mm.then_inc(turned, 1)

            gemm_slab(0)
            w = slab_of(K, first)
            for k in range(KB):
                mm = nc.tensor.matmul(ps[0:HEADS, 7, 0:DEC], w[:, k, 0:HEADS], hT[:, k, SEQ:NT],
                                      start=(k == 0), stop=(k == KB - 1))
            mm.then_inc(dtT_ps, 1)
            for s in range(1, n_slabs):
                gemm_slab(s)
                turn_slab(s - 1)
            turn_slab(n_slabs - 1)


BIAS_AT = [P * i * (i + 1) // 2 for i in range(TT + 1)]


def select(K, hT, T):
    nc, A, ps = K.nc, K.A, K.ps
    first, last = K.span["gates"]
    with ExitStack() as ctx:
        def sb(name, shape):
            return ctx.enter_context(nc.sbuf_tensor(name, shape, F32))
        relu = sb("relu", [P, IH, SEQ])
        score, work, eq, cum = (sb(n, [P, SEQ]) for n in ("score", "work", "eq", "cum"))
        top8, count = sb("top8", [P, 2, 8]), sb("count", [P, 2])
        sig = sb("sig", [P, 2, NT])
        gemm, sig_done, sig_out = K.sem("gate_sums"), K.sem("gate_sigmoids"), [K.store_sem(f"gate_out{i}") for i in range(2)]
        idx_ps, relu_done, relu_used = K.sem("index_in_psum"), K.sem("index_relus"), K.sem("index_relus_used")
        step = K.sem("select_step")
        block = ctx.enter_context(nc.Block())

        groups = [(n, fb, c) for n in range(last - first) for fb in range(2) for c in range(TC)]
        units = [(i, h) for i in range(2, TT) for h in range(IH)]
        order, g = [], 0
        for i in range(2, TT):
            order += [("index", IH * (i - 2) + h) for h in range(IH)]
            take = len(groups) - g if i == TT - 1 else 8
            order += [("gate", g + j) for j in range(take)]
            g += take

        @block.sync
        def _(sp):
            ring_load(K, sp, "gates", lambda i: (gemm, 2 * TC * (i + 1)))

        @block.gpsimd
        def _(pool):
            for b in range(2 * KB):
                pool.wait_ge(sig_done, TC * (b + 1))
                pool.dma_start(A["s_sig"][b], sig[:, b % 2, :]).then_inc(sig_out[b % 2], 16)
            pool.wait_ge(sig_out[0], 16 * KB)
            pool.wait_ge(sig_out[1], 16 * KB)

        @block.tensor
        def _(pe):
            for kind, u in order:
                if kind == "index":
                    i, h = units[u]
                    if u >= 2:
                        pe.wait_ge(relu_done, u - 1)
                    rows = slice(HD * (h % 2), HD * (h % 2) + HD)
                    for c0 in range(0, P * (i + 1), 512):
                        n = min(512, P * (i + 1) - c0)
                        mm = nc.tensor.matmul(ps[:, 4 + 2 * (u % 2) + c0 // 512, 0:n],
                                              T.qiT[rows, h // 2, P * i:P * i + P], T.kiT[rows, c0:c0 + n],
                                              start=True, stop=True)
                    mm.then_inc(idx_ps, 1)
                else:
                    n, fb, c = groups[u]
                    if fb == 0 and c == 0:
                        pe.wait_ge(*ring_landed(K, first + n))
                    if u >= 4:
                        pe.wait_ge(sig_done, u - 3)
                    w = slab_of(K, first + n)
                    for k in range(KB):
                        mm = nc.tensor.matmul(ps[:, u % 4, 0:CW], w[:, k, P * fb:P * fb + P],
                                              hT[:, k, CW * c:CW * c + CW], start=(k == 0), stop=(k == KB - 1))
                    mm.then_inc(gemm, 1)

        @block.scalar
        def _(act):
            for kind, u in order:
                if kind == "index":
                    i, h = units[u]
                    L = P * (i + 1)
                    act.wait_ge(idx_ps, u + 1)
                    if u >= IH:
                        act.wait_ge(relu_used, u - IH + 1)
                    nc.scalar.activation(relu[:, h, 0:L], ps[:, 4 + 2 * (u % 2):6 + 2 * (u % 2), :]
                                         .rearrange("p a n -> p (a n)")[:, 0:L], ACT.Relu).then_inc(relu_done, 1)
                else:
                    n, fb, c = groups[u]
                    b = 2 * n + fb
                    act.wait_ge(gemm, u + 1)
                    if c == 0 and b >= 2:
                        act.wait_ge(sig_out[b % 2], 16 * (b // 2))
                    nc.scalar.activation(sig[:, b % 2, CW * c:CW * c + CW], ps[:, u % 4, 0:CW],
                                         ACT.Sigmoid).then_inc(sig_done, 1)

        @block.vector
        def _(dve):
            n = [0]

            def link(ins):
                n[0] += 1
                ins.then_inc(step, 1)
                dve.wait_ge(step, n[0])

            v = nc.vector
            link(v.tensor_copy(T.bias[:, 0:P], K.diag_off[:]))
            link(v.memset(T.bias[:, P:2 * P], 0.0))
            link(v.tensor_copy(T.bias[:, 2 * P:3 * P], K.diag_off[:]))
            for i in range(2, TT):
                L = P * (i + 1)
                sc, wk, e, cu = score[:, 0:L], work[:, 0:L], eq[:, 0:L], cum[:, 0:L]
                for h in range(IH):
                    dve.wait_ge(relu_done, IH * (i - 2) + h + 1)
                    w = T.wi[:, i, h:h + 1]
                    dst = sc if h % 2 else cu
                    src = cu if h % 2 else sc
                    if h == 0:
                        v.tensor_scalar(dst, relu[:, h, 0:L], w, None, ALU.mult).then_inc(relu_used, 1)
                    else:
                        v.scalar_tensor_tensor(dst, relu[:, h, 0:L], w, src, ALU.mult, ALU.add).then_inc(relu_used, 1)
                    dve.wait_ge(relu_used, IH * (i - 2) + h + 1)
                link(v.tensor_tensor(sc[:, L - P:L], sc[:, L - P:L], K.diag_off[:], ALU.add))
                cur = sc
                for r in range(TOPK // 8):
                    m8 = top8[:, r % 2, :]
                    link(v.max(m8, cur))
                    if r < TOPK // 8 - 1:
                        link(v.match_replace(wk, m8, cur, FAR))
                        cur = wk
                thr = m8[:, 7:8]
                link(v.tensor_scalar(wk, sc, thr, None, ALU.is_gt, ALU.add, accum_out=count[:, 0:1]))
                link(v.tensor_scalar(count[:, 1:2], count[:, 0:1], -1.0, float(TOPK), ALU.mult, ALU.add))
                link(v.tensor_scalar(e, sc, thr, None, ALU.is_equal))
                link(v.tensor_tensor_scan(cu, K.ones[:, 0:1].to_broadcast([P, L]), e, 0.0, ALU.mult, ALU.add))
                link(v.scalar_tensor_tensor(cu, cu, count[:, 1:2], e, ALU.is_le, ALU.mult))
                link(v.scalar_tensor_tensor(wk, wk, -1.0, cu, ALU.add, ALU.add))
                link(v.tensor_scalar(T.bias[:, BIAS_AT[i]:BIAS_AT[i] + L], wk, -OFF, None, ALU.mult))


def attend(K, T):
    nc, ps = K.nc, K.ps
    with ExitStack() as ctx:
        def sb(name, shape):
            return ctx.enter_context(nc.sbuf_tensor(name, shape, F32))
        prob = sb("prob", [P, 2, SEQ])
        probT = sb("probT", [P, 2, SEQ])
        y = sb("y", [P, 2, D])
        top, nbias, total, inv = (sb(n, [P, 2]) for n in ("top", "nbias", "total", "inv"))
        qk, logits, nb = K.sem("qk_in_psum"), K.sem("logits_done"), K.sem("neg_max_done")
        probs, t_ps, t_moved = K.sem("probs_done"), K.sem("probT_in_psum"), K.sem("probT_done")
        o_ps, inv_done, o_done = K.sem("pv_in_psum"), K.sem("inv_done"), K.sem("y_head_done")
        y_ps, y_moved = K.sem("yT_in_psum"), K.sem("yT_done")
        block = ctx.enter_context(nc.Block())
        N = TT * AH

        def tile(n):
            return n // AH

        def turn_groups(n):
            return sum(1 if i < 4 else 2 for i in range(tile(n))) * AH + (n % AH) * (1 if tile(n) < 4 else 2)

        events, seen = [], {}
        for n in range(N + 1):
            if n < N:
                for q in range(turn_groups(n), turn_groups(n + 1) if n + 1 < N else turn_groups(n) + 2):
                    events.append(("prob", q, n))
            if n % AH == 2 and n > AH or n == N:
                i = (n - 1) // AH if n == N else tile(n) - 1
                events += [("y", 2 * i, i), ("y", 2 * i + 1, i)]
        for e, (kind, q, _) in enumerate(events):
            seen[kind, q] = e

        def bank_free(eng, e):
            if e >= 2:
                kind, q, _ = events[e - 2]
                eng.wait_ge(t_moved if kind == "prob" else y_moved, q + 1)

        @block.tensor
        def _(pe):
            def qk_unit(n):
                i, h = tile(n), n % AH
                rows = slice(HD * (h % 2), HD * (h % 2) + HD)
                if n >= 2:
                    pe.wait_ge(logits, n - 1)
                for c0 in range(0, P * (i + 1), 512):
                    w = min(512, P * (i + 1) - c0)
                    mm = nc.tensor.matmul(ps[:, 2 * (n % 2) + c0 // 512, 0:w], T.qT[rows, h // 2, P * i:P * i + P],
                                          T.kT[rows, h // (AH // KVH), c0:c0 + w], start=True, stop=True)
                mm.then_inc(qk, 1)

            def turn(n):
                i = tile(n)
                pe.wait_ge(probs, n + 1)
                for q in range(turn_groups(n), turn_groups(n) + (1 if i < 4 else 2)):
                    e = seen["prob", q]
                    bank_free(pe, e)
                    b0 = 4 * (q - turn_groups(n))
                    for b in range(b0, min(b0 + 4, i + 1)):
                        mm = nc.tensor.transpose(ps[:, 4 + e % 2, P * (b - b0):P * (b - b0) + P],
                                                 prob[:, n % 2, P * b:P * b + P], K.ident[:])
                    mm.then_inc(t_ps, 1)

            def pv(n):
                i, h = tile(n), n % AH
                g = h // (AH // KVH)
                pe.wait_ge(t_moved, turn_groups(n) + (1 if i < 4 else 2))
                if n >= 2:
                    pe.wait_ge(o_done, n - 1)
                for b in range(i + 1):
                    mm = nc.tensor.matmul(ps[:, 6 + n % 2, 0:HD], probT[:, n % 2, P * b:P * b + P],
                                          T.v[:, b, HD * g:HD * g + HD], start=(b == 0), stop=(b == i))
                mm.then_inc(o_ps, 1)

            def turn_y(i):
                pe.wait_ge(o_done, AH * (i + 1))
                for half in range(2):
                    e = seen["y", 2 * i + half]
                    bank_free(pe, e)
                    for j in range(4):
                        b = 4 * half + j
                        mm = nc.tensor.transpose(ps[:, 4 + e % 2, P * j:P * j + P], y[:, i % 2, P * b:P * b + P],
                                                 K.ident[:])
                    mm.then_inc(y_ps, 1)

            qk_unit(0)
            for n in range(N):
                if n + 1 < N:
                    qk_unit(n + 1)
                if n:
                    pv(n - 1)
                turn(n)
                if n % AH == 2 and n > AH:
                    turn_y(tile(n) - 1)
            pv(N - 1)
            turn_y(TT - 1)

        @block.vector
        def _(dve):
            def logit(n):
                i = tile(n)
                L = P * (i + 1)
                dve.wait_ge(qk, n + 1)
                if n >= 2:
                    dve.wait_ge(t_ps, turn_groups(n - 1))
                nc.vector.tensor_tensor_reduce(
                    out=prob[:, n % 2, 0:L], in0=ps[:, 2 * (n % 2):2 * (n % 2) + 2, :].rearrange("p a n -> p (a n)")[:, 0:L],
                    in1=T.bias[:, BIAS_AT[i]:BIAS_AT[i] + L], scale=1.0, scalar=FAR, op0=ALU.add, op1=ALU.max,
                    accum_out=top[:, n % 2:n % 2 + 1]).then_inc(logits, 1)
                dve.wait_ge(logits, n + 1)
                nc.vector.tensor_scalar(nbias[:, n % 2:n % 2 + 1], top[:, n % 2:n % 2 + 1], -ATT_SCALE, None,
                                        ALU.mult).then_inc(nb, 1)

            def head(n):
                i, h = tile(n), n % AH
                dve.wait_ge(probs, n + 1)
                nc.vector.reciprocal(inv[:, n % 2:n % 2 + 1], total[:, n % 2:n % 2 + 1]).then_inc(inv_done, 1)
                dve.wait_ge(inv_done, n + 1)
                dve.wait_ge(o_ps, n + 1)
                if h == 0 and i >= 2:
                    dve.wait_ge(y_ps, 2 * (i - 1))
                nc.vector.tensor_scalar(y[:, i % 2, HD * h:HD * h + HD], ps[:, 6 + n % 2, 0:HD], inv[:, n % 2:n % 2 + 1],
                                        None, ALU.mult).then_inc(o_done, 1)

            for n in range(N + 2):
                if n < N:
                    logit(n)
                if n >= 2:
                    head(n - 2)

        @block.scalar
        def _(act):
            e = 0

            def move(upto):
                nonlocal e
                while e < upto:
                    kind, q, n = events[e]
                    if kind == "prob":
                        i = tile(n)
                        b0 = 4 * (q - turn_groups(n))
                        w = P * (min(b0 + 4, i + 1) - b0)
                        act.wait_ge(t_ps, q + 1)
                        if n >= 2:
                            act.wait_ge(o_ps, n - 1)
                        nc.scalar.copy(probT[:, n % 2, P * b0:P * b0 + w], ps[:, 4 + e % 2, 0:w]).then_inc(t_moved, 1)
                    else:
                        act.wait_ge(y_ps, q + 1)
                        half = q % 2
                        nc.scalar.copy(T.qT[:, 4 * half:4 * half + 4, P * n:P * n + P],
                                       ps[:, 4 + e % 2, :].rearrange("p (b t) -> p b t", b=4)).then_inc(y_moved, 1)
                    e += 1

            def exp(n):
                L = P * (tile(n) + 1)
                act.wait_ge(nb, n + 1)
                if n >= 2:
                    act.wait_ge(inv_done, n - 1)
                nc.scalar.activation(prob[:, n % 2, 0:L], prob[:, n % 2, 0:L], ACT.Exp, bias=nbias[:, n % 2:n % 2 + 1],
                                     scale=ATT_SCALE, accum_out=total[:, n % 2:n % 2 + 1]).then_inc(probs, 1)

            exp(0)
            for n in range(1, N):
                exp(n)
                move(seen["prob", turn_groups(n)])
            move(len(events))


def attend_samples(K, T):
    nc, A, ps = K.nc, K.A, K.ps
    KP = 2
    with ExitStack() as ctx:
        def sb(name, shape, dt=F32):
            return ctx.enter_context(nc.sbuf_tensor(name, shape, dt))
        pages = sb("pages", [1, DEC * NPAGE], I32)
        kpage, vpage = sb("kpage", [P, DEC, NPAGE, 256]), sb("vpage", [P, DEC, NPAGE, 256])
        ipage = sb("ipage", [P, DEC, NPAGE, HD])
        q_r = sb("q_r", [DEC, D])
        skT = sb("skT", [P, DEC, KP, SKEYS])
        sqx = sb("sqx", [P, 2320])
        siT, sqiT = sb("siT", [HD, DEC, SKEYS]), sb("sqiT", [HD, DEC, IH])
        swx = sb("swx", [IH, 9 * DEC])
        srelu = sb("srelu", [IH, 2, SKEYS])
        who, whoT = sb("who", [DEC, P]), sb("whoT", [P, DEC])
        ssc, swk, seq_, scu, sbias = (sb(n, [DEC, SKEYS]) for n in ("ssc", "swk", "seq", "scu", "sbias"))
        s8, scount = sb("s8", [DEC, 8]), sb("scount", [DEC, 2])
        sp_, sdiag = sb("sprob", [P, SKEYS]), sb("sdiag", [P, P])
        spT, snew = sb("spT", [P, NPAGE, P]), sb("snew", [DEC, P])
        stat = sb("sstat", [P, 4])
        table_in, who_in = K.sem("page_table_in"), K.sem("who_in")
        i_in, k_in, v_in = K.sem("index_pages_in"), K.sem("key_pages_in"), K.sem("value_pages_in")
        step = K.sem("sample_step")
        pe_small, pe_idx, pe_key, pe_rel = K.sem("small_turned"), K.sem("ipages_turned"), K.sem("kpages_turned"), K.sem("srelu_in_psum")
        idx_moved, key_moved, rel_done = K.sem("siT_done"), K.sem("skT_done"), K.sem("srelu_done")
        pe_score, pe_logit, exp_done, pe_pT, pe_out = (K.sem(n) for n in (
            "sscore_in_psum", "slogits_in_psum", "sprobs_done", "sprobsT_in_psum", "sout_in_psum"))
        max_done, y_done, y_out = K.sem("smax_done"), K.sem("sample_y_done"), K.sem("y_att_stored")
        ready, biased, diag_done, pT_done = K.sem("small_done"), K.sem("sbias_done"), K.sem("sdiag_done"), K.sem("spT_done")
        block = ctx.enter_context(nc.Block())

        @block.sync
        def _(sp):
            sp.dma_start(pages[:], A["page_table"].rearrange("b j -> (b j)").unsqueeze(0)).then_inc(table_in, 16)
            sp.dma_start(who[:], A["k_who"]).then_inc(who_in, 16)
            sp.dma_start(A["s_att"].rearrange("k p n -> p k n")[:, :, 0:SEQ], T.qT[:, :, 0:SEQ]).then_inc(y_out, 16)
            sp.wait_ge(table_in, 16)
            for cache, dst, done in (("cache_kidx", ipage, i_in), ("cache_k", kpage, k_in), ("cache_v", vpage, v_in)):
                n_pool = A[cache].shape[1]
                for b in range(DEC):
                    for j in range(NPAGE):
                        at = sp.value_load(pages[0:1, NPAGE * b + j:NPAGE * b + j + 1], min_val=0, max_val=n_pool - 1)
                        src = A[cache][0, bass.ds(at, 1)]
                        src = src.rearrange("a t d -> (a t) d" if cache == "cache_kidx" else "a t g d -> (a t) (g d)")
                        sp.dma_start(dst[:, b, j, :], src).then_inc(done, 16)
            sp.wait_ge(y_done, 1)
            sp.dma_start(A["s_att"].rearrange("k p n -> p k n")[:, :, SEQ:NT], T.qT[:, :, SEQ:NT]).then_inc(y_out, 16)
            sp.wait_ge(y_out, 32)

        @block.tensor
        def _(pe):
            tr, mm = nc.tensor.transpose, nc.tensor.matmul
            i8, i4 = K.ident[0:DEC, 0:DEC], K.ident[0:DEC, 0:DEC]
            pe.wait_ge(step, 1)
            pe.wait_ge(who_in, 16)
            for m in range(KB):
                tr(ps[:, 0, DEC * m:DEC * m + DEC], q_r[:, P * m:P * m + P], i8)
            for p in range(KP):
                tr(ps[:, 0, 64 + DEC * p:72 + DEC * p], T.k_s[:, P * p:P * p + P], i8)
            tr(ps[0:HD, 0, 80:88], T.ki_s[:], i8)
            for h in range(IH):
                tr(ps[0:HD, 0, 88 + DEC * h:96 + DEC * h], T.qi_s[:, HD * h:HD * h + HD], i8)
            tr(ps[0:IH, 0, 120:128], T.wi[0:DEC, TT, :], i4)
            tr(ps[:, 0, 128:136], who[:], i8).then_inc(pe_small, 1)
            pe.wait_ge(i_in, 16 * DEC * NPAGE)
            for a in range(4):
                if a >= 2:
                    pe.wait_ge(idx_moved, a - 1)
                for b in range(2):
                    for j in range(NPAGE):
                        m = tr(ps[0:HD, 1 + a % 2, 256 * b + P * j:256 * b + P * j + P], ipage[:, 2 * a + b, j, :], K.ident[:])
                m.then_inc(pe_idx, 1)
            pe.wait_ge(ready, 1)
            pe.wait_ge(idx_moved, 4)
            for b in range(DEC + 1):
                if b < DEC:
                    if b >= 2:
                        pe.wait_ge(rel_done, b - 1)
                    mm(ps[0:IH, 3 + b % 2, 0:SKEYS], sqiT[:, b, :], siT[:, b, :], start=True, stop=True).then_inc(pe_rel, 1)
                if b:
                    pe.wait_ge(rel_done, b)
                    mm(ps[0:DEC, 5, 0:SKEYS], swx[:, DEC * (b - 1):DEC * b], srelu[:, (b - 1) % 2, :],
                       start=(b == 1), stop=(b == DEC)).then_inc(pe_score, 1)
            pe.wait_ge(k_in, 16 * DEC * NPAGE)
            for b in range(DEC):
                if b >= 2:
                    pe.wait_ge(key_moved, b - 1)
                for p in range(KP):
                    for j in range(NPAGE):
                        m = tr(ps[:, 6 + b % 2, 256 * p + P * j:256 * p + P * j + P], kpage[:, b, j, P * p:P * p + P], K.ident[:])
                m.then_inc(pe_key, 1)
            pe.wait_ge(key_moved, DEC)
            pe.wait_ge(biased, 1)
            mm(ps[:, 3, 0:SKEYS], who[:], sbias[:], start=True, stop=False)
            for b in range(DEC):
                for p in range(KP):
                    last = b == DEC - 1 and p == KP - 1
                    m = mm(ps[:, 3, 0:SKEYS], sqx[:, 256 * b + P * p:256 * b + P * p + P], skT[:, b, p, :],
                           start=False, stop=last)
            m.then_inc(pe_logit, 1)
            pe.wait_ge(diag_done, 1)
            for j in range(NPAGE):
                tr(ps[:, 4, P * j:P * j + P], sp_[:, P * j:P * j + P], K.ident[:])
            mm(ps[0:DEC, 5, 0:P], whoT[:], sdiag[:], start=True, stop=True).then_inc(pe_pT, 1)
            pe.wait_ge(pT_done, 1)
            pe.wait_ge(v_in, 16 * DEC * NPAGE)
            for p in range(KP):
                mm(ps[:, 6 + p, 0:P], T.v[0:DEC, TT, P * p:P * p + P], snew[:], start=True, stop=False)
                for b in range(DEC):
                    for j in range(NPAGE):
                        m = mm(ps[:, 6 + p, AH * b:AH * b + AH], vpage[:, b, j, P * p:P * p + P],
                               spT[:, j, AH * b:AH * b + AH], start=False, stop=(b == DEC - 1 and j == NPAGE - 1))
            m.then_inc(pe_out, 1)

        @block.scalar
        def _(act):
            for a in range(4):
                act.wait_ge(pe_idx, a + 1)
                nc.scalar.copy(siT[:, 2 * a:2 * a + 2, 0:PAST], ps[0:HD, 1 + a % 2, :]
                               .rearrange("p (b s) -> p b s", b=2)).then_inc(idx_moved, 1)
            for b in range(DEC):
                act.wait_ge(pe_rel, b + 1)
                if b >= 2:
                    act.wait_ge(pe_score, b - 1)
                nc.scalar.activation(srelu[:, b % 2, :], ps[0:IH, 3 + b % 2, 0:SKEYS], ACT.Relu).then_inc(rel_done, 1)
            for b in range(DEC):
                act.wait_ge(pe_key, b + 1)
                nc.scalar.copy(skT[:, b, :, 0:PAST], ps[:, 6 + b % 2, :]
                               .rearrange("p (k s) -> p k s", k=KP)).then_inc(key_moved, 1)
            act.wait_ge(max_done, 1)
            nc.scalar.activation(sp_[:], sp_[:], ACT.Exp, bias=stat[:, 1:2], scale=ATT_SCALE,
                                 accum_out=stat[:, 2:3]).then_inc(exp_done, 1)

        @block.vector
        def _(dve):
            n = [0]
            v = nc.vector

            def link(ins):
                n[0] += 1
                ins.then_inc(step, 1)
                dve.wait_ge(step, n[0])

            gq = AH // KVH
            for p in range(KP):
                src = T.q_s[:, 512 * p:512 * p + 512].rearrange("b (g r d) -> b r g d", g=2, r=gq)
                c = v.tensor_copy(q_r[:, 512 * p:512 * p + 512].rearrange("b (r g d) -> b r g d", r=gq, g=2), src)
            link(c)
            link(v.memset(sqx[:], 0.0))
            link(v.memset(swx[:], 0.0))
            dve.wait_ge(pe_small, 1)
            for p in range(KP):
                for g in range(2):
                    off = P * p + gq * (2 * p + g)
                    rows = slice(HD * g, HD * g + HD)
                    v.tensor_copy(sqx[rows, off:off + 272 * DEC].rearrange("p (b x) -> p b x", x=272)[:, :, 0:gq],
                                  ps[rows, 0, 32 * p:32 * p + 32].rearrange("p (r b) -> p b r", b=DEC))
            for p in range(KP):
                v.tensor_copy(skT[:, :, p, PAST], ps[:, 0, 64 + DEC * p:72 + DEC * p])
            v.tensor_copy(siT[:, :, PAST], ps[0:HD, 0, 80:88])
            v.tensor_copy(sqiT[:], ps[0:HD, 0, 88:120].rearrange("p (h b) -> p b h", h=IH))
            v.tensor_copy(swx[:].rearrange("p (b x) -> p b x", x=9)[:, :, 0], ps[0:IH, 0, 120:128])
            v.tensor_copy(whoT[:], ps[:, 0, 128:136]).then_inc(ready, 1)
            dve.wait_ge(pe_score, DEC)
            link(v.tensor_copy(ssc[:], ps[0:DEC, 5, 0:SKEYS]))
            cur = ssc
            for r in range(STOPK // 8):
                link(v.max(s8[:], cur[:]))
                if r < STOPK // 8 - 1:
                    link(v.match_replace(swk[:], s8[:], cur[:], FAR))
                    cur = swk
            thr = s8[:, 7:8]
            link(v.tensor_scalar(swk[:], ssc[:], thr, None, ALU.is_gt, ALU.add, accum_out=scount[:, 0:1]))
            link(v.tensor_scalar(scount[:, 1:2], scount[:, 0:1], -1.0, float(STOPK), ALU.mult, ALU.add))
            link(v.tensor_scalar(seq_[:], ssc[:], thr, None, ALU.is_equal))
            link(v.tensor_tensor_scan(scu[:], K.ones[0:DEC, 0:1].to_broadcast([DEC, SKEYS]), seq_[:], 0.0, ALU.mult, ALU.add))
            link(v.scalar_tensor_tensor(scu[:], scu[:], scount[:, 1:2], seq_[:], ALU.is_le, ALU.mult))
            link(v.scalar_tensor_tensor(swk[:], swk[:], -1.0, scu[:], ALU.add, ALU.add))
            v.tensor_scalar(sbias[:], swk[:], -OFF, None, ALU.mult).then_inc(biased, 1)
            dve.wait_ge(pe_logit, 1)
            link(v.tensor_copy(sp_[:], ps[:, 3, 0:SKEYS]))
            link(v.reduce_max(stat[:, 0:1], sp_[:], AX.X))
            v.tensor_scalar(stat[:, 1:2], stat[:, 0:1], -ATT_SCALE, None, ALU.mult).then_inc(max_done, 1)
            dve.wait_ge(exp_done, 1)
            link(v.reciprocal(stat[:, 3:4], stat[:, 2:3]))
            link(v.tensor_scalar(sp_[:], sp_[:], stat[:, 3:4], None, ALU.mult))
            v.tensor_scalar(sdiag[:], K.ident[:], sp_[:, PAST:SKEYS], None, ALU.mult).then_inc(diag_done, 1)
            dve.wait_ge(pe_pT, 1)
            v.tensor_copy(snew[:], ps[0:DEC, 5, 0:P])
            v.tensor_copy(spT[:].rearrange("p j h -> p (j h)"), ps[:, 4, 0:NPAGE * P]).then_inc(pT_done, 1)
            dve.wait_ge(pe_out, 1)
            for p in range(KP):
                for g in range(2):
                    for odd in range(2):
                        kv = 2 * p + g
                        src = ps[HD * g:HD * g + HD, 6 + p, 0:P].rearrange("p (b k a o) -> p k a o b", k=KVH, a=2, o=2)
                        c = v.tensor_copy(T.qT[HD * odd:HD * odd + HD, 2 * kv:2 * kv + 2, SEQ:NT], src[:, kv, :, odd, :])
            c.then_inc(y_done, 1)


def steps(K, S):
    nc, A, ps = K.nc, K.A, K.ps
    NC = TT * HEADS
    W = NC + DEC
    with ExitStack() as ctx:
        def sb(name, shape):
            return ctx.enter_context(nc.sbuf_tensor(name, shape, F32))
        u, e, z, t, p = (sb("dt_" + n, [P, W]) for n in "uezts")
        a_row, a_col = sb("a_row", [P, HEADS]), sb("a_col", [HEADS, 1])
        head_x = sb("head_x", [HEADS, INNER])
        spread = sb("spread", [HEADS, 17])
        d_end = sb("d_end", [P, NC])
        head_in, step = K.sem("head_in"), K.sem("dt_step")
        arg_ready, exp_done, a_done = K.sem("dt_arg"), K.sem("dt_exp"), K.sem("a_exp")
        dta_done, sums, decays = K.sem("dta_done"), K.sem("decay_sums"), K.sem("decays_done")
        sdec_arg, sdec, sp_ready, spread_ps = K.sem("sdecay_arg"), K.sem("sdecay_done"), K.sem("spread_ready"), K.sem("spread_in_psum")
        block = ctx.enter_context(nc.Block())

        @block.sync
        def _(sp):
            sp.dma_start(head_x[:], A["k_head"]).then_inc(head_in, 16)

        @block.scalar
        def _(act):
            nc.scalar.activation(a_row[:], K.heads_row[:, 1, :], ACT.Exp).then_inc(a_done, 1)
            nc.scalar.activation(a_col[:], K.heads_col[:, 1:2], ACT.Exp).then_inc(a_done, 1)
            act.wait_ge(arg_ready, 1)
            nc.scalar.activation(e[:], e[:], ACT.Exp).then_inc(exp_done, 1)
            act.wait_ge(sdec_arg, 1)
            nc.scalar.activation(spread[:, 0:DEC], spread[:, 0:DEC], ACT.Exp).then_inc(sdec, 1)
            act.wait_ge(sums, 1)
            for bank, dst in ((0, S.e_acs[:].rearrange("p c h -> p (c h)")), (1, d_end[:]),
                              (2, S.c_dec[:].rearrange("p c h -> p (c h)"))):
                nc.scalar.activation(dst, ps[:, bank, 0:NC], ACT.Exp).then_inc(decays, 1)

        @block.tensor
        def _(pe):
            pe.wait_ge(dta_done, 1)
            dta = S.dta[:].rearrange("p c h -> p (c h)")
            nc.tensor.matmul(ps[:, 0, 0:NC], K.le[:], dta, start=True, stop=True)
            nc.tensor.matmul(ps[:, 1, 0:NC], K.gt[:], dta, start=True, stop=True)
            nc.tensor.matmul(ps[:, 2, 0:NC], K.ones[:], dta, start=True, stop=True).then_inc(sums, 1)
            pe.wait_ge(sp_ready, 1)
            pe.wait_ge(head_in, 16)
            for b in range(INNER // P):
                mm = nc.tensor.matmul(ps[:, 3, 17 * b:17 * b + 17], head_x[:, P * b:P * b + P], spread[:],
                                      start=True, stop=True)
            mm.then_inc(spread_ps, 1)

        @block.vector
        def _(dve):
            n = [0]
            v = nc.vector

            def link(ins):
                n[0] += 1
                ins.then_inc(step, 1)
                dve.wait_ge(step, n[0])

            link(v.memset(u[:, NC:W], 0.0))
            link(v.tensor_tensor(u[:, 0:NC].rearrange("p (c h) -> p c h", h=HEADS), K.dt_raw[:],
                                 K.heads_row[:, 0, :].unsqueeze(1).to_broadcast([P, TT, HEADS]), ALU.add))
            link(v.tensor_scalar(u[0:HEADS, NC:W], K.dtT_raw[:], K.heads_col[:, 0:1], None, ALU.add))
            v.scalar_tensor_tensor(e[:], u[:], -1.0, u[:], ALU.mult, ALU.min).then_inc(arg_ready, 1)
            dve.wait_ge(exp_done, 1)
            link(v.tensor_scalar(t[:], e[:], 2.0, None, ALU.add))
            link(v.reciprocal(t[:], t[:]))
            link(v.tensor_tensor(z[:], e[:], t[:], ALU.mult))
            link(v.tensor_tensor(t[:], z[:], z[:], ALU.mult))
            link(v.tensor_scalar(p[:], t[:], 1.0 / 15.0, None, ALU.mult))
            for k in (13, 11, 9, 7, 5, 3):
                link(v.scalar_tensor_tensor(p[:], p[:], 1.0 / k, t[:], ALU.add, ALU.mult))
            link(v.scalar_tensor_tensor(z[:], p[:], 1.0, z[:], ALU.add, ALU.mult))
            link(v.tensor_scalar(u[:], u[:], 0.0, None, ALU.max))
            link(v.scalar_tensor_tensor(u[:], z[:], 2.0, u[:], ALU.mult, ALU.add))
            dve.wait_ge(a_done, 2)
            dt3 = u[:, 0:NC].rearrange("p (c h) -> p c h", h=HEADS)
            link(v.tensor_copy(S.dt[:], dt3))
            link(v.tensor_scalar(a_row[:], a_row[:], -1.0, None, ALU.mult))
            v.tensor_tensor(S.dta[:], dt3, a_row[:].unsqueeze(1).to_broadcast([P, TT, HEADS]), ALU.mult).then_inc(dta_done, 1)
            link(v.tensor_scalar(a_col[:], a_col[:], -1.0, None, ALU.mult))
            link(v.tensor_copy(spread[:, DEC:2 * DEC], u[0:HEADS, NC:W]))
            link(v.tensor_copy(spread[:, 16:17], K.heads_col[:, 2:3]))
            v.tensor_scalar(spread[:, 0:DEC], u[0:HEADS, NC:W], a_col[:], None, ALU.mult).then_inc(sdec_arg, 1)
            dve.wait_ge(sdec, 1)
            link(v.tensor_copy(a_col[:], a_col[:]))
            v.tensor_copy(a_col[:], K.heads_col[:, 0:1]).then_inc(sp_ready, 1)
            dve.wait_ge(decays, 3)
            link(v.tensor_tensor(S.ddt[:].rearrange("p c h -> p (c h)"), d_end[:], u[:, 0:NC], ALU.mult))
            dve.wait_ge(spread_ps, 1)
            link(v.tensor_copy(S.hx[:].rearrange("p b s -> p (b s)"), ps[:, 3, 0:17 * 16]))


def ssm(K, hT, S):
    nc, A, ps = K.nc, K.A, K.ps
    first = K.span["g0"][0]
    FBS = 6
    PW = CONV - 1 + NT
    with ExitStack() as ctx:
        def sb(name, shape):
            return ctx.enter_context(nc.sbuf_tensor(name, shape, F32))
        pre = sb("pre", [P, 2, PW])
        post = sb("post", [P, FBS, SEQ])
        z = sb("z", [P, TT, GW])
        tail = sb("tail", [P, FBS, 11])
        tail_rows = sb("tail_rows", [11, FBS, P])
        st_rows = sb("st_rows", [DEC * 3, FBS, P])
        wg = sb("wg", [P, 5, FBS])
        cx, ct = sb("cx", [P, FBS, DEC]), sb("ct", [P, FBS, DEC])
        zs, xdt_s = sb("zs", [P, 4, DEC]), sb("xdt_s", [P, 4, DEC])
        bc_diag = sb("bc_diag", [P, 2, 4, P])
        stt = sb("stt", [P, 4, 4, NST])
        tmp = sb("stmp", [P, 4, 4, NST])
        ysum = sb("ysum", [P, 4, DEC])
        ysq, yrs = sb("ysq", [P, 4, DEC]), sb("yrs", [P, DEC])
        cbm = sb("cbm", [P, 2, P])
        btok = sb("btok", [P, 2, P])
        seg = sb("seg", [P, GH, P])
        m = sb("m", [P, 2, GH, P])
        xt, xdt, xw, xd = sb("xt", [P, GW]), sb("xdt", [P, 2, GW]), sb("xw", [P, 2, GW]), sb("xd", [P, 2, GW])
        y, ysq2 = sb("ssm_y", [P, 2, GW]), sb("ssm_ysq", [P, GW])
        state = sb("state", [P, GW])
        yT = sb("ssm_yT", [P, 2, 4, P])
        stat = sb("ssm_stat", [P, 4, 2])
        fin = sb("fin", [P, 4, P])

        gemm, pre_done, conv_done, post_done = K.sem("xbc_sums"), K.sem("pre_done"), K.sem("conv_done"), K.sem("post_done")
        conv_step, tails = K.sem("conv_step"), K.sem("tails_kept")
        z_ps, z_done, zs_ps, zs_done = K.sem("z_sums"), K.sem("z_done"), K.sem("zs_sums"), K.sem("zs_done")
        st_in, st_used = K.store_sem("conv_state_in"), K.sem("conv_state_turned")
        rows_ps, rows_done, rows_out = K.sem("tail_rows_in_psum"), K.sem("tail_rows_done"), K.store_sem("tail_rows_stored")
        cs_sum, cs_done = K.sem("sample_conv_sum"), K.sem("sample_conv_done")
        diag, bc_ps, bc_used = K.sem("bc_diag_done"), K.sem("bc_in_psum"), K.sem("bc_used")
        s_in, s_dec, s_new, s_out = K.store_sem("states_in"), K.sem("states_decayed"), K.sem("states_new"), K.store_sem("states_stored")
        sstep, ysq_done, yss_ps, yroot, yrooted = (K.sem(n) for n in (
            "sample_ssm_step", "ysq_done", "ysq_summed", "yroot_arg", "yroot_done"))
        seg_in, seg_ps, m_exp, m_done = K.sem("seg_in"), K.sem("seg_in_psum"), K.sem("m_exp"), K.sem("m_done")
        bcb_ps, cb_done, xt_ps, xt_done = K.sem("cb_b_in_psum"), K.sem("cb_b_done"), K.sem("xt_in_psum"), K.sem("xt_done")
        xdt_done, xw_done, xd_done = K.sem("xdt_done"), K.sem("xw_done"), K.sem("xd_done")
        yd_ps, yo_ps, sp_ps = K.sem("ydiag_in_psum"), K.sem("yoff_in_psum"), K.sem("state_in_psum")
        yo_done, s_scaled, s_done, yd_done = K.sem("yoff_done"), K.sem("state_decayed"), K.sem("state_done"), K.sem("ydiag_done")
        ystep, ygated, ysquared, ymean, yroot2, ynormed = (K.sem(n) for n in (
            "y_step", "y_gated", "y_squared", "y_mean", "y_root", "y_normed"))
        yT_ps, yT_done, yT_out = K.sem("ssm_yT_in_psum"), K.sem("ssm_yT_done"), [K.store_sem(f"ssm_yT_stored{i}") for i in range(2)]
        fin_ps, fin_done, fin_out = K.sem("final_in_psum"), K.sem("final_done"), K.store_sem("final_stored")
        old_out = K.store_sem("old_conv_rows_stored")
        block = ctx.enter_context(nc.Block())

        def feature(g, f):
            return 4 * g + f if f < 4 else (16 + g if f == 4 else 20 + g)

        def slab(g, i):
            return first + 5 * g + i

        @block.sync
        def _(sp):
            for g in range(GROUPS):
                for i in range(5):
                    n = slab(g, i) + RING
                    if n < len(K.slabs):
                        if i < 3:
                            sp.wait_ge(gemm, 18 * g + 6 * (i + 1))
                        else:
                            sp.wait_ge(zs_ps, 2 * g + i - 2)
                        for place, src in K.slabs[n]:
                            sp.dma_start(place(K.ring[:, n % RING, :]), src).then_inc(K.landed[n % RING], 16)

        @block.gpsimd
        def _(pool):
            v = nc.gpsimd
            v.memset(pre[:, :, 0:CONV - 1], 0.0).then_inc(conv_step, 1)
            pool.dma_start(A["conv_sample"][0, :, 0:2, :], A["state_conv"][0, :, 1:3, :]).then_inc(old_out, 16)

            def rows_in(g):
                for f in range(FBS):
                    c = P * feature(g, f)
                    pool.dma_start(st_rows[:, f, :], A["state_conv"][0, :, :, c:c + P].rearrange("b j c -> (b j) c"))\
                        .then_inc(st_in, 16)

            def states(g, q, name):
                heads = A[name][0, 4 * q:4 * q + 4, GH * g:GH * g + GH]
                return heads.rearrange("b h p n -> b (h p) n").rearrange("b (k q) n -> q b k n", q=P)

            def store(g, c):
                pool.wait_ge(yT_done, TT * g + c + 1)
                pool.dma_start(A["s_ssm"].rearrange("k p n -> p k n")[:, 4 * g:4 * g + 4, P * c:P * c + P],
                               yT[:, c % 2]).then_inc(yT_out[c % 2], 16)

            rows_in(0)
            for g in range(GROUPS):
                for q in range(2):
                    h = 2 * g + q
                    if h:
                        pool.wait_ge(s_out, 16 * 4 * h)
                        pool.wait_ge(bc_used, h)
                    for b in range(4):
                        pool.dma_start(stt[:, b], states(g, q, "state_ssm")[:, b]).then_inc(s_in, 16)
                    pool.wait_ge(cs_done, g + 1)
                    if h:
                        pool.wait_ge(bc_ps, 2 * h)
                    for k in range(2):
                        v.tensor_tensor(bc_diag[:, k], K.ident[:].unsqueeze(1).to_broadcast([P, 4, P]),
                                        cx[:, 4 + k, 4 * q:4 * q + 4].unsqueeze(2).to_broadcast([P, 4, P]), ALU.mult)\
                            .then_inc(diag, 1)
                    pool.wait_ge(s_in, 16 * 4 * (h + 1))
                    for b in range(4):
                        d = v.tensor_tensor(stt[:, b], stt[:, b],
                                            S.hx[:, 4 * g:4 * g + 4, 4 * q + b].unsqueeze(2).to_broadcast([P, 4, NST]),
                                            ALU.mult)
                    d.then_inc(s_dec, 1)
                    if q == 0:
                        pool.wait_ge(rows_done, 2 * (g + 1))
                        for f in range(FBS):
                            c = P * feature(g, f)
                            pool.dma_start(A["conv_prompt"][0, 0, :, c:c + P], tail_rows[0:3, f, :]).then_inc(rows_out, 16)
                            pool.dma_start(A["conv_sample"][0, :, 2, c:c + P], tail_rows[3:11, f, :]).then_inc(rows_out, 16)
                        if g + 1 < GROUPS:
                            pool.wait_ge(st_used, g + 1)
                            rows_in(g + 1)
                    pool.wait_ge(s_new, h + 1)
                    for b in range(4):
                        pool.dma_start(states(g, q, "ssm_sample")[:, b], stt[:, b]).then_inc(s_out, 16)
                for c in range(TT):
                    n = TT * g + c
                    if n:
                        pool.wait_ge(seg_ps, n)
                    v.tensor_tensor(seg[:], K.le[:].unsqueeze(1).to_broadcast([P, GH, P]),
                                    S.dta[:, c, GH * g:GH * g + GH].unsqueeze(2).to_broadcast([P, GH, P]), ALU.mult)\
                        .then_inc(seg_in, 1)
                    pool.wait_ge(xt_done, n + 1)
                    if n >= 2:
                        pool.wait_ge(sp_ps, n - 1)
                        pool.wait_ge(yd_done, 2 * (n - 1))
                    xh = xt[:].rearrange("p (h d) -> p h d", d=HD)

                    def per_head(vec):
                        return vec.unsqueeze(2).to_broadcast([P, GH, HD])
                    v.tensor_tensor(xw[:, c % 2].rearrange("p (h d) -> p h d", d=HD), xh,
                                    per_head(S.ddt[:, c, GH * g:GH * g + GH]), ALU.mult).then_inc(xw_done, 1)
                    v.tensor_tensor(xd[:, c % 2].rearrange("p (h d) -> p h d", d=HD), xh,
                                    per_head(K.heads_row[:, 2, GH * g:GH * g + GH]), ALU.mult).then_inc(xd_done, 1)
                    if c >= 2:
                        store(g, c - 2)
                store(g, TT - 2)
                store(g, TT - 1)
                pool.wait_ge(fin_done, g + 1)
                pool.dma_start(A["ssm_prompt"][0, 0].rearrange("h p n -> (h p) n")[GW * g:GW * g + GW]
                               .rearrange("(k q) n -> q k n", q=P), fin[:]).then_inc(fin_out, 16)
            pool.wait_ge(s_out, 16 * 8 * GROUPS)
            pool.wait_ge(rows_out, 16 * 2 * FBS * GROUPS)
            for i in range(2):
                pool.wait_ge(yT_out[i], 8 * TT * GROUPS)
            pool.wait_ge(fin_out, 16 * GROUPS)
            pool.wait_ge(old_out, 16)

        @block.tensor
        def _(pe):
            tr, mm = nc.tensor.transpose, nc.tensor.matmul

            def front(g, c):
                n = TT * g + c
                cols = slice(P * c, P * c + P)
                if c == 0:
                    pe.wait_ge(post_done, FBS * (g + 1))
                if n:
                    pe.wait_ge(cb_done, 2 * n)
                tr(ps[:, 0, P:2 * P], post[:, 4, cols], K.ident[:])
                mm(ps[:, 0, 0:P], post[:, 4, cols], post[:, 5, cols], start=True, stop=True).then_inc(bcb_ps, 1)
                if n:
                    pe.wait_ge(xt_done, n)
                    pe.wait_ge(xdt_done, n)
                for j in range(4):
                    t = tr(ps[:, 3, P * j:P * j + P], post[:, j, cols], K.ident[:])
                t.then_inc(xt_ps, 1)
                pe.wait_ge(seg_in, n + 1)
                if n:
                    pe.wait_ge(m_exp, n)
                for half in range(2):
                    s = mm(ps[:, 1 + half, :], K.gt[:], seg[:, 4 * half:4 * half + 4, :].rearrange("p h l -> p (h l)"),
                           start=True, stop=True)
                s.then_inc(seg_ps, 1)

            def back(g, c):
                n = TT * g + c
                cols = slice(P * c, P * c + P)
                pe.wait_ge(m_done, n + 1)
                pe.wait_ge(xdt_done, n + 1)
                if n:
                    pe.wait_ge(yd_done, 2 * n)
                for r in range(GH):
                    d = mm(ps[:, 5, HD * r:HD * r + HD], m[:, c % 2, r, :], xdt[:, c % 2, HD * r:HD * r + HD],
                           start=True, stop=True)
                d.then_inc(yd_ps, 1)
                if c:
                    pe.wait_ge(s_done, n)
                    if n > 1:
                        pe.wait_ge(yo_done, n - g - 1)
                    mm(ps[:, 4, :], post[:, 5, cols], state[:], start=True, stop=True).then_inc(yo_ps, 1)
                pe.wait_ge(xw_done, n + 1)
                pe.wait_ge(cb_done, 2 * n + 2)
                if n:
                    pe.wait_ge(s_done, n)
                mm(ps[:, 6, :], btok[:, c % 2, :], xw[:, c % 2, :], start=True, stop=True).then_inc(sp_ps, 1)

            def turn(g, c):
                n = TT * g + c
                pe.wait_ge(ynormed, n + 1)
                if n:
                    pe.wait_ge(yT_done, n)
                for j in range(4):
                    t = tr(ps[:, 7, P * j:P * j + P], y[:, c % 2, P * j:P * j + P], K.ident[:])
                t.then_inc(yT_ps, 1)

            for g in range(GROUPS):
                if g:
                    pe.wait_ge(yT_done, TT * g)
                    pe.wait_ge(fin_done, g)
                for f in range(FBS):
                    if f % 2 == 0:
                        pe.wait_ge(*ring_landed(K, slab(g, f // 2)))
                    w = slab_of(K, slab(g, f // 2))
                    for c in range(TC):
                        u = 18 * g + 3 * f + c
                        if u >= 4:
                            pe.wait_ge(pre_done, u - 3)
                        for k in range(KB):
                            a = mm(ps[:, 4 + u % 4, 0:CW], w[:, k, P * (f % 2):P * (f % 2) + P],
                                   hT[:, k, CW * c:CW * c + CW], start=(k == 0), stop=(k == KB - 1))
                        a.then_inc(gemm, 1)
                for i in range(2):
                    n = slab(g, 3 + i)
                    pe.wait_ge(*ring_landed(K, n))
                    w = slab_of(K, n)
                    for t in range(TT):
                        u = 16 * g + 8 * i + t
                        if u >= 4:
                            pe.wait_ge(z_done, u - 3)
                        if g and i == 0 and t < 4:
                            pe.wait_ge(m_exp, TT * g)
                            pe.wait_ge(cb_done, 2 * TT * g)
                            pe.wait_ge(xdt_done, TT * g)
                        for k in range(KB):
                            a = mm(ps[:, u % 4, 0:256], hT[:, k, P * t:P * t + P], w[:, k, :],
                                   start=(k == 0), stop=(k == KB - 1))
                        a.then_inc(z_ps, 1)
                    if i == 0:
                        pe.wait_ge(pre_done, 18 * (g + 1))
                    for fb in range(2):
                        for k in range(KB):
                            a = mm(ps[:, 4, DEC * (2 * i + fb):DEC * (2 * i + fb) + DEC], w[:, k, P * fb:P * fb + P],
                                   hT[:, k, SEQ:NT], start=(k == 0), stop=(k == KB - 1))
                    a.then_inc(zs_ps, 1)
                    if i == 0:
                        pe.wait_ge(st_in, 16 * FBS * (g + 1))
                        for f in range(FBS):
                            t = tr(ps[:, 5, 24 * f:24 * f + 24], st_rows[:, f, :], K.ident[0:24, 0:24])
                        t.then_inc(st_used, 1)
                        pe.wait_ge(tails, FBS * (g + 1))
                        for f in range(FBS):
                            t = tr(ps[0:11, 6 + f // 3, P * (f % 3):P * (f % 3) + P], tail[:, f, :], K.ident[:])
                        t.then_inc(rows_ps, 1)
                for q in range(2):
                    h = 2 * g + q
                    pe.wait_ge(diag, 2 * h + 2)
                    if q == 0:
                        pe.wait_ge(rows_done, 2 * (g + 1))
                    else:
                        pe.wait_ge(bc_used, h)
                    for k in range(2):
                        mm(ps[:, 6 + k, :], K.ones[:], bc_diag[:, k].rearrange("p b n -> p (b n)"),
                           start=True, stop=True).then_inc(bc_ps, 1)
                pe.wait_ge(ysq_done, g + 1)
                for j in range(4):
                    a = mm(ps[:, 5, 0:DEC], K.ones[:], ysq[:, j, :], start=(j == 0), stop=(j == 3))
                a.then_inc(yss_ps, 1)
                pe.wait_ge(z_done, 16 * (g + 1))
                pe.wait_ge(zs_done, g + 1)
                pe.wait_ge(bc_used, 2 * (g + 1))
                pe.wait_ge(yroot, g + 1)
                front(g, 0)
                for c in range(TT):
                    if c + 1 < TT:
                        front(g, c + 1)
                    back(g, c)
                    if c:
                        turn(g, c - 1)
                turn(g, TT - 1)
                pe.wait_ge(s_done, TT * (g + 1))
                for j in range(4):
                    t = tr(ps[:, 4, P * j:P * j + P], state[:, P * j:P * j + P], K.ident[:])
                t.then_inc(fin_ps, 1)

        @block.scalar
        def _(act):
            a = nc.scalar
            for g in range(GROUPS):
                def silu(f):
                    act.wait_ge(conv_done, FBS * g + f + 1)
                    a.activation(post[:, f, :], post[:, f, :], ACT.Silu).then_inc(post_done, 1)
                for f in range(FBS):
                    for c in range(TC):
                        u = 18 * g + 3 * f + c
                        act.wait_ge(gemm, u + 1)
                        if c == 0 and FBS * g + f >= 2:
                            act.wait_ge(conv_done, FBS * g + f - 1)
                            act.wait_ge(tails, FBS * g + f - 1)
                        a.copy(pre[:, f % 2, CONV - 1 + CW * c:CONV - 1 + CW * c + CW], ps[:, 4 + u % 4, 0:CW])\
                            .then_inc(pre_done, 1)
                    if f:
                        silu(f - 1)
                silu(FBS - 1)

                def z_rows(i):
                    for t in range(TT):
                        u = 16 * g + 8 * i + t
                        act.wait_ge(z_ps, u + 1)
                        if g and i == 0 and t == 0:
                            act.wait_ge(ygated, TT * g)
                        a.activation(z[:, t, 256 * i:256 * i + 256], ps[:, u % 4, 0:256], ACT.Silu).then_inc(z_done, 1)
                z_rows(0)
                act.wait_ge(rows_ps, g + 1)
                if g:
                    act.wait_ge(rows_out, 16 * 2 * FBS * g)
                for half in range(2):
                    a.copy(tail_rows[:, 3 * half:3 * half + 3, :].rearrange("p f c -> p (f c)"),
                           ps[0:11, 6 + half, 0:3 * P]).then_inc(rows_done, 1)
                act.wait_ge(cs_sum, g + 1)
                a.activation(cx[:], ct[:], ACT.Silu).then_inc(cs_done, 1)
                z_rows(1)
                act.wait_ge(zs_ps, 2 * g + 2)
                a.activation(zs[:].rearrange("p b s -> p (b s)"), ps[:, 4, 0:4 * DEC], ACT.Silu).then_inc(zs_done, 1)
                act.wait_ge(yroot, g + 1)
                a.activation(yrs[:], yrs[:], ACT.Sqrt).then_inc(yrooted, 1)

                def decay(c):
                    n = TT * g + c
                    act.wait_ge(xt_ps, n + 1)
                    if n:
                        act.wait_ge(xd_done, n)
                    a.copy(xt[:], ps[:, 3, :]).then_inc(xt_done, 1)
                    act.wait_ge(seg_ps, n + 1)
                    if n >= 2:
                        act.wait_ge(yd_ps, n - 1)
                    a.activation(m[:, c % 2].rearrange("p h l -> p (h l)"), ps[:, 1:3, :].rearrange("p a n -> p (a n)"),
                                 ACT.Exp).then_inc(m_exp, 1)

                def norm(c):
                    n = TT * g + c
                    act.wait_ge(ygated, n + 1)
                    if n:
                        act.wait_ge(ysquared, n)
                    a.activation(ysq2[:], y[:, c % 2, :], ACT.Square, accum_out=stat[:, 0, c % 2:c % 2 + 1])\
                        .then_inc(ysquared, 1)
                    act.wait_ge(ymean, n + 1)
                    a.activation(stat[:, 2, c % 2:c % 2 + 1], stat[:, 1, c % 2:c % 2 + 1], ACT.Sqrt).then_inc(yroot2, 1)

                def out(c):
                    n = TT * g + c
                    act.wait_ge(yT_ps, n + 1)
                    if n >= 2:
                        act.wait_ge(yT_out[c % 2], 16 * (n // 2))
                    for j in range(4):
                        k = 136 + 4 * g + j
                        o = a.activation(yT[:, c % 2, j, :], ps[:, 7, P * j:P * j + P], ACT.Copy, scale=K.vecs[:, k:k + 1])
                    o.then_inc(yT_done, 1)

                decay(0)
                for c in range(TT):
                    if c + 1 < TT:
                        decay(c + 1)
                    norm(c)
                    if c:
                        out(c - 1)
                out(TT - 1)
                act.wait_ge(fin_ps, g + 1)
                if g:
                    act.wait_ge(fin_out, 16 * g)
                a.copy(fin[:].rearrange("p k n -> p (k n)"), ps[:, 4, :]).then_inc(fin_done, 1)

        @block.vector
        def _(dve):
            v = nc.vector
            nconv, nss, ny = [0], [0], [0]

            def link(ins, sem, count):
                count[0] += 1
                ins.then_inc(sem, 1)
                dve.wait_ge(sem, count[0])

            nconv[0] = 1
            for g in range(GROUPS):
                for f in range(FBS):
                    b = feature(g, f)
                    src = pre[:, f % 2, :]
                    dve.wait_ge(pre_done, 18 * g + 3 * f + 3)
                    if g == 0 and f == 0:
                        dve.wait_ge(conv_step, 1)
                    if g and f == 0:
                        dve.wait_ge(yT_done, TT * g)
                        dve.wait_ge(st_used, g)
                        dve.wait_ge(rows_ps, g)
                    v.tensor_copy(tail[:, f, :], src[:, SEQ:PW]).then_inc(tails, 1)
                    link(v.tensor_scalar(post[:, f, :], src[:, 0:SEQ], K.vecs[:, b:b + 1], K.vecs[:, 96 + b:97 + b],
                                         ALU.mult, ALU.add), conv_step, nconv)
                    for i in range(1, CONV):
                        ins = v.scalar_tensor_tensor(post[:, f, :], src[:, i:i + SEQ], K.vecs[:, 24 * i + b:24 * i + b + 1],
                                                     post[:, f, :], ALU.mult, ALU.add)
                        if i < CONV - 1:
                            link(ins, conv_step, nconv)
                        else:
                            ins.then_inc(conv_done, 1)
                allv = K.vecs[:, 0:120].rearrange("p (i b) -> p i b", b=24)
                v.tensor_copy(wg[:, :, 0:4], allv[:, :, 4 * g:4 * g + 4])
                v.tensor_copy(wg[:, :, 4:5], allv[:, :, 16 + g:17 + g])
                link(v.tensor_copy(wg[:, :, 5:6], allv[:, :, 20 + g:21 + g]), sstep, nss)
                dve.wait_ge(st_used, g + 1)
                dve.wait_ge(tails, FBS * (g + 1))
                if g:
                    dve.wait_ge(cs_done, g)

                def tap(i):
                    return wg[:, i, :].unsqueeze(2).to_broadcast([P, FBS, DEC])
                old = ps[:, 5, 0:24 * FBS].rearrange("p (f b j) -> p f b j", f=FBS, j=3)
                link(v.tensor_tensor(ct[:], tail[:, :, 3:11], tap(3), ALU.mult), sstep, nss)
                link(v.tensor_tensor(ct[:], ct[:], tap(4), ALU.add), sstep, nss)
                for i in range(3):
                    w8 = tmp[:, 0, 0, 0:FBS * DEC].rearrange("p (f b) -> p f b", f=FBS)
                    link(v.tensor_tensor(w8, old[:, :, :, i], tap(i), ALU.mult), sstep, nss)
                    ins = v.tensor_tensor(ct[:], ct[:], w8, ALU.add)
                    if i < 2:
                        link(ins, sstep, nss)
                    else:
                        ins.then_inc(cs_sum, 1)
                dve.wait_ge(cs_done, g + 1)
                hx = S.hx[:, 4 * g:4 * g + 4, :]
                link(v.tensor_tensor(xdt_s[:], cx[:, 0:4, :], hx[:, :, 8:16], ALU.mult), sstep, nss)
                for q in range(2):
                    h = 2 * g + q
                    dve.wait_ge(bc_ps, 2 * h + 2)
                    for b in range(4):
                        bb = ps[:, 6, P * b:P * b + P].unsqueeze(1).to_broadcast([P, 4, NST])
                        t = v.tensor_tensor(tmp[:, b], bb, xdt_s[:, :, 4 * q + b].unsqueeze(2).to_broadcast([P, 4, NST]), ALU.mult)
                    link(t, sstep, nss)
                    dve.wait_ge(s_dec, h + 1)
                    v.tensor_tensor(stt[:], stt[:], tmp[:], ALU.add).then_inc(s_new, 1)
                    dve.wait_ge(s_new, h + 1)
                    for b in range(4):
                        cc = ps[:, 7, P * b:P * b + P].unsqueeze(1).to_broadcast([P, 4, NST])
                        t = v.tensor_tensor(tmp[:, b], cc, stt[:, b], ALU.mult)
                    t.then_inc(bc_used, 1)
                    dve.wait_ge(bc_used, h + 1)
                    link(v.tensor_reduce(ysum[:, :, 4 * q:4 * q + 4].rearrange("p k b -> p b k"), tmp[:], AX.X, ALU.add),
                         sstep, nss)
                link(v.tensor_tensor(xdt_s[:], cx[:, 0:4, :], hx[:, :, 16:17].to_broadcast([P, 4, DEC]), ALU.mult), sstep, nss)
                link(v.tensor_tensor(ysum[:], ysum[:], xdt_s[:], ALU.add), sstep, nss)
                dve.wait_ge(zs_done, g + 1)
                link(v.tensor_tensor(ysum[:], ysum[:], zs[:], ALU.mult), sstep, nss)
                v.tensor_tensor(ysq[:], ysum[:], ysum[:], ALU.mult).then_inc(ysq_done, 1)
                dve.wait_ge(yss_ps, g + 1)
                v.tensor_scalar(yrs[:], ps[:, 5, 0:DEC], 1.0 / GW, EPS, ALU.mult, ALU.add).then_inc(yroot, 1)
                dve.wait_ge(yrooted, g + 1)
                link(v.reciprocal(yrs[:], yrs[:]), sstep, nss)
                link(v.tensor_tensor(ysum[:], ysum[:], yrs[:].unsqueeze(1).to_broadcast([P, 4, DEC]), ALU.mult), sstep, nss)
                ng = K.vecs[:, 136 + 4 * g:140 + 4 * g].unsqueeze(2).to_broadcast([P, 4, DEC])
                link(v.tensor_tensor(S.ysT[:, 4 * g:4 * g + 4, :], ysum[:], ng, ALU.mult), sstep, nss)

                def heads(vec):
                    return vec.unsqueeze(2).to_broadcast([P, GH, HD])

                def front(c):
                    n = TT * g + c
                    dve.wait_ge(bcb_ps, n + 1)
                    if n >= 2:
                        dve.wait_ge(sp_ps, n - 1)
                    v.tensor_tensor(cbm[:, c % 2, :], ps[:, 0, 0:P], K.le[:], ALU.mult).then_inc(cb_done, 1)
                    v.tensor_copy(btok[:, c % 2, :], ps[:, 0, P:2 * P]).then_inc(cb_done, 1)
                    dve.wait_ge(xt_ps, n + 1)
                    dve.wait_ge(xt_done, n + 1)
                    if n >= 2:
                        dve.wait_ge(yd_ps, n - 1)
                    v.tensor_tensor(xdt[:, c % 2, :].rearrange("p (h d) -> p h d", d=HD),
                                    ps[:, 3, :].rearrange("p (h d) -> p h d", d=HD),
                                    heads(S.dt[:, c, GH * g:GH * g + GH]), ALU.mult).then_inc(xdt_done, 1)
                    dve.wait_ge(m_exp, n + 1)
                    dve.wait_ge(cb_done, 2 * n + 2)
                    v.tensor_tensor(m[:, c % 2], m[:, c % 2], cbm[:, c % 2, :].unsqueeze(1).to_broadcast([P, GH, P]),
                                    ALU.mult).then_inc(m_done, 1)

                def back(c):
                    n = TT * g + c
                    yc = y[:, c % 2, :]
                    yh = yc.rearrange("p (h d) -> p h d", d=HD)
                    dve.wait_ge(yd_ps, n + 1)
                    dve.wait_ge(xd_done, n + 1)
                    if n >= 2:
                        dve.wait_ge(yT_ps, n - 1)
                    v.tensor_tensor(yc, ps[:, 5, :], xd[:, c % 2, :], ALU.add).then_inc(yd_done, 2)
                    if c:
                        t = tmp[:, 0].rearrange("p k n -> p (k n)")
                        dve.wait_ge(yo_ps, n - g)
                        v.tensor_tensor(t.rearrange("p (h d) -> p h d", d=HD), ps[:, 4, :].rearrange("p (h d) -> p h d", d=HD),
                                        heads(S.e_acs[:, c, GH * g:GH * g + GH]), ALU.mult).then_inc(yo_done, 1)
                        dve.wait_ge(yo_done, n - g)
                        dve.wait_ge(yd_done, 2 * (n + 1))
                        link(v.tensor_tensor(yc, yc, t, ALU.add), ystep, ny)
                    else:
                        dve.wait_ge(yd_done, 2 * (n + 1))
                    v.tensor_tensor(yc, yc, z[:, c, :], ALU.mult).then_inc(ygated, 1)
                    dve.wait_ge(sp_ps, n + 1)
                    if c == 0:
                        if g:
                            dve.wait_ge(fin_ps, g)
                        v.tensor_copy(state[:], ps[:, 6, :]).then_inc(s_done, 1)
                    else:
                        sh = state[:].rearrange("p (h d) -> p h d", d=HD)
                        dve.wait_ge(s_done, n)
                        v.tensor_tensor(sh, sh, heads(S.c_dec[:, c, GH * g:GH * g + GH]), ALU.mult).then_inc(s_scaled, 1)
                        dve.wait_ge(s_scaled, n - g)
                        v.tensor_tensor(state[:], state[:], ps[:, 6, :], ALU.add).then_inc(s_done, 1)
                    i = c % 2
                    dve.wait_ge(ysquared, n + 1)
                    v.tensor_scalar(stat[:, 1, i:i + 1], stat[:, 0, i:i + 1], 1.0 / GW, EPS, ALU.mult, ALU.add).then_inc(ymean, 1)

                def scale(c):
                    n = TT * g + c
                    i = c % 2
                    dve.wait_ge(yroot2, n + 1)
                    link(v.reciprocal(stat[:, 3, i:i + 1], stat[:, 2, i:i + 1]), ystep, ny)
                    v.tensor_scalar(y[:, i, :], y[:, i, :], stat[:, 3, i:i + 1], None, ALU.mult).then_inc(ynormed, 1)

                front(0)
                for c in range(TT):
                    if c + 1 < TT:
                        front(c + 1)
                    back(c)
                    scale(c)


def second_slabs(A):
    slabs, span = [], {}

    def cols(w, k0, nk, c0, n):
        return w[0, P * k0:P * (k0 + nk), c0:c0 + n].rearrange("(k p) n -> p k n", p=P)

    def add(name, nk, *parts):
        span.setdefault(name, [len(slabs), 0])
        slabs.append((nk, parts))
        span[name][1] = len(slabs)

    for w, k0 in (("w_proj_ssm", 0), ("w_proj_ssm", KB), ("w_proj_attn", 0)):
        for i in range(4):
            add("merge", KB, (0, cols(A[w], k0, KB, 256 * i, 256)))
    for i in range(4):
        add("out", KB, (0, cols(A["w_out"], 0, KB, 256 * i, 256)))
    for f0, nf in ffn_parts():
        for f in range(f0, f0 + nf):
            add("ffn", KB, (0, cols(A["w_ffn_in"], 0, KB, P * f, P)), (P, cols(A["w_ffn_in"], 0, KB, FFN + P * f, P)))
        for h in range(2):
            add("ffn", nf, (0, cols(A["w_ffn_out"], f0, nf, 512 * h, 512)))
    return slabs, span


FPART = 4


def ffn_parts():
    return [(f, min(FPART, FB - f)) for f in range(0, FB, FPART)]


class SplitRing:

    def __init__(self, K, ctx, kept):
        nc = K.nc
        self.nc = nc
        self.slabs, self.span = second_slabs(K.A)
        self.raw = ctx.enter_context(nc.sbuf_tensor("w_raw", [P, 2, SLAB], F32))
        self.hi = ctx.enter_context(nc.sbuf_tensor("w_hi", [P, 2, SLAB], F32R))
        self.lo = ctx.enter_context(nc.sbuf_tensor("w_lo", [P, 2, SLAB], F32R))
        self.landed = [kept("raw_slab_landed0"), kept("raw_slab_landed1")]
        self.hi_done, self.split = kept("w_hi_done"), kept("w_split")

    def load(self, eng, n):
        if n >= len(self.slabs):
            return
        if n >= 2:
            eng.wait_ge(self.split, n - 1)
        nk, parts = self.slabs[n]
        for at, src in parts:
            dst = self.raw[:, n % 2, :].rearrange("p (k n) -> p k n", n=256 if nk == KB else 512)
            w = src.shape[2]
            eng.dma_start(dst[:, 0:nk, at:at + w], src).then_inc(self.landed[n % 2], 16)

    def load_stage(self, eng, stage):
        first, last = self.span[stage]
        for n in range(first + 3, last + 3):
            self.load(eng, n)

    def split_slab(self, pool, n, used=None):
        if n >= len(self.slabs):
            return
        pool.wait_ge(self.landed[n % 2], 16 * sum(len(self.slabs[m][1]) for m in range(n % 2, n + 1, 2)))
        if used:
            pool.wait_ge(*used)
        w = self.slabs[n][0] * (256 if self.slabs[n][0] == KB else 512)
        raw, hi, lo = (a[:, n % 2, 0:w] for a in (self.raw, self.hi, self.lo))
        self.nc.gpsimd.tensor_copy(hi, raw).then_inc(self.hi_done, 1)
        pool.wait_ge(self.hi_done, n + 1)
        self.nc.gpsimd.tensor_tensor(lo, raw, hi.bitcast(F32), ALU.subtract).then_inc(self.split, 1)

    def split_stage(self, pool, stage, used):
        first, last = self.span[stage]
        for n in range(first + 1, last + 1):
            self.split_slab(pool, n, used(n - 2 - first) if n - 2 >= first else None)

    def pair(self, n):
        nw = 256 if self.slabs[n][0] == KB else 512
        return [a[:, n % 2, :].rearrange("p (k n) -> p k n", n=nw) for a in (self.hi, self.lo)]


def product(nc, out, terms):
    for i, (ah, al, bh, bl) in enumerate(terms):
        nc.tensor.matmul(out, ah, bl, start=(i == 0), stop=False)
        nc.tensor.matmul(out, ah, bh, start=False, stop=False)
        mm = nc.tensor.matmul(out, al, bh, start=False, stop=(i == len(terms) - 1))
    return mm


def merge(K, W, merged):
    nc, A, ps = K.nc, K.A, K.ps
    first = W.span["merge"][0]
    PU = KB * TC
    NU = 3 * PU
    with ExitStack() as ctx:
        def sb(name, shape, dt=F32):
            return ctx.enter_context(nc.sbuf_tensor(name, shape, dt))
        raw = sb("m_raw", [P, 2, KB, CW])
        hi, lo = sb("m_hi", [P, 4, KB, CW], F32R), sb("m_lo", [P, 4, KB, CW], F32R)
        sig = sb("m_sig", [P, 2, NT])
        part = sb("m_part", [P, 2, CW])
        raw_in, sig_in = [K.sem(f"m_raw_in{i}") for i in range(2)], [K.sem(f"m_sig_in{i}") for i in range(2)]
        hi_done, split = K.sem("m_hi_done"), K.sem("m_split")
        gemm, freed, done = K.sem("m_sums"), K.sem("m_bank_free"), K.sem("m_done")
        block = ctx.enter_context(nc.Block())

        def sample_parts(q):
            return 2 if q % TC == TC - 1 and q // TC < 2 else 1

        @block.sync
        def _(sp):
            for n in range(3):
                W.load(sp, n)
            W.load_stage(sp, "merge")

        @block.gpsimd
        def _(pool):
            W.split_slab(pool, first)
            W.split_stage(pool, "merge", lambda i: (gemm, 2 * TC * (i + 1)))

        @block.scalar
        def _(act):
            def load(q):
                s, c = q // TC, q % TC
                if q >= 2:
                    act.wait_ge(split, q - 1)
                w = CW - (DEC if sample_parts(q) == 2 else 0)
                src = A["s_ssm"][KB * s:KB * s + KB] if s < 2 else A["s_att"]
                act.dma_start(raw[:, q % 2, :, 0:w], src.rearrange("k p n -> p k n")[:, :, CW * c:CW * c + w])\
                    .then_inc(raw_in[q % 2], 16)
                if w < CW:
                    act.dma_start(raw[:, q % 2, :, w:CW], K.ysT[:, KB * s:KB * s + KB, :]).then_inc(raw_in[q % 2], 16)

            def round_chunk(q):
                act.wait_ge(raw_in[q % 2], 16 * sum(sample_parts(m) for m in range(q % 2, q + 1, 2)))
                nc.scalar.copy(hi[:, q % 4].rearrange("p k n -> p (k n)"),
                               raw[:, q % 2].rearrange("p k n -> p (k n)")).then_inc(hi_done, 1)
                if q + 2 < 3 * TC:
                    load(q + 2)

            def load_sig(b):
                act.dma_start(sig[:, b % 2, :], A["s_sig"][b]).then_inc(sig_in[b % 2], 16)

            load(0)
            load(1)
            load_sig(0)
            load_sig(1)
            for q in range(4):
                round_chunk(q)
            for u in range(NU):
                s, b, c = u // PU, u // TC % KB, u % TC
                if b == KB - 1 and TC * s + c + 4 < 3 * TC:
                    act.wait_ge(gemm, u + 1)
                    round_chunk(TC * s + c + 4)
                if s and c == TC - 1 and KB * (s - 1) + b + 2 < 2 * KB:
                    act.wait_ge(done, u + 1 - PU)
                    load_sig(KB * (s - 1) + b + 2)

        @block.tensor
        def _(pe):
            for u in range(NU):
                s, b, c = u // PU, u // TC % KB, u % TC
                n, q = first + u // (2 * TC), TC * s + c
                if u % (2 * TC) == 0:
                    pe.wait_ge(W.split, n + 1)
                if b == 0:
                    pe.wait_ge(split, q + 1)
                if u >= 8:
                    pe.wait_ge(freed, u - 7)
                wh, wl = W.pair(n)
                cols = slice(P * (b % 2), P * (b % 2) + P)
                product(nc, ps[:, u % 8, 0:CW], [(wh[:, k, cols], wl[:, k, cols], hi[:, q % 4, k, :], lo[:, q % 4, k, :])
                                                 for k in range(KB)]).then_inc(gemm, 1)

        @block.vector
        def _(dve):
            v = nc.vector

            def rest(q):
                dve.wait_ge(hi_done, q + 1)
                flat = "p k n -> p (k n)"
                v.tensor_tensor(lo[:, q % 4].rearrange(flat), raw[:, q % 2].rearrange(flat),
                                hi[:, q % 4].rearrange(flat).bitcast(F32), ALU.subtract).then_inc(split, 1)

            for q in range(4):
                rest(q)
            for u in range(NU):
                s, b, c = u // PU, u // TC % KB, u % TC
                if u and (u - 1) // TC % KB == KB - 1:
                    q = TC * ((u - 1) // PU) + (u - 1) % TC + 4
                    if q < 3 * TC:
                        rest(q)
                cols = slice(CW * c, CW * c + CW)
                bank, to = ps[:, u % 8, 0:CW], merged[:, b, cols]
                dve.wait_ge(gemm, u + 1)
                if s == 0:
                    v.tensor_copy(to, bank).then_inc(freed, 1)
                    dve.wait_ge(freed, u + 1)
                    continue
                if c == 0:
                    dve.wait_ge(sig_in[b % 2], 16 * ((KB * (s - 1) + b) // 2 + 1))
                first_op, second_op = (ALU.add, ALU.mult) if s == 1 else (ALU.mult, ALU.add)
                other = sig[:, b % 2, cols]
                v.tensor_tensor(part[:, u % 2, :], bank, to if s == 1 else other, first_op).then_inc(freed, 1)
                dve.wait_ge(freed, u + 1)
                v.tensor_tensor(to, part[:, u % 2, :], other if s == 1 else to, second_op).then_inc(done, 1)


def project_out(K, W, merged, source):
    nc, A, ps = K.nc, K.A, K.ps
    first = W.span["out"][0]
    with ExitStack() as ctx:
        def sb(name, shape, dt=F32):
            return ctx.enter_context(nc.sbuf_tensor(name, shape, dt))
        hi, lo = sb("o_hi", [P, KB, NT], F32R), sb("o_lo", [P, KB, NT], F32R)
        x = sb("o_x", [P, 9, D])
        gate = sb("o_gate", [P, 2, D])
        part = sb("o_part", [P, 2, 256])
        x_in, gate_in, gemm = K.sem("o_x_in"), K.sem("o_gate_in"), K.sem("o_sums")
        hi_done, split = K.sem("o_hi_done"), K.sem("o_split")
        part_done, added, out = K.sem("o_part_done"), K.sem("o_added"), K.sem("o_stored")
        block = ctx.enter_context(nc.Block())

        def token_cols(t):
            return slice(P * t, P * t + rows_of(t))

        @block.sync
        def _(sp):
            for b in range(2):
                r = P if b == 0 else DEC
                sp.dma_start(gate[0:r, b, :], A["s_gates"][b, 0:r, :]).then_inc(gate_in, 16)
            for t in range(9):
                sp.dma_start(x[0:rows_of(t), t, :], source(t)).then_inc(x_in, 16)
            W.load_stage(sp, "out")

        @block.gpsimd
        def _(pool):
            W.split_stage(pool, "out", lambda i: (gemm, 9 * (i + 1)))

        @block.scalar
        def _(act):
            for t in range(9):
                nc.scalar.copy(hi[:, :, token_cols(t)], merged[:, :, token_cols(t)]).then_inc(hi_done, 1)
            for t in range(9):
                act.wait_ge(added, 27 + t + 1)
                act.dma_start(A["s_x1"][P * t:P * t + rows_of(t), :], x[0:rows_of(t), t, :]).then_inc(out, 16)
            act.wait_ge(out, 16 * 9)

        @block.tensor
        def _(pe):
            for s in range(4):
                wh, wl = W.pair(first + s)
                pe.wait_ge(W.split, first + s + 1)
                for t in range(9):
                    u, cols = 9 * s + t, token_cols(t)
                    if s == 0:
                        pe.wait_ge(split, t + 1)
                    if u >= 8:
                        pe.wait_ge(part_done, u - 7)
                    product(nc, ps[0:rows_of(t), u % 8, 0:256], [(hi[:, k, cols], lo[:, k, cols], wh[:, k, :], wl[:, k, :])
                                                                 for k in range(KB)]).then_inc(gemm, 1)

        @block.vector
        def _(dve):
            v = nc.vector

            def rest(t):
                cols = token_cols(t)
                dve.wait_ge(hi_done, t + 1)
                v.tensor_tensor(lo[:, :, cols], merged[:, :, cols], hi[:, :, cols].bitcast(F32), ALU.subtract).then_inc(split, 1)

            rest(0)
            rest(1)
            dve.wait_ge(gate_in, 32)
            dve.wait_ge(x_in, 16 * 9)
            for s in range(4):
                for t in range(9):
                    r, u = rows_of(t), 9 * s + t
                    cols = slice(256 * s, 256 * s + 256)
                    if s == 0 and t + 2 < 9:
                        rest(t + 2)
                    dve.wait_ge(gemm, u + 1)
                    v.tensor_tensor(part[0:r, u % 2, :], ps[0:r, u % 8, 0:256], gate[0:r, t // TT, cols], ALU.mult)\
                        .then_inc(part_done, 1)
                    dve.wait_ge(part_done, u + 1)
                    v.tensor_tensor(x[0:r, t, cols], x[0:r, t, cols], part[0:r, u % 2, :], ALU.add).then_inc(added, 1)


def second_norm(K, W, x, hi, lo):
    nc, A, ps = K.nc, K.A, K.ps
    shift, scale = K.modT[:, 2, :, :], K.modT[:, 3, :, :]
    with ExitStack() as ctx:
        def sb(name, shape):
            return ctx.enter_context(nc.sbuf_tensor("n2" + name, shape, F32))
        xn = sb("xn", [P, 2, D])
        full = sb("full", [P, 2, KB, P])
        sq = sb("sq", [P, D])
        stat = sb("stat", [P, 4, 9])
        x_in, x_in_s = K.sem("n2x_in"), K.sem("n2x_in_odd")
        squared, mean, root, inv = K.sem("n2squared"), K.sem("n2mean"), K.sem("n2root"), K.sem("n2inv")
        scaled, turned, moved = K.sem("n2scaled"), K.sem("n2turned"), K.sem("n2moved")
        hi_done, split, extra = K.sem("n2hi"), K.sem("n2split"), K.sem("n2sample_step")
        x_ins = [x_in, x_in_s]
        block = ctx.enter_context(nc.Block())

        @block.sync
        def _(sp):
            for t in range(9):
                if t >= 2:
                    sp.wait_ge(squared, t - 1)
                sp.dma_start(x[0:rows_of(t), t, :], A["s_x1"][P * t:P * t + rows_of(t), :]).then_inc(x_ins[t % 2], 16)

        @block.scalar
        def _(act):
            def square(t):
                r = rows_of(t)
                act.wait_ge(x_ins[t % 2], 16 * (t // 2 + 1))
                if t:
                    act.wait_ge(squared, t)
                nc.scalar.activation(sq[0:r, :], x[0:r, t, :], ACT.Square,
                                     accum_out=stat[0:r, 0, t:t + 1]).then_inc(squared, 1)
                act.wait_ge(mean, t + 1)
                nc.scalar.activation(stat[0:r, 2, t:t + 1], stat[0:r, 1, t:t + 1], ACT.Sqrt).then_inc(root, 1)

            square(0)
            for t in range(TT):
                square(t + 1)
                if t >= 2:
                    act.wait_ge(split, t - 1)
                for h in range(2):
                    act.wait_ge(turned, 2 * t + h + 1)
                    for j in range(4):
                        k = 4 * h + j
                        mv = nc.scalar.activation(full[:, t % 2, k, :], ps[:, 2 * (t % 2) + h, P * j:P * j + P],
                                                  ACT.Identity, bias=shift[:, k, 0:1], scale=scale[:, k, 0:1])
                    mv.then_inc(moved, 1)

        @block.vector
        def _(dve):
            v = nc.vector

            def divide(t):
                r = rows_of(t)
                dve.wait_ge(squared, t + 1)
                v.tensor_scalar(stat[0:r, 1, t:t + 1], stat[0:r, 0, t:t + 1], 1.0 / D, EPS, ALU.mult, ALU.add).then_inc(mean, 1)
                dve.wait_ge(root, t + 1)
                v.reciprocal(stat[0:r, 3, t:t + 1], stat[0:r, 2, t:t + 1]).then_inc(inv, 1)
                dve.wait_ge(inv, t + 1)
                if t >= 2:
                    dve.wait_ge(turned, 2 * (t - 1))
                v.tensor_scalar(xn[0:r, t % 2, :], x[0:r, t, :], stat[0:r, 3, t:t + 1], None, ALU.mult).then_inc(scaled, 1)

            def part(t):
                cols = slice(P * t, P * t + P)
                dve.wait_ge(moved, 2 * t + 2)
                v.tensor_copy(hi[:, :, cols], full[:, t % 2]).then_inc(hi_done, 1)
                dve.wait_ge(hi_done, t + 1)
                v.tensor_tensor(lo[:, :, cols], full[:, t % 2], hi[:, :, cols].bitcast(F32), ALU.subtract).then_inc(split, 1)

            divide(0)
            divide(1)
            for t in range(2, 9):
                divide(t)
                part(t - 2)
            part(TT - 1)
            dve.wait_ge(turned, 2 * TT + 1)
            dve.wait_ge(split, TT - 1)
            hs, cols = full[:, 0, :, 0:DEC], slice(SEQ, NT)
            v.tensor_tensor(hs, ps[:, 4, 0:64].rearrange("p (k s) -> p k s", k=KB), scale[:, :, 1:9], ALU.mult).then_inc(extra, 1)
            dve.wait_ge(extra, 1)
            v.tensor_tensor(hs, hs, shift[:, :, 1:9], ALU.add).then_inc(extra, 1)
            dve.wait_ge(extra, 2)
            v.tensor_copy(hi[:, :, cols], hs).then_inc(extra, 1)
            dve.wait_ge(extra, 3)
            v.tensor_tensor(lo[:, :, cols], hs, hi[:, :, cols].bitcast(F32), ALU.subtract)

        @block.tensor
        def _(pe):
            for t in range(9):
                pe.wait_ge(scaled, t + 1)
                if t == TT:
                    for k in range(KB):
                        mm = nc.tensor.transpose(ps[:, 4, 8 * k:8 * k + 8], xn[0:DEC, t % 2, P * k:P * k + P],
                                                 K.ident[0:DEC, 0:DEC])
                    mm.then_inc(turned, 1)
                    break
                for h in range(2):
                    if t >= 2:
                        pe.wait_ge(moved, 2 * (t - 2) + h + 1)
                    for j in range(4):
                        k = 4 * h + j
                        mm = nc.tensor.transpose(ps[:, 2 * (t % 2) + h, P * j:P * j + P],
                                                 xn[:, t % 2, P * k:P * k + P], K.ident[:])
                    mm.then_inc(turned, 1)


def ffn(K, W, x, h_hi, h_lo):
    nc, A, ps = K.nc, K.A, K.ps
    first = W.span["ffn"][0]
    parts = ffn_parts()
    with ExitStack() as ctx:
        def sb(name, shape, dt=F32):
            return ctx.enter_context(nc.sbuf_tensor(name, shape, dt))
        a_hi, a_lo = sb("a_hi", [P, FPART, NT], F32R), sb("a_lo", [P, FPART, NT], F32R)
        silu, prod = sb("f_silu", [P, 2, CW]), sb("f_prod", [P, 2, CW])
        gate = sb("f_gate", [P, 2, D])
        fg = sb("final_g", [P, D])
        scaled = sb("f_scaled", [P, 2, 512])
        stat = sb("f_stat", [P, 4, 9])
        gate_in, g_in = K.sem("gate2_in"), K.sem("final_g_in")
        up, silu_done, act_done = K.sem("hidden_sums"), K.sem("silu_done"), K.sem("hidden_done")
        hi_done, split = K.sem("hidden_hi"), K.sem("hidden_split")
        down, free, added = K.sem("down_sums"), K.sem("down_bank_free"), K.sem("down_added")
        squared, mean, root, inv, done = (K.sem(n) for n in ("squared2", "mean2", "root2", "inv2", "y_done"))
        out = K.store_sem("y_stored")
        block = ctx.enter_context(nc.Block())

        @block.sync
        def _(sp):
            for b in range(2):
                r = P if b == 0 else DEC
                sp.dma_start(gate[0:r, b, :], A["s_gates"][2 + b, 0:r, :]).then_inc(gate_in, 16)
            sp.dma_start(fg[:], A["final_g"].partition_broadcast(P)).then_inc(g_in, 16)
            W.load_stage(sp, "ffn")
            for t in range(9):
                sp.wait_ge(done, t + 1)
                dst = A["y_prompt"][0, P * t:P * t + P, :] if t < TT else A["y_sample"][:, 0, :]
                sp.dma_start(dst, x[0:rows_of(t), t, :]).then_inc(out, 16)
            sp.wait_ge(out, 16 * 9)

        @block.gpsimd
        def _(pool):
            used, ups, downs = [], 0, 0
            for f0, nf in parts:
                used += [(up, ups + TC * (f + 1)) for f in range(nf)] + [(down, downs + 9), (down, downs + 18)]
                ups, downs = ups + TC * nf, downs + 18
            W.split_stage(pool, "ffn", used.__getitem__)

        @block.tensor
        def _(pe):
            n, i, d = first, 0, 0
            for f0, nf in parts:
                for f in range(nf):
                    pe.wait_ge(W.split, n + 1)
                    wh, wl = W.pair(n)
                    for c in range(TC):
                        cols = slice(CW * c, CW * c + CW)
                        if i >= 3:
                            pe.wait_ge(act_done, i - 2)
                        for h in range(2):
                            w = slice(P * h, P * h + P)
                            mm = product(nc, ps[:, 2 * (i % 3) + h, 0:CW], [
                                (wh[:, k, w], wl[:, k, w], h_hi[:, k, cols], h_lo[:, k, cols]) for k in range(KB)])
                        mm.then_inc(up, 1)
                        i += 1
                    n += 1
                for h in range(2):
                    pe.wait_ge(W.split, n + 1)
                    wh, wl = W.pair(n)
                    for t in range(9):
                        r, cols = rows_of(t), slice(P * t, P * t + rows_of(t))
                        if h == 0 and t in (0, 2, 5):
                            pe.wait_ge(split, i - TC + {0: 1, 2: 2, 5: 3}[t])
                        if d >= 2:
                            pe.wait_ge(free, d - 1)
                        product(nc, ps[0:r, 6 + d % 2, :], [
                            (a_hi[:, k, cols], a_lo[:, k, cols], wh[:, k, :], wl[:, k, :]) for k in range(nf)]).then_inc(down, 1)
                        d += 1
                    n += 1

        @block.scalar
        def _(act):
            for i in range(TC * FB):
                act.wait_ge(up, i + 1)
                if i >= 2:
                    act.wait_ge(act_done, i - 1)
                nc.scalar.activation(silu[:, i % 2, :], ps[:, 2 * (i % 3), 0:CW], ACT.Silu).then_inc(silu_done, 1)
            for t in range(9):
                r = rows_of(t)
                act.wait_ge(added, 18 * len(parts) - 9 + t + 1)
                if t:
                    act.wait_ge(squared, t)
                nc.scalar.activation(ps[0:r, 4:6, :].rearrange("p a n -> p (a n)"), x[0:r, t, :], ACT.Square,
                                     accum_out=stat[0:r, 0, t:t + 1]).then_inc(squared, 1)
                act.wait_ge(mean, t + 1)
                nc.scalar.activation(stat[0:r, 2, t:t + 1], stat[0:r, 1, t:t + 1], ACT.Sqrt).then_inc(root, 1)

        @block.vector
        def _(dve):
            v = nc.vector

            def final(t):
                r = rows_of(t)
                dve.wait_ge(squared, t + 1)
                v.tensor_scalar(stat[0:r, 1, t:t + 1], stat[0:r, 0, t:t + 1], 1.0 / D, EPS, ALU.mult, ALU.add).then_inc(mean, 1)
                dve.wait_ge(root, t + 1)
                v.reciprocal(stat[0:r, 3, t:t + 1], stat[0:r, 2, t:t + 1]).then_inc(inv, 1)
                dve.wait_ge(inv, t + 1)
                v.scalar_tensor_tensor(x[0:r, t, :], x[0:r, t, :], stat[0:r, 3, t:t + 1], fg[0:r, :],
                                       ALU.mult, ALU.mult).then_inc(done, 1)

            dve.wait_ge(gate_in, 32)
            dve.wait_ge(g_in, 16)
            i = d = 0
            for f0, nf in parts:
                for f in range(nf):
                    for c in range(TC):
                        cols = slice(CW * c, CW * c + CW)
                        dve.wait_ge(silu_done, i + 1)
                        v.tensor_tensor(prod[:, i % 2, :], ps[:, 2 * (i % 3) + 1, 0:CW], silu[:, i % 2, :], ALU.mult).then_inc(act_done, 1)
                        dve.wait_ge(act_done, i + 1)
                        if f0 and f == 0 and c == 0:
                            dve.wait_ge(down, d)
                        v.tensor_copy(a_hi[:, f, cols], prod[:, i % 2, :]).then_inc(hi_done, 1)
                        dve.wait_ge(hi_done, i + 1)
                        v.tensor_tensor(a_lo[:, f, cols], prod[:, i % 2, :], a_hi[:, f, cols].bitcast(F32), ALU.subtract).then_inc(split, 1)
                        i += 1
                last = f0 + nf == FB
                for h in range(2):
                    for t in range(9):
                        r, cols = rows_of(t), slice(512 * h, 512 * h + 512)
                        dve.wait_ge(down, d + 1)
                        v.tensor_tensor(scaled[0:r, d % 2, :], ps[0:r, 6 + d % 2, :], gate[0:r, t // TT, cols], ALU.mult).then_inc(free, 1)
                        dve.wait_ge(free, d + 1)
                        if d >= 9:
                            dve.wait_ge(added, d - 8)
                        v.tensor_tensor(x[0:r, t, cols], x[0:r, t, cols], scaled[0:r, d % 2, :], ALU.add).then_inc(added, 1)
                        d += 1
                        if last and h and t:
                            final(t - 1)
            final(8)


def program(nc, A):
    K = Chip()
    K.nc, K.A = nc, A
    K.slabs, K.span = weight_slabs(A)
    A["s_sig"] = nc.dram_tensor("s_sig", (2 * KB, P, NT), F32, kind="Internal").ap()
    A["s_att"] = nc.dram_tensor("s_att", (KB, P, NT), F32, kind="Internal").ap()
    A["s_ssm"] = nc.dram_tensor("s_ssm", (2 * KB, P, SEQ), F32, kind="Internal").ap()
    A["s_x1"] = nc.dram_tensor("s_x1", (NT, D), F32, kind="Internal").ap()
    A["s_gates"] = nc.dram_tensor("s_gates", (4, P, D), F32, kind="Internal").ap()
    with ExitStack() as ctx:
        def sb(name, shape, into=None):
            return (into or ctx).enter_context(nc.sbuf_tensor(name, shape, F32))
        K.lent = []
        kept = lambda name: ctx.enter_context(nc.semaphore(name))

        def lend(name):
            K.lent.append(nc.alloc_semaphore(name=name))
            return K.lent[-1]

        def retire():
            with nc.Block() as block:
                @block.sync
                def _(sp):
                    for s in K.lent:
                        sp.sem_clear(s)
            for s in reversed(K.lent):
                nc.release_semaphore(s)
            K.lent = []

        K.sem = lend
        stores = {n: kept(n) for n in (
            "ki_stored", "k_stored", "v_stored", "tail_rows_stored", "states_stored", "final_stored",
            "old_conv_rows_stored", "y_stored", "gate_out0", "gate_out1", "conv_state_in", "states_in",
            "ssm_yT_stored0", "ssm_yT_stored1")}
        K.store_sem = stores.__getitem__
        K.ps = ctx.enter_context(nc.psum_tensor("ps", [P, 8, 512], F32))
        K.landed = [kept(f"slab_landed{i}") for i in range(RING)]
        K.ident_in, K.const_in = kept("ident_in"), kept("const_in")
        K.ident = sb("ident", [P, P])
        K.vecs = sb("vecs", [P, 152])
        K.modT = sb("modT", [P, 4, KB, 9])
        K.ysT = sb("ysT", [P, INNER // P, DEC])
        xp, xs = A["x_prompt"][0], A["x_sample"][:, 0]

        def x_tile(t):
            return xp[P * t:P * t + P, :] if t < TT else xs

        with ExitStack() as first:
            K.ring = sb("ring", [P, RING, SLAB], first)
            K.le, K.gt, K.ones, K.diag_off = (sb(n, [P, P], first) for n in ("le", "gt", "ones", "diag_off"))
            K.cos, K.sin = sb("cos", [P, TT + 1, HD], first), sb("sin", [P, TT + 1, HD], first)
            K.heads_row, K.heads_col = sb("heads_row", [P, 3, HEADS], first), sb("heads_col", [HEADS, 3], first)
            K.dt_raw, K.dtT_raw = sb("dt_raw", [P, TT, HEADS], first), sb("dtT_raw", [HEADS, DEC], first)
            modulation(K)
            hT = sb("hT", [P, KB, NT], first)
            norm_stage(K, "n1", 0, hT, x_tile)
            with ExitStack() as att:
                T = Chip()
                T.qT = sb("qT", [P, KB, NT], att)
                T.v = sb("v", [P, TT + 1, KVH * HD], att)
                T.wi = sb("wi", [P, TT + 1, IH], att)
                T.q_s, T.k_s = sb("q_s", [DEC, D], att), sb("k_s", [DEC, KVH * HD], att)
                T.qi_s, T.ki_s = sb("qi_s", [DEC, IH * HD], att), sb("ki_s", [DEC, HD], att)
                T.dt_raw, T.dtT_raw = K.dt_raw, K.dtT_raw
                with ExitStack() as keys:
                    T.kT, T.kiT = sb("kT", [P, KVH, SEQ], keys), sb("kiT", [P, SEQ], keys)
                    T.qiT = sb("qiT", [P, 2, SEQ], keys)
                    T.bias = keys.enter_context(nc.sbuf_tensor("sel_bias", [P, BIAS_AT[TT]], BF16))
                    project(K, hT, T)
                    select(K, hT, T)
                    attend(K, T)
                attend_samples(K, T)
            retire()
            with ExitStack() as rec:
                S = Chip()
                S.dt, S.dta, S.ddt, S.e_acs, S.c_dec = (sb("s_" + n, [P, TT, HEADS], rec) for n in ("dt", "dta", "ddt", "e", "c"))
                S.hx = sb("s_hx", [P, INNER // P, 17], rec)
                S.ysT = K.ysT
                steps(K, S)
                ssm(K, hT, S)
            retire()
        with ExitStack() as second:
            W = SplitRing(K, second, lambda name: second.enter_context(nc.semaphore(name)))
            with ExitStack() as mix:
                merged = sb("merged", [P, KB, NT], mix)
                merge(K, W, merged)
                project_out(K, W, merged, x_tile)
            with ExitStack() as mlp:
                x1 = sb("x1", [P, 9, D], mlp)
                h_hi, h_lo = (mlp.enter_context(nc.sbuf_tensor(n, [P, KB, NT], F32R)) for n in ("h_hi", "h_lo"))
                second_norm(K, W, x1, h_hi, h_lo)
                ffn(K, W, x1, h_hi, h_lo)


_INS = ["x_prompt", "x_sample", "cache_k", "cache_v", "cache_kidx", "state_conv", "state_ssm", "page_table",
        "c_prompt", "c_sample", "w_ada", "b_ada", "norm1_g", "w_in", "conv_w", "conv_b", "dt_bias", "a_log",
        "d_skip", "ssm_norm_g", "w_proj_ssm", "w_proj_attn", "w_out", "norm2_g", "w_ffn_in", "w_ffn_out", "final_g"]
_OUTS = [("y_prompt", (1, SEQ, D)), ("y_sample", (DEC, 1, D)),
         ("k_prompt", (1, 1, SEQ, KVH, HD)), ("v_prompt", (1, 1, SEQ, KVH, HD)), ("kidx_prompt", (1, 1, SEQ, HD)),
         ("conv_prompt", (1, 1, CONV - 1, XBC)), ("ssm_prompt", (1, 1, HEADS, HD, NST)),
         ("k_sample", (1, DEC, 1, KVH, HD)), ("v_sample", (1, DEC, 1, KVH, HD)), ("kidx_sample", (1, DEC, 1, HD)),
         ("conv_sample", (1, DEC, CONV - 1, XBC)), ("ssm_sample", (1, DEC, HEADS, HD, NST))]


def shape_constants():
    import numpy as np
    i = np.arange(P)
    f = np.float32
    half = HD // 2
    inv = f(10000.0) ** (-np.arange(half, dtype=f) / f(half))
    pos = np.concatenate([np.arange(SEQ), np.full(P, PAST)]).astype(f)
    ang = (pos[:, None] * inv[None, :]).astype(f)
    cos, sin = np.cos(ang).astype(f), np.sin(ang).astype(f)
    tiled = lambda a: np.ascontiguousarray(a.reshape(TT + 1, P, HD).transpose(1, 0, 2))
    return {
        "k_ident": np.eye(P, dtype=f),
        "k_le": (i[:, None] <= i[None, :]).astype(f),
        "k_gt": (i[:, None] > i[None, :]).astype(f),
        "k_ones": np.ones((P, P), f),
        "k_diag_off": np.where(i[None, :] <= i[:, None], f(0), f(OFF)).astype(f),
        "k_diag_far": np.where(i[None, :] <= i[:, None], f(0), f(FAR)).astype(f),
        "k_cos": tiled(np.concatenate([cos, cos], 1)),
        "k_sin": tiled(np.concatenate([-sin, sin], 1)),
        "k_head": (np.arange(HEADS)[:, None] == np.arange(INNER)[None, :] // HD).astype(f),
        "k_who": (np.arange(DEC)[:, None] == i[None, :] // AH).astype(f),
    }


def kernel(**inputs):
    import numpy as _np
    import concourse.bacc as _bacc
    from concourse import mybir as _mybir
    from concourse.bass_utils import run_bass_kernel_spmd as _run

    nc = _bacc.Bacc("TRN2", target_bir_lowering=False, num_devices=1)
    arrays, A = {}, {}
    given = {n: _np.ascontiguousarray(inputs[n]) for n in _INS}
    given.update(shape_constants())
    for name, a in given.items():
        arrays[f"in_{name}"] = a
        A[name] = nc.dram_tensor(f"in_{name}", a.shape, _mybir.dt.from_np(a.dtype), kind="ExternalInput").ap()
    for name, shape in _OUTS:
        A[name] = nc.dram_tensor(f"out_{name}", shape, F32, kind="ExternalOutput").ap()
    program(nc, A)
    r = _run(nc, [arrays], core_ids=[0])
    return tuple(r.results[0][f"out_{name}"] for name, _ in _OUTS)
```

```python
from contextlib import ExitStack

import concourse.bass as bass
from concourse import mybir

F32 = mybir.dt.float32
F32R = mybir.dt.float32r
I32 = mybir.dt.int32
BF16 = mybir.dt.bfloat16
ALU = mybir.AluOpType
ACT = mybir.ActivationFunctionType
AX = mybir.AxisListType

P = 128
D = 1024
SEQ, DEC = 1024, 8
NT = SEQ + DEC
TT = SEQ // P
KB = D // P
TC, CW = 3, NT // 3
EPS = 1e-6
INNER, HEADS, HD, GROUPS, NST, CONV = 2048, 32, 64, 4, 128, 4
GW = INNER // GROUPS
GH = HEADS // GROUPS
XBC = INNER + 2 * GROUPS * NST
AH, KVH = 16, 4
IH = 4
PAST, PAGE = 256, 128
NPAGE = PAST // PAGE
SKEYS = PAST + 1
TOPK = min(256, SEQ // 4)
STOPK = min(256, SKEYS // 4)
FFN = 2816
FB = FFN // P
C_Z, C_X, C_B, C_C, C_DT = 0, 2048, 4096, 4608, 5120
C_Q, C_K, C_V, C_QI, C_KI, C_WI, C_GS, C_GA = 5152, 6176, 6432, 6688, 6944, 7008, 7012, 8036
IDX_SCALE = IH ** -0.5 * HD ** -0.5
ATT_SCALE = HD ** -0.5
FAR = -3.0e38
OFF = -1.0e30
SLAB = 2048
ADA_FIRST = 8
RING = 3


def rows_of(t):
    return P if t < TT else DEC


class Chip:
    pass


def weight_slabs(A):
    slabs, span = [], {}

    def cols(w, c0, n):
        return w[0, :, c0:c0 + n].rearrange("(k p) n -> p k n", p=P)

    def k8(at, n=256):
        return lambda s: s.rearrange("p (k n) -> p k n", k=KB)[:, :, at:at + n]

    def add(name, *parts):
        span.setdefault(name, [len(slabs), 0])
        slabs.append(list(parts))
        span[name][1] = len(slabs)

    for i in range(ADA_FIRST):
        add("ada", (k8(0), cols(A["w_ada"], 256 * i, 256)))
    add("qkv", (k8(0, 32), cols(A["w_in"], C_DT, 32)), (k8(32, 68), cols(A["w_in"], C_KI, 68)))
    add("qkv", (k8(0), cols(A["w_in"], C_QI, 256)))
    add("qkv", (k8(0), cols(A["w_in"], C_K, 256)))
    add("qkv", (k8(0), cols(A["w_in"], C_V, 256)))
    for i in range(4):
        add("qkv", (k8(0), cols(A["w_in"], C_Q + 256 * i, 256)))
    for i in range(8):
        add("gates", (k8(0), cols(A["w_in"], (C_GS, C_GA)[i // 4] + 256 * (i % 4), 256)))
        for j in range(2):
            add("gates", (k8(0), cols(A["w_ada"], 256 * (ADA_FIRST + 2 * i + j), 256)))
    for g in range(GROUPS):
        n = f"g{g}" if g else "gates"
        for i in range(2):
            add(n, (k8(0), cols(A["w_in"], C_X + GW * g + 256 * i, 256)))
        add(n, (k8(0, P), cols(A["w_in"], C_B + P * g, P)), (k8(P, P), cols(A["w_in"], C_C + P * g, P)))
        n = f"g{g}"
        for i in range(2):
            add(n, (k8(0), cols(A["w_in"], C_Z + GW * g + 256 * i, 256)))
    return slabs, span


def ring_landed(K, n):
    return K.landed[n % RING], 16 * sum(len(K.slabs[m]) for m in range(n % RING, n + 1, RING))


def ring_load(K, eng, stage, used):
    first, last = K.span[stage]
    for n in range(first + RING, min(last + RING, len(K.slabs))):
        eng.wait_ge(*used(n - RING - first))
        for place, src in K.slabs[n]:
            eng.dma_start(place(K.ring[:, n % RING, :]), src).then_inc(K.landed[n % RING], 16)


def slab_of(K, n, k=KB):
    return K.ring[:, n % RING, :].rearrange("p (k n) -> p k n", k=k)


def modulation(K):
    nc, A, ps = K.nc, K.A, K.ps
    first, last = K.span["ada"]
    with ExitStack() as ctx:
        def sb(name, shape):
            return ctx.enter_context(nc.sbuf_tensor(name, shape, F32))
        c_rows = sb("c_rows", [9, D])
        c_silu = sb("c_silu", [9, D])
        cT = K.cT
        mod = sb("mod", [9, 2 * D])
        vec_rows = sb("vec_rows", [P, 2, P])
        c_in, vec_in, mod_b = K.sem("c_in"), K.sem("vec_in"), K.sem("mod_bias_in")
        silu_done, cT_ps, cT_done = K.sem("c_silu_done"), K.sem("cT_in_psum"), K.sem("cT_done")
        vec_ps = K.sem("vec_in_psum")
        prod, summed = K.sem("mod_product"), K.sem("mod_summed")
        modT_ps, modT_done = K.sem("modT_in_psum"), K.sem("modT_done")
        step = K.sem("mod_vector_step")
        block = ctx.enter_context(nc.Block())

        @block.sync
        def _(sp):
            sp.dma_start(c_rows[0:1, :], A["c_prompt"]).then_inc(c_in, 16)
            sp.dma_start(c_rows[1:9, :], A["c_sample"]).then_inc(c_in, 16)
            sp.dma_start(K.ident[:], A["k_ident"]).then_inc(K.ident_in, 16)
            for n in range(RING):
                for place, src in K.slabs[n]:
                    sp.dma_start(place(K.ring[:, n, :]), src).then_inc(K.landed[n], 16)
            sp.dma_start(mod[:, :], A["b_ada"][0, 0:2 * D].partition_broadcast(9)).then_inc(mod_b, 16)
            rows = ((0, 0, A["conv_w"][0].rearrange("i (b p) -> (i b) p", p=P), 96),
                    (0, 96, A["conv_b"][0].rearrange("(b p) -> b p", p=P), 24),
                    (1, 0, A["norm1_g"][0].rearrange("(b p) -> b p", p=P), 8),
                    (1, 8, A["norm2_g"][0].rearrange("(b p) -> b p", p=P), 8),
                    (1, 16, A["ssm_norm_g"][0].rearrange("(b p) -> b p", p=P), 16))
            for part, r0, src, n in rows:
                sp.dma_start(vec_rows[r0:r0 + n, part, :], src).then_inc(vec_in, 16)
            for dst, name in ((K.le, "k_le"), (K.gt, "k_gt"), (K.ones, "k_ones"), (K.diag_off, "k_diag_off")):
                sp.dma_start(dst[:], A[name]).then_inc(K.const_in, 16)
            for i, name in enumerate(("dt_bias", "a_log", "d_skip")):
                sp.dma_start(K.heads_row[:, i, :], A[name][0].partition_broadcast(P)).then_inc(K.const_in, 16)
                sp.dma_start(K.heads_col[:, i:i + 1], A[name][0].unsqueeze(1)).then_inc(K.const_in, 16)
            ring_load(K, sp, "ada", lambda i: (prod, i + 1))

        @block.scalar
        def _(act):
            act.wait_ge(c_in, 32)
            nc.scalar.activation(c_silu[:], c_rows[:], ACT.Silu).then_inc(silu_done, 1)

        @block.tensor
        def _(pe):
            pe.wait_ge(K.ident_in, 16)
            pe.wait_ge(silu_done, 1)
            for k in range(KB):
                mm = nc.tensor.transpose(ps[:, 7, 9 * k:9 * k + 9], c_silu[:, P * k:P * k + P], K.ident[0:9, 0:9])
            mm.then_inc(cT_ps, 1)
            pe.wait_ge(cT_done, 1)
            for n in range(first, last):
                i = n - first
                pe.wait_ge(*ring_landed(K, n))
                if i >= 2:
                    pe.wait_ge(summed, i - 1)
                for k in range(KB):
                    mm = nc.tensor.matmul(ps[0:9, i % 2, 0:256], cT[:, k, :], slab_of(K, n)[:, k, :],
                                          start=(k == 0), stop=(k == KB - 1))
                mm.then_inc(prod, 1)
            pe.wait_ge(vec_in, 80)
            nc.tensor.transpose(ps[:, 4, 0:120], vec_rows[0:120, 0, :], K.ident[0:120, 0:120])
            nc.tensor.transpose(ps[:, 4, 120:152], vec_rows[0:32, 1, :], K.ident[0:32, 0:32]).then_inc(vec_ps, 1)
            pe.wait_ge(summed, last - first)
            for a, part in enumerate((0, 1)):
                for k in range(KB):
                    mm = nc.tensor.transpose(ps[:, 5, (8 * a + k) * 9:(8 * a + k) * 9 + 9],
                                             mod[:, D * part + P * k:D * part + P * k + P], K.ident[0:9, 0:9])
            mm.then_inc(modT_ps, 1)

        @block.vector
        def _(dve):
            dve.wait_ge(cT_ps, 1)
            nc.vector.tensor_copy(cT[:].rearrange("p k s -> p (k s)"), ps[:, 7, 0:72]).then_inc(cT_done, 1)
            dve.wait_ge(mod_b, 16)
            for i in range(last - first):
                dve.wait_ge(prod, i + 1)
                nc.vector.tensor_tensor(mod[:, 256 * i:256 * i + 256], ps[0:9, i % 2, 0:256],
                                        mod[:, 256 * i:256 * i + 256], ALU.add).then_inc(summed, 1)
            dve.wait_ge(vec_ps, 1)
            nc.vector.tensor_copy(K.vecs[:], ps[:, 4, 0:152]).then_inc(step, 1)
            dve.wait_ge(modT_ps, 1)
            nc.vector.tensor_copy(K.modT[:, 0:2].rearrange("p a k s -> p (a k s)"), ps[:, 5, 0:144]).then_inc(step, 1)
            dve.wait_ge(step, 2)
            sc = K.modT[:, 1, :, :]
            nc.vector.tensor_scalar(sc, sc, 1.0, None, ALU.add).then_inc(step, 1)
            dve.wait_ge(step, 3)
            g = K.vecs[:, 120:128].unsqueeze(2).to_broadcast([P, KB, 9])
            nc.vector.tensor_tensor(sc, sc, g, ALU.mult)


def norm_stage(K, tag, which, hT, source):
    nc, ps = K.nc, K.ps
    with ExitStack() as ctx:
        def sb(name, shape):
            return ctx.enter_context(nc.sbuf_tensor(tag + name, shape, F32))
        x = sb("x", [P, 3, D])
        xn = sb("xn", [P, 2, D])
        sq = sb("sq", [P, D])
        stat = sb("stat", [P, 4, 9])
        x_in = [K.sem(f"{tag}x_in{i}") for i in range(3)]
        squared, mean, root, inv = K.sem(tag + "squared"), K.sem(tag + "mean"), K.sem(tag + "root"), K.sem(tag + "inv")
        scaled, turned, moved = K.sem(tag + "scaled"), K.sem(tag + "turned"), K.sem(tag + "moved")
        extra = K.sem(tag + "sample_scaled")
        block = ctx.enter_context(nc.Block())

        @block.sync
        def _(sp):
            for t in range(9):
                if t >= 3:
                    sp.wait_ge(scaled, t - 2)
                    sp.wait_ge(squared, t - 2)
                sp.dma_start(x[0:rows_of(t), t % 3, :], source(t)).then_inc(x_in[t % 3], 16)

        @block.scalar
        def _(act):
            def square(t):
                r = rows_of(t)
                act.wait_ge(x_in[t % 3], 16 * (t // 3 + 1))
                if t:
                    act.wait_ge(squared, t)
                nc.scalar.activation(sq[0:r, :], x[0:r, t % 3, :], ACT.Square,
                                     accum_out=stat[0:r, 0, t:t + 1]).then_inc(squared, 1)
                act.wait_ge(mean, t + 1)
                nc.scalar.activation(stat[0:r, 2, t:t + 1], stat[0:r, 1, t:t + 1], ACT.Sqrt).then_inc(root, 1)

            def move(t):
                for h in range(2):
                    act.wait_ge(turned, 2 * t + h + 1)
                    for j in range(4):
                        k = 4 * h + j
                        mv = nc.scalar.activation(hT[:, k, P * t:P * t + P], ps[:, 2 * (t % 2) + h, P * j:P * j + P],
                                                  ACT.Identity, bias=K.modT[:, 2 * which, k, 0:1],
                                                  scale=K.modT[:, 2 * which + 1, k, 0:1])
                    mv.then_inc(moved, 1)

            square(0)
            for t in range(TT):
                square(t + 1)
                move(t)

        @block.vector
        def _(dve):
            for t in range(9):
                r = rows_of(t)
                dve.wait_ge(squared, t + 1)
                nc.vector.tensor_scalar(stat[0:r, 1, t:t + 1], stat[0:r, 0, t:t + 1], 1.0 / D, EPS,
                                        ALU.mult, ALU.add).then_inc(mean, 1)
                dve.wait_ge(root, t + 1)
                nc.vector.reciprocal(stat[0:r, 3, t:t + 1], stat[0:r, 2, t:t + 1]).then_inc(inv, 1)
                dve.wait_ge(inv, t + 1)
                if t >= 2:
                    dve.wait_ge(turned, 2 * (t - 1))
                nc.vector.tensor_scalar(xn[0:r, t % 2, :], x[0:r, t % 3, :], stat[0:r, 3, t:t + 1], None,
                                        ALU.mult).then_inc(scaled, 1)
            dve.wait_ge(turned, 2 * TT + 1)
            hs = hT[:, :, SEQ:NT]
            nc.vector.tensor_tensor(hs, ps[:, 4, 0:64].rearrange("p (k s) -> p k s", k=KB),
                                    K.modT[:, 2 * which + 1, :, 1:9], ALU.mult).then_inc(extra, 1)
            dve.wait_ge(extra, 1)
            nc.vector.tensor_tensor(hs, hs, K.modT[:, 2 * which, :, 1:9], ALU.add).then_inc(extra, 1)

        @block.tensor
        def _(pe):
            for t in range(9):
                pe.wait_ge(scaled, t + 1)
                if t == TT:
                    for k in range(KB):
                        mm = nc.tensor.transpose(ps[:, 4, 8 * k:8 * k + 8], xn[0:DEC, t % 2, P * k:P * k + P],
                                                 K.ident[0:DEC, 0:DEC])
                    mm.then_inc(turned, 1)
                    break
                for h in range(2):
                    if t >= 2:
                        pe.wait_ge(moved, 2 * (t - 2) + h + 1)
                    for j in range(4):
                        k = 4 * h + j
                        mm = nc.tensor.transpose(ps[:, 2 * (t % 2) + h, P * j:P * j + P],
                                                 xn[:, t % 2, P * k:P * k + P], K.ident[:])
                    mm.then_inc(turned, 1)


def project(K, hT, T):
    nc, A, ps = K.nc, K.A, K.ps
    first, last = K.span["qkv"]
    n_slabs = last - first
    SMALL, QI, KK, V, Q0 = 0, 1, 2, 3, 4
    with ExitStack() as ctx:
        def sb(name, shape):
            return ctx.enter_context(nc.sbuf_tensor(name, shape, F32))
        stg = sb("stg", [P, 2, 9, 256])
        rot = sb("rot", [P, 2, 9, 256])
        tmp = sb("tmp", [P, 2, 256])
        gemm, out_of_ps = K.sem("qkv_in_psum"), K.sem("qkv_rows")
        t_a, t_b, rotated = K.sem("rope_cos_part"), K.sem("rope_sin_part"), K.sem("roped_tiles")
        dtT_ps, kept = K.sem("dtT_in_psum"), K.sem("sample_rows_kept")
        turned, moved = K.sem("qk_turned"), K.sem("qk_moved")
        ki_stored, k_stored, v_stored = (K.store_sem(n) for n in ("ki_stored", "k_stored", "v_stored"))
        block = ctx.enter_context(nc.Block())

        rope_cols = [(32, 1), (0, 4), (0, 4), None] + [(0, 4)] * 4
        roped_before = [9 * sum(1 for c in rope_cols[:s] if c) for s in range(n_slabs + 1)]

        def turns(s):
            r, lo, hi = rot[:, s % 2], slice(0, HD), slice(HD, P)
            if s == SMALL:
                return [(lambda t: r[:, t, 32:96], HD, [(lo, T.kiT[lo, :]), (lo, T.kiT[hi, :])])]
            if s == KK:
                return [(lambda t, j=j: r[:, t, P * j:P * j + P], P,
                         [(lo, T.kT[lo, 2 * j, :]), (lo, T.kT[hi, 2 * j, :]),
                          (hi, T.kT[lo, 2 * j + 1, :]), (hi, T.kT[hi, 2 * j + 1, :])]) for j in range(2)]
            if s == V:
                return []
            full = slice(0, P)
            return [(lambda t, j=j: r[:, t, P * j:P * j + P], P,
                     [(full, T.qiT[:, j, :] if s == QI else T.qT[:, 2 * (s - Q0) + j, 0:SEQ])]) for j in range(2)]

        units = [(s, src, w, dst, h) for s in range(n_slabs) for src, w, dst in turns(s) for h in range(2)]
        units_before = [sum(1 for u in units if u[0] < s) for s in range(n_slabs + 1)]

        @block.sync
        def _(sp):
            for dst, name in ((K.cos, "k_cos"), (K.sin, "k_sin")):
                sp.dma_start(dst[:], A[name]).then_inc(K.const_in, 16)
            ring_load(K, sp, "qkv", lambda i: (gemm, 9 * i + 9) if i else (dtT_ps, 1))

        @block.gpsimd
        def _(pool):
            pool.wait_ge(rotated, roped_before[SMALL + 1])
            r = rot[:, SMALL % 2]
            pool.dma_start(A["kidx_prompt"][0, 0].rearrange("(t p) d -> p t d", p=P), r[:, 0:TT, 32:96]).then_inc(ki_stored, 16)
            pool.dma_start(A["kidx_sample"][0, :, 0], r[0:DEC, TT, 32:96]).then_inc(ki_stored, 16)
            pool.wait_ge(rotated, roped_before[KK + 1])
            r = rot[:, KK % 2]
            pool.dma_start(A["k_prompt"][0, 0].rearrange("(t p) g d -> p t (g d)", p=P), r[:, 0:TT, :]).then_inc(k_stored, 16)
            pool.dma_start(A["k_sample"][0, :, 0].rearrange("b g d -> b (g d)"), r[0:DEC, TT, :]).then_inc(k_stored, 16)
            pool.wait_ge(out_of_ps, 9 * (V + 1))
            pool.dma_start(A["v_prompt"][0, 0].rearrange("(t p) g d -> p t (g d)", p=P), T.v[:, 0:TT, :]).then_inc(v_stored, 16)
            pool.dma_start(A["v_sample"][0, :, 0].rearrange("b g d -> b (g d)"), T.v[0:DEC, TT, :]).then_inc(v_stored, 16)
            for done in (ki_stored, k_stored, v_stored):
                pool.wait_ge(done, 32)

        @block.scalar
        def _(act):
            def rows(s):
                for t in range(9):
                    r, n = rows_of(t), 100 if s == SMALL else 256
                    act.wait_ge(gemm, 9 * s + t + 1)
                    if s >= 2 and t == 0:
                        act.wait_ge(kept, roped_before[s - 1] // 9)
                    dst = T.v[0:r, t, :] if s == V else stg[0:r, s % 2, t, 0:n]
                    nc.scalar.copy(dst, ps[0:r, (9 * s + t) % 4, 0:n]).then_inc(out_of_ps, 1)

            def turn_moves(s):
                for u in range(units_before[s], units_before[s + 1]):
                    _, _, _, places, h = units[u]
                    act.wait_ge(turned, u + 1)
                    for rows, dst in places:
                        mv = nc.scalar.copy(dst[:, 512 * h:512 * h + 512], ps[rows, 4 + u % 3, :])
                    mv.then_inc(moved, 1)

            rows(0)
            for s in range(1, n_slabs):
                rows(s)
                turn_moves(s - 1)
            turn_moves(n_slabs - 1)

        @block.vector
        def _(dve):
            m = 0
            dve.wait_ge(K.const_in, 16 * 12)
            for s in range(n_slabs):
                if rope_cols[s] is None:
                    continue
                c0, nh = rope_cols[s]
                w = HD * nh
                if s == QI + 1:
                    dve.wait_ge(ki_stored, 32)
                if s == Q0:
                    dve.wait_ge(k_stored, 32)
                if s >= 2:
                    dve.wait_ge(turned, units_before[s - 1])
                for t in range(9):
                    r = rows_of(t)
                    dve.wait_ge(out_of_ps, 9 * s + t + 1)
                    x = stg[0:r, s % 2, t, c0:c0 + w].rearrange("p (h d) -> p h d", d=HD)
                    o = rot[0:r, s % 2, t, c0:c0 + w].rearrange("p (h d) -> p h d", d=HD)
                    b = tmp[0:r, m % 2, 0:w].rearrange("p (h d) -> p h d", d=HD)
                    hh = HD // 2
                    cos = K.cos[0:r, t, :].unsqueeze(1).to_broadcast([r, nh, HD])
                    sin = K.sin[0:r, t, :].unsqueeze(1)
                    nc.vector.tensor_tensor(b[:, :, 0:hh], x[:, :, hh:HD], sin[:, :, 0:hh].to_broadcast([r, nh, hh]), ALU.mult)
                    nc.vector.tensor_tensor(b[:, :, hh:HD], x[:, :, 0:hh], sin[:, :, hh:HD].to_broadcast([r, nh, hh]),
                                            ALU.mult).then_inc(t_b, 1)
                    nc.vector.tensor_tensor(o, x, cos, ALU.mult).then_inc(t_a, 1)
                    m += 1
                    dve.wait_ge(t_b, m)
                    dve.wait_ge(t_a, m)
                    nc.vector.tensor_tensor(o, o, b, ALU.add).then_inc(rotated, 1)
                dve.wait_ge(rotated, m)
                if s == SMALL:
                    nc.vector.tensor_copy(T.dt_raw[:], stg[:, 0, 0:TT, 0:32])
                    nc.vector.tensor_scalar(T.wi[:, 0:TT, :], stg[:, 0, 0:TT, 96:100], IDX_SCALE, None, ALU.mult)
                    nc.vector.tensor_scalar(T.wi[0:DEC, TT, :], stg[0:DEC, 0, TT, 96:100], IDX_SCALE, None, ALU.mult)
                    nc.vector.tensor_copy(T.ki_s[:], rot[0:DEC, 0, TT, 32:96]).then_inc(kept, 1)
                elif s == QI:
                    nc.vector.tensor_copy(T.qi_s[:], rot[0:DEC, 1, TT, :]).then_inc(kept, 1)
                elif s == KK:
                    nc.vector.tensor_copy(T.k_s[:], rot[0:DEC, 0, TT, :]).then_inc(kept, 1)
                else:
                    nc.vector.tensor_copy(T.q_s[:, 256 * (s - Q0):256 * (s - Q0) + 256],
                                          rot[0:DEC, s % 2, TT, :]).then_inc(kept, 1)
            dve.wait_ge(dtT_ps, 1)
            nc.vector.tensor_copy(T.dtT_raw[:], ps[0:32, 7, 0:DEC])

        @block.tensor
        def _(pe):
            def gemm_slab(s):
                n = first + s
                w = slab_of(K, n)
                width = 100 if s == SMALL else 256
                pe.wait_ge(*ring_landed(K, n))
                for t in range(9):
                    r = rows_of(t)
                    if 9 * s + t >= 4:
                        pe.wait_ge(out_of_ps, 9 * s + t - 3)
                    for k in range(KB):
                        mm = nc.tensor.matmul(ps[0:r, (9 * s + t) % 4, 0:width], hT[:, k, P * t:P * t + r], w[:, k, 0:width],
                                              start=(k == 0), stop=(k == KB - 1))
                    mm.then_inc(gemm, 1)

            def turn_slab(s):
                for u in range(units_before[s], units_before[s + 1]):
                    _, src, w, _, h = units[u]
                    if u >= 3:
                        pe.wait_ge(moved, u - 2)
                    for j in range(4):
                        t = 4 * h + j
                        pe.wait_ge(rotated, roped_before[s] + t + 1)
                        mm = nc.tensor.transpose(ps[0:w, 4 + u % 3, P * j:P * j + P], src(t), K.ident[:])
                    mm.then_inc(turned, 1)

            gemm_slab(0)
            w = slab_of(K, first)
            for k in range(KB):
                mm = nc.tensor.matmul(ps[0:HEADS, 7, 0:DEC], w[:, k, 0:HEADS], hT[:, k, SEQ:NT],
                                      start=(k == 0), stop=(k == KB - 1))
            mm.then_inc(dtT_ps, 1)
            for s in range(1, n_slabs):
                gemm_slab(s)
                turn_slab(s - 1)
            turn_slab(n_slabs - 1)


BIAS_AT = [P * i * (i + 1) // 2 for i in range(TT + 1)]


def select(K, hT, T):
    nc, A, ps = K.nc, K.A, K.ps
    first, last = K.span["gates"]
    with ExitStack() as ctx:
        def sb(name, shape):
            return ctx.enter_context(nc.sbuf_tensor(name, shape, F32))
        relu = sb("relu", [P, IH, SEQ])
        score, term = sb("score", [P, 2, SEQ]), sb("score_term", [P, SEQ])
        work, eq, cum = (sb(n, [P, SEQ]) for n in ("work", "eq", "cum"))
        top8, count = sb("top8", [P, 2, 8]), sb("count", [P, 2])
        sig = sb("sig", [P, 2, NT])
        xbc = sb("xbc_out", [P, 2, CW])
        xbc_sum, xbc_kept, xbc_out = K.sem("xbc0_sums"), K.sem("xbc0_kept"), [K.sem(f"xbc0_stored{i}") for i in range(2)]
        mod_new = sb("mod_new", [9, 2, 256])
        gemm, sig_done, sig_out = K.sem("gate_sums"), K.sem("gate_sigmoids"), [K.store_sem(f"gate_out{i}") for i in range(2)]
        idx_ps, relu_done, relu_used = K.sem("index_in_psum"), K.sem("index_relus"), K.sem("index_relus_used")
        step = K.sem("select_step")
        score_step, score_done, picked = K.sem("score_step"), K.sem("score_done"), K.sem("keys_picked")
        mod_sum, mod_kept, mod_out = K.sem("mod_sums"), K.sem("mod_kept"), [K.store_sem(f"mod_stored{i}") for i in range(2)]
        block = ctx.enter_context(nc.Block())

        groups = [(n, fb, c) for n in range(8) for fb in range(2) for c in range(TC)]
        fill = []
        for n in range(8):
            fill += [("gate", 6 * n + j) for j in range(6)] + [("mod", 2 * n + j) for j in range(2)]
        fill += [("xbc", j) for j in range(6 * TC)]
        take = dict(zip(range(2, TT), (6, 9, 10, 12, 14, 31)))
        units = [(i, h) for i in range(2, TT) for h in range(IH)]
        order, g = [], 0
        for i in range(2, TT):
            order += [("index", IH * (i - 2) + h) for h in range(IH)]
            order += fill[g:g + take[i]]
            g += take[i]
        place = {f: j for j, f in enumerate(fill)}

        def emptied(j):
            kind, u = fill[j]
            return {"gate": sig_done, "mod": mod_kept, "xbc": xbc_kept}[kind], u + 1

        @block.sync
        def _(sp):
            def used(i):
                if i >= 24:
                    return xbc_sum, 2 * TC * (i - 23)
                return (mod_sum, 2 * (i // 3) + i % 3) if i % 3 else (gemm, 2 * TC * (i // 3 + 1))
            ring_load(K, sp, "gates", used)

        @block.gpsimd
        def _(pool):
            v, n = nc.gpsimd, [0]

            def link(ins):
                n[0] += 1
                ins.then_inc(score_step, 1)
                pool.wait_ge(score_step, n[0])

            for i in range(2, TT):
                L = P * (i + 1)
                sc = score[:, i % 2, 0:L]
                if i >= 4:
                    pool.wait_ge(picked, i - 3)
                for h in range(IH):
                    pool.wait_ge(relu_done, IH * (i - 2) + h + 1)
                    w = T.wi[:, i, h:h + 1].to_broadcast([P, L])
                    to = term[:, 0:L] if h else sc
                    v.tensor_tensor(to, relu[:, h, 0:L], w, ALU.mult).then_inc(relu_used, 1)
                    pool.wait_ge(relu_used, IH * (i - 2) + h + 1)
                    if h:
                        link(v.tensor_tensor(sc, sc, term[:, 0:L], ALU.add))
                v.tensor_tensor(sc[:, L - P:L], sc[:, L - P:L], K.diag_off[:], ALU.add).then_inc(score_done, 1)

        @block.tensor
        def _(pe):
            for kind, u in order:
                if kind == "index":
                    i, h = units[u]
                    if u >= 2:
                        pe.wait_ge(relu_done, u - 1)
                    rows = slice(HD * (h % 2), HD * (h % 2) + HD)
                    for c0 in range(0, P * (i + 1), 512):
                        n = min(512, P * (i + 1) - c0)
                        mm = nc.tensor.matmul(ps[:, 4 + 2 * (u % 2) + c0 // 512, 0:n],
                                              T.qiT[rows, h // 2, P * i:P * i + P], T.kiT[rows, c0:c0 + n],
                                              start=True, stop=True)
                    mm.then_inc(idx_ps, 1)
                else:
                    j = place[kind, u]
                    if j >= 4:
                        pe.wait_ge(*emptied(j - 4))
                    if kind == "mod":
                        n = first + 3 * (u // 2) + 1 + u % 2
                        pe.wait_ge(*ring_landed(K, n))
                        for k in range(KB):
                            mm = nc.tensor.matmul(ps[0:9, j % 4, 0:256], K.cT[:, k, :], slab_of(K, n)[:, k, :],
                                                  start=(k == 0), stop=(k == KB - 1))
                        mm.then_inc(mod_sum, 1)
                        continue
                    if kind == "xbc":
                        f, c = u // TC, u % TC
                        if u % (2 * TC) == 0:
                            pe.wait_ge(*ring_landed(K, first + 24 + f // 2))
                        w = slab_of(K, first + 24 + f // 2)
                        for k in range(KB):
                            mm = nc.tensor.matmul(ps[:, j % 4, 0:CW], w[:, k, P * (f % 2):P * (f % 2) + P],
                                                  hT[:, k, CW * c:CW * c + CW], start=(k == 0), stop=(k == KB - 1))
                        mm.then_inc(xbc_sum, 1)
                        continue
                    n, fb, c = groups[u]
                    if fb == 0 and c == 0:
                        pe.wait_ge(*ring_landed(K, first + 3 * n))
                    w = slab_of(K, first + 3 * n)
                    for k in range(KB):
                        mm = nc.tensor.matmul(ps[:, j % 4, 0:CW], w[:, k, P * fb:P * fb + P],
                                              hT[:, k, CW * c:CW * c + CW], start=(k == 0), stop=(k == KB - 1))
                    mm.then_inc(gemm, 1)

        @block.scalar
        def _(act):
            for kind, u in order:
                if kind == "index":
                    i, h = units[u]
                    L = P * (i + 1)
                    act.wait_ge(idx_ps, u + 1)
                    if u >= IH:
                        act.wait_ge(relu_used, u - IH + 1)
                    nc.scalar.activation(relu[:, h, 0:L], ps[:, 4 + 2 * (u % 2):6 + 2 * (u % 2), :]
                                         .rearrange("p a n -> p (a n)")[:, 0:L], ACT.Relu).then_inc(relu_done, 1)
                elif kind == "xbc":
                    act.wait_ge(xbc_sum, u + 1)
                    if u >= 2:
                        act.wait_ge(xbc_out[u % 2], 16 * (u // 2))
                    nc.scalar.copy(xbc[:, u % 2, :], ps[:, place[kind, u] % 4, 0:CW]).then_inc(xbc_kept, 1)
                    act.wait_ge(xbc_kept, u + 1)
                    c = u % TC
                    act.dma_start(A["s_xbc"][u // TC, :, CW * c:CW * c + CW], xbc[:, u % 2, :]).then_inc(xbc_out[u % 2], 16)
                elif kind == "mod":
                    act.wait_ge(mod_sum, u + 1)
                    if u >= 2:
                        act.wait_ge(mod_out[u % 2], 16 * (u // 2))
                    nc.scalar.copy(mod_new[:, u % 2, :], ps[0:9, place[kind, u] % 4, 0:256]).then_inc(mod_kept, 1)
                    act.wait_ge(mod_kept, u + 1)
                    act.dma_start(A["s_mod"][:, 256 * u:256 * u + 256], mod_new[:, u % 2, :]).then_inc(mod_out[u % 2], 16)
                else:
                    n, fb, c = groups[u]
                    b = 2 * n + fb
                    act.wait_ge(gemm, u + 1)
                    if c == 0 and b >= 2:
                        act.wait_ge(sig_out[b % 2], 16 * (b // 2))
                    nc.scalar.activation(sig[:, b % 2, CW * c:CW * c + CW], ps[:, place[kind, u] % 4, 0:CW],
                                         ACT.Sigmoid).then_inc(sig_done, 1)
                    if c == TC - 1:
                        act.wait_ge(sig_done, u + 1)
                        act.dma_start(A["s_sig"][b], sig[:, b % 2, :]).then_inc(sig_out[b % 2], 16)
            for done in mod_out + sig_out:
                act.wait_ge(done, 16 * KB)
            for done in xbc_out:
                act.wait_ge(done, 16 * 3 * TC)

        @block.vector
        def _(dve):
            n = [0]

            def link(ins):
                n[0] += 1
                ins.then_inc(step, 1)
                dve.wait_ge(step, n[0])

            v = nc.vector
            link(v.tensor_copy(T.bias[:, 0:P], K.diag_off[:]))
            link(v.memset(T.bias[:, P:2 * P], 0.0))
            link(v.tensor_copy(T.bias[:, 2 * P:3 * P], K.diag_off[:]))
            for i in range(2, TT):
                L = P * (i + 1)
                sc, wk, e, cu = score[:, i % 2, 0:L], work[:, 0:L], eq[:, 0:L], cum[:, 0:L]
                dve.wait_ge(score_done, i - 1)
                cur = sc
                for r in range(TOPK // 8):
                    m8 = top8[:, r % 2, :]
                    link(v.max(m8, cur))
                    if r < TOPK // 8 - 1:
                        link(v.match_replace(wk, m8, cur, FAR))
                        cur = wk
                thr = m8[:, 7:8]
                link(v.tensor_scalar(wk, sc, thr, None, ALU.is_gt, ALU.add, accum_out=count[:, 0:1]))
                link(v.tensor_scalar(count[:, 1:2], count[:, 0:1], -1.0, float(TOPK), ALU.mult, ALU.add))
                v.tensor_scalar(e, sc, thr, None, ALU.is_equal).then_inc(picked, 1)
                dve.wait_ge(picked, i - 1)
                link(v.tensor_tensor_scan(cu, K.ones[:, 0:1].to_broadcast([P, L]), e, 0.0, ALU.mult, ALU.add))
                link(v.scalar_tensor_tensor(cu, cu, count[:, 1:2], e, ALU.is_le, ALU.mult))
                link(v.scalar_tensor_tensor(wk, wk, -1.0, cu, ALU.add, ALU.add))
                link(v.tensor_scalar(T.bias[:, BIAS_AT[i]:BIAS_AT[i] + L], wk, -OFF, None, ALU.mult))


def attend(K, T):
    nc, ps = K.nc, K.ps
    with ExitStack() as ctx:
        def sb(name, shape):
            return ctx.enter_context(nc.sbuf_tensor(name, shape, F32))
        prob = sb("prob", [P, 2, SEQ])
        probT = sb("probT", [P, 2, SEQ])
        y = sb("y", [P, 2, D])
        k_hi, k_lo = (ctx.enter_context(nc.sbuf_tensor(n, [P, KVH, SEQ], F32R)) for n in ("k_hi", "k_lo"))
        q_both = ctx.enter_context(nc.sbuf_tensor("q_both", [P, 2, AH // 2, P], F32R))
        k_rounded, k_split, q_rounded, q_split = (K.sem(n) for n in ("k_rounded", "k_split", "q_rounded", "q_split"))
        top, nbias, total, inv = (sb(n, [P, 2]) for n in ("top", "nbias", "total", "inv"))
        qk, logits, nb = K.sem("qk_in_psum"), K.sem("logits_done"), K.sem("neg_max_done")
        probs, t_ps, t_moved = K.sem("probs_done"), K.sem("probT_in_psum"), K.sem("probT_done")
        o_ps, inv_done, o_done = K.sem("pv_in_psum"), K.sem("inv_done"), K.sem("y_head_done")
        y_ps, y_moved = K.sem("yT_in_psum"), K.sem("yT_done")
        block = ctx.enter_context(nc.Block())
        N = TT * AH

        def tile(n):
            return n // AH

        def chunks(i):
            L = P * (i + 1)
            if L <= 512:
                return 0, [(0, L)]
            at = P if L < 7 * P else 0
            return at, [(0, 512 - at), (512 - at, L)]

        @block.gpsimd
        def _(pool):
            half = AH // 2
            for i in range(TT):
                cols = slice(P * i, P * i + P)
                if i:
                    pool.wait_ge(q_split, 4 * i)
                nc.gpsimd.tensor_copy(k_hi[:, :, cols], T.kT[:, :, cols]).then_inc(k_rounded, 1)
                pool.wait_ge(k_rounded, i + 1)
                nc.gpsimd.tensor_tensor(k_lo[:, :, cols], T.kT[:, :, cols], k_hi[:, :, cols].bitcast(F32),
                                        ALU.subtract).then_inc(k_split, 1)
                for g in range(2):
                    if i:
                        pool.wait_ge(qk, AH * (i - 1) + half * (g + 1))
                    q = T.qT[:, half // 2 * g:half // 2 * (g + 1), cols]
                    out = q_both[:, g].rearrange("p (j o) t -> p o j t", o=2)
                    pool.wait_ge(k_split, i + 1)
                    for odd in range(2):
                        own, other = slice(HD * odd, HD * odd + HD), slice(HD * (1 - odd), HD * (1 - odd) + HD)
                        n = 2 * (2 * i + g) + odd
                        if n:
                            pool.wait_ge(q_split, n)
                        nc.gpsimd.tensor_copy(out[own, odd], q[own]).then_inc(q_rounded, 1)
                        pool.wait_ge(q_rounded, n + 1)
                        nc.gpsimd.tensor_tensor(out[other, odd], q[own], out[own, odd].bitcast(F32),
                                                ALU.subtract).then_inc(q_split, 1)

        def turn_groups(n):
            return sum(1 if i < 4 else 2 for i in range(tile(n))) * AH + (n % AH) * (1 if tile(n) < 4 else 2)

        events, seen = [], {}
        for n in range(N + 1):
            if n < N:
                for q in range(turn_groups(n), turn_groups(n + 1) if n + 1 < N else turn_groups(n) + 2):
                    events.append(("prob", q, n))
            if n % AH == 2 and n > AH or n == N:
                i = (n - 1) // AH if n == N else tile(n) - 1
                events += [("y", 2 * i, i), ("y", 2 * i + 1, i)]
        for e, (kind, q, _) in enumerate(events):
            seen[kind, q] = e

        def bank_free(eng, e):
            if e >= 3:
                kind, q, _ = events[e - 3]
                eng.wait_ge(t_moved if kind == "prob" else y_moved, q + 1)

        @block.tensor
        def _(pe):
            def qk_unit(n):
                i, h = tile(n), n % AH
                g, r = h // (AH // 2), h % (AH // 2)
                pe.wait_ge(k_split, i + 1)
                pe.wait_ge(q_split, 2 * (2 * i + g) + 2)
                if n >= 2:
                    pe.wait_ge(logits, n - 1)
                at, parts = chunks(i)
                for bank, (c0, c1) in enumerate(parts):
                    to = ps[:, 2 * (n % 2) + bank, (0 if bank else at):(0 if bank else at) + c1 - c0]
                    kv = h // (AH // KVH)
                    nc.tensor.matmul(to, q_both[:, g, r, :], k_lo[:, kv, c0:c1], start=True, stop=False)
                    mm = nc.tensor.matmul(to, q_both[:, g, r, :], k_hi[:, kv, c0:c1], start=False, stop=True)
                mm.then_inc(qk, 1)

            def turn(n):
                i = tile(n)
                pe.wait_ge(probs, n + 1)
                for q in range(turn_groups(n), turn_groups(n) + (1 if i < 4 else 2)):
                    e = seen["prob", q]
                    bank_free(pe, e)
                    b0 = 4 * (q - turn_groups(n))
                    for b in range(b0, min(b0 + 4, i + 1)):
                        mm = nc.tensor.transpose(ps[:, 4 + e % 3, P * (b - b0):P * (b - b0) + P],
                                                 prob[:, n % 2, P * b:P * b + P], K.ident[:])
                    mm.then_inc(t_ps, 1)

            def pv(n):
                i, h = tile(n), n % AH
                g = h // (AH // KVH)
                pe.wait_ge(t_moved, turn_groups(n) + (1 if i < 4 else 2))
                if n:
                    pe.wait_ge(o_done, n)
                for b in range(i + 1):
                    mm = nc.tensor.matmul(ps[:, 7, 0:HD], probT[:, n % 2, P * b:P * b + P],
                                          T.v[:, b, HD * g:HD * g + HD], start=(b == 0), stop=(b == i))
                mm.then_inc(o_ps, 1)

            def turn_y(i):
                pe.wait_ge(o_done, AH * (i + 1))
                for half in range(2):
                    e = seen["y", 2 * i + half]
                    bank_free(pe, e)
                    for j in range(4):
                        b = 4 * half + j
                        mm = nc.tensor.transpose(ps[:, 4 + e % 3, P * j:P * j + P], y[:, i % 2, P * b:P * b + P],
                                                 K.ident[:])
                    mm.then_inc(y_ps, 1)

            qk_unit(0)
            qk_unit(1)
            for n in range(N):
                turn(n)
                if n + 2 < N:
                    qk_unit(n + 2)
                if n:
                    pv(n - 1)
                if n % AH == 2 and n > AH:
                    turn_y(tile(n) - 1)
            pv(N - 1)
            turn_y(TT - 1)

        @block.vector
        def _(dve):
            def logit(n):
                i = tile(n)
                L = P * (i + 1)
                dve.wait_ge(qk, n + 1)
                if n >= 2:
                    dve.wait_ge(t_ps, turn_groups(n - 1))
                nc.vector.tensor_tensor_reduce(
                    out=prob[:, n % 2, 0:L], in0=ps[:, 2 * (n % 2):2 * (n % 2) + 2, :].rearrange("p a n -> p (a n)")[:, chunks(i)[0]:chunks(i)[0] + L],
                    in1=T.bias[:, BIAS_AT[i]:BIAS_AT[i] + L], scale=1.0, scalar=FAR, op0=ALU.add, op1=ALU.max,
                    accum_out=top[:, n % 2:n % 2 + 1]).then_inc(logits, 1)
                dve.wait_ge(logits, n + 1)
                nc.vector.tensor_scalar(nbias[:, n % 2:n % 2 + 1], top[:, n % 2:n % 2 + 1], -ATT_SCALE, None,
                                        ALU.mult).then_inc(nb, 1)

            def head(n):
                i, h = tile(n), n % AH
                dve.wait_ge(probs, n + 1)
                nc.vector.reciprocal(inv[:, n % 2:n % 2 + 1], total[:, n % 2:n % 2 + 1]).then_inc(inv_done, 1)
                dve.wait_ge(inv_done, n + 1)
                dve.wait_ge(o_ps, n + 1)
                if h == 0 and i >= 2:
                    dve.wait_ge(y_ps, 2 * (i - 1))
                nc.vector.tensor_scalar(y[:, i % 2, HD * h:HD * h + HD], ps[:, 7, 0:HD], inv[:, n % 2:n % 2 + 1],
                                        None, ALU.mult).then_inc(o_done, 1)

            for n in range(N + 2):
                if n < N:
                    logit(n)
                if n >= 2:
                    head(n - 2)

        @block.scalar
        def _(act):
            e = 0

            def move(upto):
                nonlocal e
                while e < upto:
                    kind, q, n = events[e]
                    if kind == "prob":
                        i = tile(n)
                        b0 = 4 * (q - turn_groups(n))
                        w = P * (min(b0 + 4, i + 1) - b0)
                        act.wait_ge(t_ps, q + 1)
                        if n >= 2:
                            act.wait_ge(o_ps, n - 1)
                        nc.scalar.copy(probT[:, n % 2, P * b0:P * b0 + w], ps[:, 4 + e % 3, 0:w]).then_inc(t_moved, 1)
                    else:
                        act.wait_ge(y_ps, q + 1)
                        half = q % 2
                        nc.scalar.copy(T.qT[:, 4 * half:4 * half + 4, P * n:P * n + P],
                                       ps[:, 4 + e % 3, :].rearrange("p (b t) -> p b t", b=4)).then_inc(y_moved, 1)
                    e += 1

            def exp(n):
                L = P * (tile(n) + 1)
                act.wait_ge(nb, n + 1)
                if n >= 2:
                    act.wait_ge(inv_done, n - 1)
                nc.scalar.activation(prob[:, n % 2, 0:L], prob[:, n % 2, 0:L], ACT.Exp, bias=nbias[:, n % 2:n % 2 + 1],
                                     scale=ATT_SCALE, accum_out=total[:, n % 2:n % 2 + 1]).then_inc(probs, 1)

            exp(0)
            for n in range(1, N):
                exp(n)
                move(seen["prob", turn_groups(n)])
            move(len(events))


def attend_samples(K, T):
    nc, A, ps = K.nc, K.A, K.ps
    KP = 2
    with ExitStack() as ctx:
        def sb(name, shape, dt=F32):
            return ctx.enter_context(nc.sbuf_tensor(name, shape, dt))
        pages = sb("pages", [1, DEC * NPAGE], I32)
        kpage, vpage = sb("kpage", [P, DEC, NPAGE, 256]), sb("vpage", [P, DEC, NPAGE, 256])
        ipage = sb("ipage", [P, DEC, NPAGE, HD])
        q_r = sb("q_r", [DEC, D])
        skT = sb("skT", [P, DEC, KP, SKEYS])
        sqx = sb("sqx", [P, 2320])
        siT, sqiT = sb("siT", [HD, DEC, SKEYS]), sb("sqiT", [HD, DEC, IH])
        swx = sb("swx", [IH, 9 * DEC])
        srelu = sb("srelu", [IH, 2, SKEYS])
        who, whoT = sb("who", [DEC, P]), sb("whoT", [P, DEC])
        ssc, swk, seq_, scu, sbias = (sb(n, [DEC, SKEYS]) for n in ("ssc", "swk", "seq", "scu", "sbias"))
        s8, scount = sb("s8", [DEC, 8]), sb("scount", [DEC, 2])
        sp_, sdiag = sb("sprob", [P, SKEYS]), sb("sdiag", [P, P])
        spT, snew = sb("spT", [P, NPAGE, P]), sb("snew", [DEC, P])
        stat = sb("sstat", [P, 4])
        table_in, who_in = K.sem("page_table_in"), K.sem("who_in")
        i_in, k_in, v_in = K.sem("index_pages_in"), K.sem("key_pages_in"), K.sem("value_pages_in")
        step = K.sem("sample_step")
        pe_small, pe_idx, pe_key, pe_rel = K.sem("small_turned"), K.sem("ipages_turned"), K.sem("kpages_turned"), K.sem("srelu_in_psum")
        idx_moved, key_moved, rel_done = K.sem("siT_done"), K.sem("skT_done"), K.sem("srelu_done")
        pe_score, pe_logit, exp_done, pe_pT, pe_out = (K.sem(n) for n in (
            "sscore_in_psum", "slogits_in_psum", "sprobs_done", "sprobsT_in_psum", "sout_in_psum"))
        max_done, y_done, y_out = K.sem("smax_done"), K.sem("sample_y_done"), K.sem("y_att_stored")
        ready, biased, diag_done, pT_done = K.sem("small_done"), K.sem("sbias_done"), K.sem("sdiag_done"), K.sem("spT_done")
        block = ctx.enter_context(nc.Block())

        @block.sync
        def _(sp):
            sp.dma_start(pages[:], A["page_table"].rearrange("b j -> (b j)").unsqueeze(0)).then_inc(table_in, 16)
            sp.dma_start(who[:], A["k_who"]).then_inc(who_in, 16)
            sp.dma_start(A["s_att"].rearrange("k p n -> p k n")[:, :, 0:SEQ], T.qT[:, :, 0:SEQ]).then_inc(y_out, 16)
            sp.wait_ge(table_in, 16)
            for cache, dst, done in (("cache_kidx", ipage, i_in), ("cache_k", kpage, k_in), ("cache_v", vpage, v_in)):
                n_pool = A[cache].shape[1]
                for b in range(DEC):
                    for j in range(NPAGE):
                        at = sp.value_load(pages[0:1, NPAGE * b + j:NPAGE * b + j + 1], min_val=0, max_val=n_pool - 1)
                        src = A[cache][0, bass.ds(at, 1)]
                        src = src.rearrange("a t d -> (a t) d" if cache == "cache_kidx" else "a t g d -> (a t) (g d)")
                        sp.dma_start(dst[:, b, j, :], src).then_inc(done, 16)
            sp.wait_ge(y_done, 1)
            sp.dma_start(A["s_att"].rearrange("k p n -> p k n")[:, :, SEQ:NT], T.qT[:, :, SEQ:NT]).then_inc(y_out, 16)
            sp.wait_ge(y_out, 32)

        @block.tensor
        def _(pe):
            tr, mm = nc.tensor.transpose, nc.tensor.matmul
            i8, i4 = K.ident[0:DEC, 0:DEC], K.ident[0:DEC, 0:DEC]
            pe.wait_ge(step, 1)
            pe.wait_ge(who_in, 16)
            for m in range(KB):
                tr(ps[:, 0, DEC * m:DEC * m + DEC], q_r[:, P * m:P * m + P], i8)
            for p in range(KP):
                tr(ps[:, 0, 64 + DEC * p:72 + DEC * p], T.k_s[:, P * p:P * p + P], i8)
            tr(ps[0:HD, 0, 80:88], T.ki_s[:], i8)
            for h in range(IH):
                tr(ps[0:HD, 0, 88 + DEC * h:96 + DEC * h], T.qi_s[:, HD * h:HD * h + HD], i8)
            tr(ps[0:IH, 0, 120:128], T.wi[0:DEC, TT, :], i4)
            tr(ps[:, 0, 128:136], who[:], i8).then_inc(pe_small, 1)
            pe.wait_ge(i_in, 16 * DEC * NPAGE)
            for a in range(4):
                if a >= 2:
                    pe.wait_ge(idx_moved, a - 1)
                for b in range(2):
                    for j in range(NPAGE):
                        m = tr(ps[0:HD, 1 + a % 2, 256 * b + P * j:256 * b + P * j + P], ipage[:, 2 * a + b, j, :], K.ident[:])
                m.then_inc(pe_idx, 1)
            pe.wait_ge(ready, 1)
            pe.wait_ge(idx_moved, 4)
            for b in range(DEC + 1):
                if b < DEC:
                    if b >= 2:
                        pe.wait_ge(rel_done, b - 1)
                    mm(ps[0:IH, 3 + b % 2, 0:SKEYS], sqiT[:, b, :], siT[:, b, :], start=True, stop=True).then_inc(pe_rel, 1)
                if b:
                    pe.wait_ge(rel_done, b)
                    mm(ps[0:DEC, 5, 0:SKEYS], swx[:, DEC * (b - 1):DEC * b], srelu[:, (b - 1) % 2, :],
                       start=(b == 1), stop=(b == DEC)).then_inc(pe_score, 1)
            pe.wait_ge(k_in, 16 * DEC * NPAGE)
            for b in range(DEC):
                if b >= 2:
                    pe.wait_ge(key_moved, b - 1)
                for p in range(KP):
                    for j in range(NPAGE):
                        m = tr(ps[:, 6 + b % 2, 256 * p + P * j:256 * p + P * j + P], kpage[:, b, j, P * p:P * p + P], K.ident[:])
                m.then_inc(pe_key, 1)
            pe.wait_ge(key_moved, DEC)
            pe.wait_ge(biased, 1)
            mm(ps[:, 3, 0:SKEYS], who[:], sbias[:], start=True, stop=False)
            for b in range(DEC):
                for p in range(KP):
                    last = b == DEC - 1 and p == KP - 1
                    m = mm(ps[:, 3, 0:SKEYS], sqx[:, 256 * b + P * p:256 * b + P * p + P], skT[:, b, p, :],
                           start=False, stop=last)
            m.then_inc(pe_logit, 1)
            pe.wait_ge(diag_done, 1)
            for j in range(NPAGE):
                tr(ps[:, 4, P * j:P * j + P], sp_[:, P * j:P * j + P], K.ident[:])
            mm(ps[0:DEC, 5, 0:P], whoT[:], sdiag[:], start=True, stop=True).then_inc(pe_pT, 1)
            pe.wait_ge(pT_done, 1)
            pe.wait_ge(v_in, 16 * DEC * NPAGE)
            for p in range(KP):
                mm(ps[:, 6 + p, 0:P], T.v[0:DEC, TT, P * p:P * p + P], snew[:], start=True, stop=False)
                for b in range(DEC):
                    for j in range(NPAGE):
                        m = mm(ps[:, 6 + p, AH * b:AH * b + AH], vpage[:, b, j, P * p:P * p + P],
                               spT[:, j, AH * b:AH * b + AH], start=False, stop=(b == DEC - 1 and j == NPAGE - 1))
            m.then_inc(pe_out, 1)

        @block.scalar
        def _(act):
            for a in range(4):
                act.wait_ge(pe_idx, a + 1)
                nc.scalar.copy(siT[:, 2 * a:2 * a + 2, 0:PAST], ps[0:HD, 1 + a % 2, :]
                               .rearrange("p (b s) -> p b s", b=2)).then_inc(idx_moved, 1)
            for b in range(DEC):
                act.wait_ge(pe_rel, b + 1)
                if b >= 2:
                    act.wait_ge(pe_score, b - 1)
                nc.scalar.activation(srelu[:, b % 2, :], ps[0:IH, 3 + b % 2, 0:SKEYS], ACT.Relu).then_inc(rel_done, 1)
            for b in range(DEC):
                act.wait_ge(pe_key, b + 1)
                nc.scalar.copy(skT[:, b, :, 0:PAST], ps[:, 6 + b % 2, :]
                               .rearrange("p (k s) -> p k s", k=KP)).then_inc(key_moved, 1)
            act.wait_ge(max_done, 1)
            nc.scalar.activation(sp_[:], sp_[:], ACT.Exp, bias=stat[:, 1:2], scale=ATT_SCALE,
                                 accum_out=stat[:, 2:3]).then_inc(exp_done, 1)

        @block.vector
        def _(dve):
            n = [0]
            v = nc.vector

            def link(ins):
                n[0] += 1
                ins.then_inc(step, 1)
                dve.wait_ge(step, n[0])

            gq = AH // KVH
            for p in range(KP):
                src = T.q_s[:, 512 * p:512 * p + 512].rearrange("b (g r d) -> b r g d", g=2, r=gq)
                c = v.tensor_copy(q_r[:, 512 * p:512 * p + 512].rearrange("b (r g d) -> b r g d", r=gq, g=2), src)
            link(c)
            link(v.memset(sqx[:], 0.0))
            link(v.memset(swx[:], 0.0))
            dve.wait_ge(pe_small, 1)
            for p in range(KP):
                for g in range(2):
                    off = P * p + gq * (2 * p + g)
                    rows = slice(HD * g, HD * g + HD)
                    v.tensor_copy(sqx[rows, off:off + 272 * DEC].rearrange("p (b x) -> p b x", x=272)[:, :, 0:gq],
                                  ps[rows, 0, 32 * p:32 * p + 32].rearrange("p (r b) -> p b r", b=DEC))
            for p in range(KP):
                v.tensor_copy(skT[:, :, p, PAST], ps[:, 0, 64 + DEC * p:72 + DEC * p])
            v.tensor_copy(siT[:, :, PAST], ps[0:HD, 0, 80:88])
            v.tensor_copy(sqiT[:], ps[0:HD, 0, 88:120].rearrange("p (h b) -> p b h", h=IH))
            v.tensor_copy(swx[:].rearrange("p (b x) -> p b x", x=9)[:, :, 0], ps[0:IH, 0, 120:128])
            v.tensor_copy(whoT[:], ps[:, 0, 128:136]).then_inc(ready, 1)
            dve.wait_ge(pe_score, DEC)
            link(v.tensor_copy(ssc[:], ps[0:DEC, 5, 0:SKEYS]))
            cur = ssc
            for r in range(STOPK // 8):
                link(v.max(s8[:], cur[:]))
                if r < STOPK // 8 - 1:
                    link(v.match_replace(swk[:], s8[:], cur[:], FAR))
                    cur = swk
            thr = s8[:, 7:8]
            link(v.tensor_scalar(swk[:], ssc[:], thr, None, ALU.is_gt, ALU.add, accum_out=scount[:, 0:1]))
            link(v.tensor_scalar(scount[:, 1:2], scount[:, 0:1], -1.0, float(STOPK), ALU.mult, ALU.add))
            link(v.tensor_scalar(seq_[:], ssc[:], thr, None, ALU.is_equal))
            link(v.tensor_tensor_scan(scu[:], K.ones[0:DEC, 0:1].to_broadcast([DEC, SKEYS]), seq_[:], 0.0, ALU.mult, ALU.add))
            link(v.scalar_tensor_tensor(scu[:], scu[:], scount[:, 1:2], seq_[:], ALU.is_le, ALU.mult))
            link(v.scalar_tensor_tensor(swk[:], swk[:], -1.0, scu[:], ALU.add, ALU.add))
            v.tensor_scalar(sbias[:], swk[:], -OFF, None, ALU.mult).then_inc(biased, 1)
            dve.wait_ge(pe_logit, 1)
            link(v.tensor_copy(sp_[:], ps[:, 3, 0:SKEYS]))
            link(v.reduce_max(stat[:, 0:1], sp_[:], AX.X))
            v.tensor_scalar(stat[:, 1:2], stat[:, 0:1], -ATT_SCALE, None, ALU.mult).then_inc(max_done, 1)
            dve.wait_ge(exp_done, 1)
            link(v.reciprocal(stat[:, 3:4], stat[:, 2:3]))
            link(v.tensor_scalar(sp_[:], sp_[:], stat[:, 3:4], None, ALU.mult))
            v.tensor_scalar(sdiag[:], K.ident[:], sp_[:, PAST:SKEYS], None, ALU.mult).then_inc(diag_done, 1)
            dve.wait_ge(pe_pT, 1)
            v.tensor_copy(snew[:], ps[0:DEC, 5, 0:P])
            v.tensor_copy(spT[:].rearrange("p j h -> p (j h)"), ps[:, 4, 0:NPAGE * P]).then_inc(pT_done, 1)
            dve.wait_ge(pe_out, 1)
            for p in range(KP):
                for g in range(2):
                    for odd in range(2):
                        kv = 2 * p + g
                        src = ps[HD * g:HD * g + HD, 6 + p, 0:P].rearrange("p (b k a o) -> p k a o b", k=KVH, a=2, o=2)
                        c = v.tensor_copy(T.qT[HD * odd:HD * odd + HD, 2 * kv:2 * kv + 2, SEQ:NT], src[:, kv, :, odd, :])
            c.then_inc(y_done, 1)


def steps(K, S):
    nc, A, ps = K.nc, K.A, K.ps
    NC = TT * HEADS
    W = NC + DEC
    with ExitStack() as ctx:
        def sb(name, shape):
            return ctx.enter_context(nc.sbuf_tensor(name, shape, F32))
        u, e, z, t, p = (sb("dt_" + n, [P, W]) for n in "uezts")
        a_row, a_col = sb("a_row", [P, HEADS]), sb("a_col", [HEADS, 1])
        head_x = sb("head_x", [HEADS, INNER])
        spread = sb("spread", [HEADS, 17])
        d_end = sb("d_end", [P, NC])
        mod = sb("mod3", [9, 4 * D])
        mod_bias = sb("mod_bias", [9, 4 * D])
        gate_sb = sb("gate_sb", [P, 4, D])
        mod_done = K.sem("mod_done")
        mod_in, modT_ps, modT_step = K.sem("mod3_in"), K.sem("modT_in_psum"), K.sem("modT_step")
        gate_ps, gate_done, gate_out = K.sem("gate_in_psum"), K.sem("gate_done"), K.sem("gate_stored")
        head_in, step = K.sem("head_in"), K.sem("dt_step")
        arg_ready, exp_done, a_done = K.sem("dt_arg"), K.sem("dt_exp"), K.sem("a_exp")
        dta_done, sums, decays = K.sem("dta_done"), K.sem("decay_sums"), K.sem("decays_done")
        sdec_arg, sdec, spread_ps = K.sem("sdecay_arg"), K.sem("sdecay_done"), K.sem("spread_in_psum")
        block = ctx.enter_context(nc.Block())

        @block.sync
        def _(sp):
            sp.dma_start(head_x[:], A["k_head"]).then_inc(head_in, 16)
            sp.dma_start(mod[:], A["s_mod"]).then_inc(mod_in, 16)
            sp.dma_start(mod_bias[:], A["b_ada"][0, 2 * D:6 * D].partition_broadcast(9)).then_inc(mod_in, 16)
            sp.wait_ge(gate_done, 4)
            for b in range(4):
                r = P if b % 2 == 0 else DEC
                sp.dma_start(A["s_gates"][b, 0:r, :], gate_sb[0:r, b, :]).then_inc(gate_out, 16)
            sp.wait_ge(gate_out, 64)

        @block.scalar
        def _(act):
            nc.scalar.activation(a_row[:], K.heads_row[:, 1, :], ACT.Exp).then_inc(a_done, 1)
            nc.scalar.activation(a_col[:], K.heads_col[:, 1:2], ACT.Exp).then_inc(a_done, 1)
            act.wait_ge(arg_ready, 1)
            nc.scalar.activation(e[:], e[:], ACT.Exp).then_inc(exp_done, 1)
            act.wait_ge(sdec_arg, 1)
            nc.scalar.activation(spread[:, 0:DEC], spread[:, 0:DEC], ACT.Exp).then_inc(sdec, 1)
            act.wait_ge(sums, 1)
            for bank, dst in ((0, S.e_acs[:].rearrange("p c h -> p (c h)")), (1, d_end[:]),
                              (2, S.c_dec[:].rearrange("p c h -> p (c h)"))):
                nc.scalar.activation(dst, ps[:, bank, 0:NC], ACT.Exp).then_inc(decays, 1)
            for b in range(4):
                r, bank = P if b % 2 == 0 else DEC, 4 + 2 * (b % 2)
                act.wait_ge(gate_ps, b + 1)
                nc.scalar.copy(gate_sb[0:r, b, :], ps[0:r, bank:bank + 2, :].rearrange("p a n -> p (a n)")).then_inc(gate_done, 1)

        @block.gpsimd
        def _(pool):
            pool.wait_ge(mod_in, 32)
            for c0, n in ((D, 2 * D), (0, D), (3 * D, D)):
                cols = slice(c0, c0 + n)
                nc.gpsimd.tensor_tensor(mod[:, cols], mod[:, cols], mod_bias[:, cols], ALU.add).then_inc(mod_done, 1)

        @block.tensor
        def _(pe):
            pe.wait_ge(mod_done, 1)
            for a, part in enumerate((1, 2)):
                for k in range(KB):
                    mm = nc.tensor.transpose(ps[:, 3, 272 + (8 * a + k) * 9:272 + (8 * a + k) * 9 + 9],
                                             mod[:, D * part + P * k:D * part + P * k + P], K.ident[0:9, 0:9])
            mm.then_inc(modT_ps, 1)

            def gates(b):
                base, r, bank = (0 if b < 2 else 3 * D), (P if b % 2 == 0 else DEC), 4 + 2 * (b % 2)
                who = K.ident[0:9, 0:1].to_broadcast([9, P]) if b % 2 == 0 else K.ident[0:9, 1:9]
                for h in range(2):
                    mm = nc.tensor.matmul(ps[0:r, bank + h, :], who, mod[:, base + 512 * h:base + 512 * h + 512],
                                          start=True, stop=True)
                mm.then_inc(gate_ps, 1)

            pe.wait_ge(mod_done, 2)
            gates(0)
            gates(1)
            pe.wait_ge(dta_done, 1)
            dta = S.dta[:].rearrange("p c h -> p (c h)")
            nc.tensor.matmul(ps[:, 0, 0:NC], K.le[:], dta, start=True, stop=True)
            nc.tensor.matmul(ps[:, 1, 0:NC], K.gt[:], dta, start=True, stop=True)
            nc.tensor.matmul(ps[:, 2, 0:NC], K.ones[:], dta, start=True, stop=True).then_inc(sums, 1)
            pe.wait_ge(sdec, 1)
            pe.wait_ge(head_in, 16)
            pe.wait_ge(modT_step, 1)
            for b in range(INNER // P):
                mm = nc.tensor.matmul(ps[:, 3, 17 * b:17 * b + 17], head_x[:, P * b:P * b + P], spread[:],
                                      start=True, stop=True)
            mm.then_inc(spread_ps, 1)
            pe.wait_ge(mod_done, 3)
            for b in (2, 3):
                pe.wait_ge(gate_done, b - 1)
                gates(b)

        @block.vector
        def _(dve):
            n = [0]
            v = nc.vector

            def link(ins):
                n[0] += 1
                ins.then_inc(step, 1)
                dve.wait_ge(step, n[0])

            link(v.memset(u[:, NC:W], 0.0))
            link(v.tensor_tensor(u[:, 0:NC].rearrange("p (c h) -> p c h", h=HEADS), K.dt_raw[:],
                                 K.heads_row[:, 0, :].unsqueeze(1).to_broadcast([P, TT, HEADS]), ALU.add))
            link(v.tensor_scalar(u[0:HEADS, NC:W], K.dtT_raw[:], K.heads_col[:, 0:1], None, ALU.add))
            v.scalar_tensor_tensor(e[:], u[:], -1.0, u[:], ALU.mult, ALU.min).then_inc(arg_ready, 1)
            dve.wait_ge(exp_done, 1)
            link(v.tensor_scalar(t[:], e[:], 2.0, None, ALU.add))
            link(v.reciprocal(t[:], t[:]))
            link(v.tensor_tensor(z[:], e[:], t[:], ALU.mult))
            link(v.tensor_tensor(t[:], z[:], z[:], ALU.mult))
            link(v.tensor_scalar(p[:], t[:], 1.0 / 15.0, None, ALU.mult))
            for k in (13, 11, 9, 7, 5, 3):
                link(v.scalar_tensor_tensor(p[:], p[:], 1.0 / k, t[:], ALU.add, ALU.mult))
            link(v.scalar_tensor_tensor(z[:], p[:], 1.0, z[:], ALU.add, ALU.mult))
            link(v.tensor_scalar(u[:], u[:], 0.0, None, ALU.max))
            link(v.scalar_tensor_tensor(u[:], z[:], 2.0, u[:], ALU.mult, ALU.add))
            dve.wait_ge(a_done, 2)
            dt3 = u[:, 0:NC].rearrange("p (c h) -> p c h", h=HEADS)
            link(v.tensor_copy(S.dt[:], dt3))
            link(v.tensor_scalar(a_row[:], a_row[:], -1.0, None, ALU.mult))
            v.tensor_tensor(S.dta[:], dt3, a_row[:].unsqueeze(1).to_broadcast([P, TT, HEADS]), ALU.mult).then_inc(dta_done, 1)
            link(v.tensor_scalar(a_col[:], a_col[:], -1.0, None, ALU.mult))
            link(v.tensor_copy(spread[:, DEC:2 * DEC], u[0:HEADS, NC:W]))
            link(v.tensor_copy(spread[:, 16:17], K.heads_col[:, 2:3]))
            v.tensor_scalar(spread[:, 0:DEC], u[0:HEADS, NC:W], a_col[:], None, ALU.mult).then_inc(sdec_arg, 1)
            dve.wait_ge(decays, 3)
            dve.wait_ge(modT_ps, 1)
            v.tensor_copy(K.modT[:, 2:4].rearrange("p a k s -> p (a k s)"), ps[:, 3, 272:416]).then_inc(modT_step, 1)
            dve.wait_ge(modT_step, 1)
            sc = K.modT[:, 3, :, :]
            v.tensor_scalar(sc, sc, 1.0, None, ALU.add).then_inc(modT_step, 1)
            dve.wait_ge(modT_step, 2)
            v.tensor_tensor(sc, sc, K.vecs[:, 128:136].unsqueeze(2).to_broadcast([P, KB, 9]), ALU.mult)
            link(v.tensor_tensor(S.ddt[:].rearrange("p c h -> p (c h)"), d_end[:], u[:, 0:NC], ALU.mult))
            dve.wait_ge(spread_ps, 1)
            link(v.tensor_copy(S.hx[:].rearrange("p b s -> p (b s)"), ps[:, 3, 0:17 * 16]))


def ssm(K, hT, S):
    nc, A, ps = K.nc, K.A, K.ps
    first = K.span["g0"][0] - 3
    FBS = 6
    PW = CONV - 1 + NT
    with ExitStack() as ctx:
        def sb(name, shape):
            return ctx.enter_context(nc.sbuf_tensor(name, shape, F32))
        pre = sb("pre", [P, 2, PW])
        posts = sb("post", [P, 2, FBS, SEQ])
        z = sb("z", [P, TT, GW])
        tail = sb("tail", [P, FBS, 11])
        tail_rows = sb("tail_rows", [11, FBS, P])
        st_rows = sb("st_rows", [DEC * 3, FBS, P])
        wg = sb("wg", [P, 5, FBS])
        cx, ct = sb("cx", [P, FBS, DEC]), sb("ct", [P, FBS, DEC])
        zs, xdt_s = sb("zs", [P, 4, DEC]), sb("xdt_s", [P, 4, DEC])
        bc_diag = sb("bc_diag", [P, 2, 4, P])
        stt = sb("stt", [P, 4, 4, NST])
        tmp = sb("stmp", [P, 2, 4, NST])
        ysum = sb("ysum", [P, 4, DEC])
        ysq, yrs = sb("ysq", [P, 4, DEC]), sb("yrs", [P, DEC])
        cbm = sb("cbm", [P, 2, P])
        btok = sb("btok", [P, 2, P])
        seg = sb("seg", [P, GH, P])
        m = sb("m", [P, 2, GH, P])
        xt, xdt, xw, xd = sb("xt", [P, GW]), sb("xdt", [P, 2, GW]), sb("xw", [P, 2, GW]), sb("xd", [P, 2, GW])
        y, ysq2 = sb("ssm_y", [P, 2, GW]), sb("ssm_ysq", [P, GW])
        state = sb("state", [P, GW])
        yT = sb("ssm_yT", [P, 2, 4, P])
        stat = sb("ssm_stat", [P, 4, 2])
        fin = sb("fin", [P, 4, P])

        pre_in = [K.sem(f"pre_in{i}") for i in range(2)]
        gemm, pre_done, conv_done, post_done = K.sem("xbc_sums"), K.sem("pre_done"), K.sem("conv_done"), K.sem("post_done")
        conv_step, tails = K.sem("conv_step"), K.sem("tails_kept")
        z_ps, z_done, zs_ps, zs_done = K.sem("z_sums"), K.sem("z_done"), K.sem("zs_sums"), K.sem("zs_done")
        st_in, st_used = K.store_sem("conv_state_in"), K.sem("conv_state_turned")
        rows_ps, rows_done, rows_out = K.sem("tail_rows_in_psum"), K.sem("tail_rows_done"), K.store_sem("tail_rows_stored")
        cs_sum, cs_done = K.sem("sample_conv_sum"), K.sem("sample_conv_done")
        diag, bc_ps, bc_used = K.sem("bc_diag_done"), K.sem("bc_in_psum"), K.sem("bc_used")
        s_in, s_dec, s_new, s_out = K.store_sem("states_in"), K.sem("states_decayed"), K.sem("states_new"), K.store_sem("states_stored")
        sstep, ysq_done, yss_ps, yroot, yrooted = (K.sem(n) for n in (
            "sample_ssm_step", "ysq_done", "ysq_summed", "yroot_arg", "yroot_done"))
        seg_in, seg_ps, m_exp, m_done = K.sem("seg_in"), K.sem("seg_in_psum"), K.sem("m_exp"), K.sem("m_done")
        bcb_ps, cb_done, xt_ps, xt_done = K.sem("cb_b_in_psum"), K.sem("cb_b_done"), K.sem("xt_in_psum"), K.sem("xt_done")
        xdt_done, xw_done, xd_done = K.sem("xdt_done"), K.sem("xw_done"), K.sem("xd_done")
        yd_ps, yo_ps, sp_ps = K.sem("ydiag_in_psum"), K.sem("yoff_in_psum"), K.sem("state_in_psum")
        yo_done, s_scaled, s_done, yd_done = K.sem("yoff_done"), K.sem("state_decayed"), K.sem("state_done"), K.sem("ydiag_done")
        ystep, ygated, ysquared, ymean, yroot2, ynormed = (K.sem(n) for n in (
            "y_step", "y_gated", "y_squared", "y_mean", "y_root", "y_normed"))
        yT_ps, yT_done, yT_out = K.sem("ssm_yT_in_psum"), K.sem("ssm_yT_done"), [K.store_sem(f"ssm_yT_stored{i}") for i in range(2)]
        fin_ps, fin_done, fin_out = K.sem("final_in_psum"), K.sem("final_done"), K.store_sem("final_stored")
        old_out = K.store_sem("old_conv_rows_stored")
        block = ctx.enter_context(nc.Block())

        here = [3, 3, 2, 2, 2, 2, 2, 2]
        before = [sum(here[:c]) for c in range(TT + 1)]
        blocks_at = [[f for f in range(FBS) if before[c] < 3 * f + 3 <= before[c + 1]] for c in range(TT)]

        def feature(g, f):
            return 4 * g + f if f < 4 else (16 + g if f == 4 else 20 + g)

        def slab(g, i):
            return first + 5 * g + i

        def states(g, q, name):
            heads = A[name][0, 4 * q:4 * q + 4, GH * g:GH * g + GH]
            return heads.rearrange("b h p n -> b (h p) n").rearrange("b (k q) n -> q b k n", q=P)

        @block.sync
        def _(sp):
            def load_slab(g, i):
                n = slab(g, i) + RING
                if n < len(K.slabs):
                    sp.wait_ge(*((gemm, 18 * (g - 1) + 6 * (i + 1)) if i < 3 else (zs_ps, 2 * g + i - 2)))
                    for place, src in K.slabs[n]:
                        sp.dma_start(place(K.ring[:, n % RING, :]), src).then_inc(K.landed[n % RING], 16)

            def load_conv_rows(g):
                for f in range(FBS):
                    c = P * feature(g, f)
                    sp.dma_start(st_rows[:, f, :], A["state_conv"][0, :, :, c:c + P].rearrange("b j c -> (b j) c"))\
                        .then_inc(st_in, 16)

            def load_states(h):
                for b in range(4):
                    sp.dma_start(stt[:, b], states(h // 2, h % 2, "state_ssm")[:, b]).then_inc(s_in, 16)

            def exchange_states(h):
                sp.wait_ge(s_new, h + 1)
                for b in range(4):
                    sp.dma_start(states(h // 2, h % 2, "ssm_sample")[:, b], stt[:, b]).then_inc(s_out, 16)
                if h + 1 < 2 * GROUPS:
                    sp.wait_ge(s_out, 16 * 4 * (h + 1))
                    sp.wait_ge(bc_used, h + 1)
                    load_states(h + 1)

            sp.dma_start(A["conv_sample"][0, :, 0:2, :], A["state_conv"][0, :, 1:3, :]).then_inc(old_out, 16)
            load_conv_rows(0)
            load_states(0)
            for f in range(FBS):
                if f >= 2:
                    sp.wait_ge(conv_done, f - 1)
                    sp.wait_ge(tails, f - 1)
                sp.dma_start(pre[:, f % 2, CONV - 1:PW], A["s_xbc"][f]).then_inc(pre_in[f % 2], 16)
            for g in range(GROUPS):
                sp.wait_ge(rows_done, 2 * (g + 1))
                for f in range(FBS):
                    c = P * feature(g, f)
                    sp.dma_start(A["conv_prompt"][0, 0, :, c:c + P], tail_rows[0:3, f, :]).then_inc(rows_out, 16)
                    sp.dma_start(A["conv_sample"][0, :, 2, c:c + P], tail_rows[3:11, f, :]).then_inc(rows_out, 16)
                if g + 1 < GROUPS:
                    sp.wait_ge(st_used, g + 1)
                    load_conv_rows(g + 1)
                load_slab(g, 3)
                exchange_states(2 * g)
                load_slab(g, 4)
                exchange_states(2 * g + 1)
                if g + 1 < GROUPS:
                    for i in range(3):
                        load_slab(g + 1, i)
            sp.wait_ge(s_out, 16 * 8 * GROUPS)
            sp.wait_ge(rows_out, 16 * 2 * FBS * GROUPS)
            sp.wait_ge(old_out, 16)

        @block.gpsimd
        def _(pool):
            v = nc.gpsimd
            v.memset(pre[:, :, 0:CONV - 1], 0.0).then_inc(conv_step, 1)
            def store(g, c):
                pool.wait_ge(yT_done, TT * g + c + 1)
                pool.dma_start(A["s_ssm"].rearrange("k p n -> p k n")[:, 4 * g:4 * g + 4, P * c:P * c + P],
                               yT[:, c % 2]).then_inc(yT_out[c % 2], 16)

            def segments(g, c):
                n = TT * g + c
                if n:
                    pool.wait_ge(seg_ps, n)
                v.tensor_tensor(seg[:], K.le[:].unsqueeze(1).to_broadcast([P, GH, P]),
                                S.dta[:, c, GH * g:GH * g + GH].unsqueeze(2).to_broadcast([P, GH, P]), ALU.mult)\
                    .then_inc(seg_in, 1)

            for g in range(GROUPS):
                for q in range(2):
                    h = 2 * g + q
                    pool.wait_ge(cs_done, g + 1)
                    if h:
                        pool.wait_ge(bc_ps, 2 * h)
                    for k in range(2):
                        v.tensor_tensor(bc_diag[:, k], K.ident[:].unsqueeze(1).to_broadcast([P, 4, P]),
                                        cx[:, 4 + k, 4 * q:4 * q + 4].unsqueeze(2).to_broadcast([P, 4, P]), ALU.mult)\
                            .then_inc(diag, 1)
                    pool.wait_ge(s_in, 16 * 4 * (h + 1))
                    for b in range(4):
                        d = v.tensor_tensor(stt[:, b], stt[:, b],
                                            S.hx[:, 4 * g:4 * g + 4, 4 * q + b].unsqueeze(2).to_broadcast([P, 4, NST]),
                                            ALU.mult)
                    d.then_inc(s_dec, 1)
                segments(g, 0)
                for c in range(TT):
                    n = TT * g + c
                    pool.wait_ge(xt_done, n + 1)
                    if n >= 2:
                        pool.wait_ge(sp_ps, n - 1)
                        pool.wait_ge(yd_done, 2 * (n - 1))
                    xh = xt[:].rearrange("p (h d) -> p h d", d=HD)

                    def per_head(vec):
                        return vec.unsqueeze(2).to_broadcast([P, GH, HD])
                    v.tensor_tensor(xw[:, c % 2].rearrange("p (h d) -> p h d", d=HD), xh,
                                    per_head(S.ddt[:, c, GH * g:GH * g + GH]), ALU.mult).then_inc(xw_done, 1)
                    v.tensor_tensor(xd[:, c % 2].rearrange("p (h d) -> p h d", d=HD), xh,
                                    per_head(K.heads_row[:, 2, GH * g:GH * g + GH]), ALU.mult).then_inc(xd_done, 1)
                    if c + 1 < TT:
                        segments(g, c + 1)
                    if c >= 2:
                        store(g, c - 2)
                store(g, TT - 2)
                store(g, TT - 1)
                pool.wait_ge(fin_done, g + 1)
                pool.dma_start(A["ssm_prompt"][0, 0].rearrange("h p n -> (h p) n")[GW * g:GW * g + GW]
                               .rearrange("(k q) n -> q k n", q=P), fin[:]).then_inc(fin_out, 16)
            for i in range(2):
                pool.wait_ge(yT_out[i], 8 * TT * GROUPS)
            pool.wait_ge(fin_out, 16 * GROUPS)

        @block.tensor
        def _(pe):
            tr, mm = nc.tensor.transpose, nc.tensor.matmul

            def unit(g, j):
                f, c, u = j // TC, j % TC, FBS * TC * (g - 1) + j
                if j % (2 * TC) == 0:
                    pe.wait_ge(*ring_landed(K, slab(g, f // 2)))
                if u >= 2:
                    pe.wait_ge(pre_done, u - 1)
                w = slab_of(K, slab(g, f // 2))
                for k in range(KB):
                    a = mm(ps[:, 6 + u % 2, 0:CW], w[:, k, P * (f % 2):P * (f % 2) + P],
                           hT[:, k, CW * c:CW * c + CW], start=(k == 0), stop=(k == KB - 1))
                a.then_inc(gemm, 1)

            def front(g, c):
                n = TT * g + c
                post = posts[:, g % 2]
                cols = slice(P * c, P * c + P)
                if c == 0:
                    pe.wait_ge(post_done, FBS * (g + 1))
                if n:
                    pe.wait_ge(cb_done, 2 * n)
                if g and c == 0:
                    pe.wait_ge(yT_done, n)
                    pe.wait_ge(s_done, n)
                if c >= 2:
                    pe.wait_ge(yT_done, n - 2)
                    pe.wait_ge(s_done, n - 1)
                tr(ps[:, 0, P:2 * P], post[:, 4, cols], K.ident[:])
                mm(ps[:, 0, 0:P], post[:, 4, cols], post[:, 5, cols], start=True, stop=True).then_inc(bcb_ps, 1)
                if n:
                    pe.wait_ge(xt_done, n)
                    pe.wait_ge(xdt_done, n)
                for j in range(4):
                    t = tr(ps[:, 3, P * j:P * j + P], post[:, j, cols], K.ident[:])
                t.then_inc(xt_ps, 1)
                pe.wait_ge(seg_in, n + 1)
                if n:
                    pe.wait_ge(m_exp, n)
                for half in range(2):
                    s = mm(ps[:, 1 + half, :], K.gt[:], seg[:, 4 * half:4 * half + 4, :].rearrange("p h l -> p (h l)"),
                           start=True, stop=True)
                s.then_inc(seg_ps, 1)

            def back(g, c):
                n = TT * g + c
                post = posts[:, g % 2]
                cols = slice(P * c, P * c + P)
                pe.wait_ge(m_done, n + 1)
                pe.wait_ge(xdt_done, n + 1)
                if n:
                    pe.wait_ge(yd_done, 2 * n)
                for r in range(GH):
                    d = mm(ps[:, 5, HD * r:HD * r + HD], m[:, c % 2, r, :], xdt[:, c % 2, HD * r:HD * r + HD],
                           start=True, stop=True)
                d.then_inc(yd_ps, 1)
                if c:
                    pe.wait_ge(s_done, n)
                    if n > 1:
                        pe.wait_ge(yo_done, n - g - 1)
                    mm(ps[:, 4, :], post[:, 5, cols], state[:], start=True, stop=True).then_inc(yo_ps, 1)
                pe.wait_ge(xw_done, n + 1)
                pe.wait_ge(cb_done, 2 * n + 2)
                ahead = n + 2 if c + 1 < TT else n + 1
                pe.wait_ge(xt_done, ahead)
                pe.wait_ge(xdt_done, ahead)
                if c == TT - 1:
                    pe.wait_ge(s_done, n)
                mm(ps[:, 3, :], btok[:, c % 2, :], xw[:, c % 2, :], start=True, stop=True).then_inc(sp_ps, 1)

            def turn(g, c):
                n = TT * g + c
                pe.wait_ge(ynormed, n + 1)
                pe.wait_ge(cb_done, 2 * min(n + 3, TT * (g + 1)))
                if c == TT - 1:
                    pe.wait_ge(yT_done, n)
                for j in range(4):
                    t = tr(ps[:, 0, P * j:P * j + P], y[:, c % 2, P * j:P * j + P], K.ident[:])
                t.then_inc(yT_ps, 1)

            def z_unit(g, u):
                i, t, w = u // TT, u % TT, slab_of(K, slab(g, 3 + u // TT))
                if t == 0:
                    pe.wait_ge(*ring_landed(K, slab(g, 3 + i)))
                if u + g >= 2:
                    pe.wait_ge(z_done, 2 * TT * g + u - 1)
                if g and u == 0:
                    pe.wait_ge(m_exp, TT * g)
                for k in range(KB):
                    a = mm(ps[:, 1 + u % 2, 0:256], hT[:, k, P * t:P * t + P], w[:, k, :], start=(k == 0), stop=(k == KB - 1))
                a.then_inc(z_ps, 1)

            def z_samples(g, i):
                w = slab_of(K, slab(g, 3 + i))
                if g:
                    pe.wait_ge(fin_done, g)
                for fb in range(2):
                    for k in range(KB):
                        a = mm(ps[:, 4, DEC * (2 * i + fb):DEC * (2 * i + fb) + DEC], w[:, k, P * fb:P * fb + P],
                               hT[:, k, SEQ:NT], start=(k == 0), stop=(k == KB - 1))
                a.then_inc(zs_ps, 1)

            def raw_rows(g):
                pe.wait_ge(st_in, 16 * FBS * (g + 1))
                if g:
                    pe.wait_ge(yd_done, 2 * TT * g)
                for f in range(FBS):
                    t = tr(ps[:, 5, 24 * f:24 * f + 24], st_rows[:, f, :], K.ident[0:24, 0:24])
                t.then_inc(st_used, 1)
                if g:
                    pe.wait_ge(pre_done, 18 * g)
                pe.wait_ge(tails, FBS * (g + 1))
                for f in range(FBS):
                    t = tr(ps[0:11, 6 + f // 3, P * (f % 3):P * (f % 3) + P], tail[:, f, :], K.ident[:])
                t.then_inc(rows_ps, 1)

            def spread(g, q):
                h = 2 * g + q
                pe.wait_ge(diag, 2 * h + 2)
                if q == 0:
                    pe.wait_ge(rows_done, 2 * (g + 1))
                else:
                    pe.wait_ge(bc_used, h)
                for k in range(2):
                    mm(ps[:, 6 + k, :], K.ones[:], bc_diag[:, k].rearrange("p b n -> p (b n)"),
                       start=True, stop=True).then_inc(bc_ps, 1)

            def final_state(g):
                pe.wait_ge(s_done, TT * (g + 1))
                for j in range(4):
                    t = tr(ps[:, 4, P * j:P * j + P], state[:, P * j:P * j + P], K.ident[:])
                t.then_inc(fin_ps, 1)

            for g in range(GROUPS):
                raw_at, spread_at = (1, 4) if g else (10, 13)
                for u in range(2 * TT):
                    z_unit(g, u)
                    if u == 0 and g:
                        turn(g - 1, TT - 1)
                        final_state(g - 1)
                    if u == raw_at:
                        raw_rows(g)
                    if u == spread_at:
                        spread(g, 0)
                    if g and u == 12:
                        spread(g, 1)
                    if u % TT == TT - 1:
                        z_samples(g, u // TT)
                if g == 0:
                    spread(g, 1)
                pe.wait_ge(ysq_done, g + 1)
                for j in range(4):
                    a = mm(ps[:, 5, 0:DEC], K.ones[:], ysq[:, j, :], start=(j == 0), stop=(j == 3))
                a.then_inc(yss_ps, 1)
                pe.wait_ge(z_done, 16 * (g + 1))
                pe.wait_ge(zs_done, g + 1)
                pe.wait_ge(bc_used, 2 * (g + 1))
                pe.wait_ge(yroot, g + 1)
                front(g, 0)
                for c in range(TT):
                    if c + 1 < TT:
                        front(g, c + 1)
                    if g + 1 < GROUPS:
                        for j in range(before[c], before[c + 1] - 1):
                            unit(g + 1, j)
                    back(g, c)
                    if c:
                        turn(g, c - 1)
                    if g + 1 < GROUPS:
                        unit(g + 1, before[c + 1] - 1)
            turn(GROUPS - 1, TT - 1)
            final_state(GROUPS - 1)

        @block.scalar
        def _(act):
            a = nc.scalar
            def silu(g, f):
                act.wait_ge(conv_done, FBS * g + f + 1)
                a.activation(posts[:, g % 2, f, :], posts[:, g % 2, f, :], ACT.Silu).then_inc(post_done, 1)

            first_silu = [3, 5, 6, 8, 9, 11]

            def keep(g, j):
                f, c, u = j // TC, j % TC, FBS * TC * (g - 1) + j
                act.wait_ge(gemm, u + 1)
                if c == 0 and FBS * g + f >= 2:
                    act.wait_ge(conv_done, FBS * g + f - 1)
                    act.wait_ge(tails, FBS * g + f - 1)
                a.copy(pre[:, f % 2, CONV - 1 + CW * c:CONV - 1 + CW * c + CW], ps[:, 6 + u % 2, 0:CW]).then_inc(pre_done, 1)

            def decay(g, c):
                n = TT * g + c
                act.wait_ge(xt_ps, n + 1)
                if n:
                    act.wait_ge(xd_done, n)
                a.copy(xt[:], ps[:, 3, :]).then_inc(xt_done, 1)
                act.wait_ge(seg_ps, n + 1)
                if n >= 2:
                    act.wait_ge(yd_ps, n - 1)
                a.activation(m[:, c % 2].rearrange("p h l -> p (h l)"), ps[:, 1:3, :].rearrange("p a n -> p (a n)"),
                             ACT.Exp).then_inc(m_exp, 1)

            def norm(g, c):
                n = TT * g + c
                act.wait_ge(ygated, n + 1)
                if n:
                    act.wait_ge(ysquared, n)
                a.activation(ysq2[:], y[:, c % 2, :], ACT.Square, accum_out=stat[:, 0, c % 2:c % 2 + 1])\
                    .then_inc(ysquared, 1)
                act.wait_ge(ymean, n + 1)
                a.activation(stat[:, 2, c % 2:c % 2 + 1], stat[:, 1, c % 2:c % 2 + 1], ACT.Sqrt).then_inc(yroot2, 1)

            def out(g, c):
                n = TT * g + c
                act.wait_ge(yT_ps, n + 1)
                if n >= 2:
                    act.wait_ge(yT_out[c % 2], 16 * (n // 2))
                for j in range(4):
                    k = 136 + 4 * g + j
                    o = a.activation(yT[:, c % 2, j, :], ps[:, 0, P * j:P * j + P], ACT.Copy, scale=K.vecs[:, k:k + 1])
                o.then_inc(yT_done, 1)

            def keep_final(g):
                act.wait_ge(fin_ps, g + 1)
                if g:
                    act.wait_ge(fin_out, 16 * g)
                a.copy(fin[:].rearrange("p k n -> p (k n)"), ps[:, 4, :]).then_inc(fin_done, 1)

            for g in range(GROUPS):
                for u in range(2 * TT):
                    i, t = u // TT, u % TT
                    act.wait_ge(z_ps, 2 * TT * g + u + 1)
                    if g and u == 0:
                        act.wait_ge(ygated, TT * g)
                    a.activation(z[:, t, 256 * i:256 * i + 256], ps[:, 1 + u % 2, 0:256], ACT.Silu).then_inc(z_done, 1)
                    if u == 0 and g:
                        out(g - 1, TT - 1)
                        keep_final(g - 1)
                    if g == 0 and u in first_silu:
                        silu(0, first_silu.index(u))
                    if u == (1 if g else 10):
                        act.wait_ge(rows_ps, g + 1)
                        if g:
                            act.wait_ge(rows_out, 16 * 2 * FBS * g)
                        for half in range(2):
                            a.copy(tail_rows[:, 3 * half:3 * half + 3, :].rearrange("p f c -> p (f c)"),
                                   ps[0:11, 6 + half, 0:3 * P]).then_inc(rows_done, 1)
                        act.wait_ge(cs_sum, g + 1)
                        a.activation(cx[:], ct[:], ACT.Silu).then_inc(cs_done, 1)
                act.wait_ge(zs_ps, 2 * g + 2)
                a.activation(zs[:].rearrange("p b s -> p (b s)"), ps[:, 4, 0:4 * DEC], ACT.Silu).then_inc(zs_done, 1)
                act.wait_ge(yroot, g + 1)
                a.activation(yrs[:], yrs[:], ACT.Sqrt).then_inc(yrooted, 1)

                decay(g, 0)
                for c in range(TT):
                    if c + 1 < TT:
                        decay(g, c + 1)
                    units = list(range(before[c], before[c + 1])) if g + 1 < GROUPS else []
                    if units and c:
                        for f in blocks_at[c - 1]:
                            silu(g + 1, f)
                    for j in units[:-1]:
                        keep(g + 1, j)
                    if c:
                        out(g, c - 1)
                    for j in units[-1:]:
                        keep(g + 1, j)
                    norm(g, c)
                if g + 1 < GROUPS:
                    for f in blocks_at[TT - 1]:
                        silu(g + 1, f)
            out(GROUPS - 1, TT - 1)
            keep_final(GROUPS - 1)

        @block.vector
        def _(dve):
            v = nc.vector
            nconv, nss, ny = [0], [0], [0]

            def link(ins, sem, count):
                count[0] += 1
                ins.then_inc(sem, 1)
                dve.wait_ge(sem, count[0])

            nconv[0] = 1

            def convolve(g, f):
                b, post, src = feature(g, f), posts[:, g % 2, f, :], pre[:, f % 2, :]
                if g:
                    dve.wait_ge(pre_done, 18 * (g - 1) + 3 * f + 3)
                else:
                    dve.wait_ge(pre_in[f % 2], 16 * (f // 2 + 1))
                if g == 0 and f == 0:
                    dve.wait_ge(conv_step, 1)
                if g and f == 0:
                    dve.wait_ge(rows_ps, g)
                v.tensor_copy(tail[:, f, :], src[:, SEQ:PW]).then_inc(tails, 1)
                link(v.tensor_scalar(post, src[:, 0:SEQ], K.vecs[:, b:b + 1], K.vecs[:, 96 + b:97 + b], ALU.mult, ALU.add),
                     conv_step, nconv)
                for i in range(1, CONV):
                    ins = v.scalar_tensor_tensor(post, src[:, i:i + SEQ], K.vecs[:, 24 * i + b:24 * i + b + 1], post,
                                                 ALU.mult, ALU.add)
                    if i < CONV - 1:
                        link(ins, conv_step, nconv)
                    else:
                        ins.then_inc(conv_done, 1)

            for f in range(FBS):
                convolve(0, f)
            for g in range(GROUPS):
                allv = K.vecs[:, 0:120].rearrange("p (i b) -> p i b", b=24)
                v.tensor_copy(wg[:, :, 0:4], allv[:, :, 4 * g:4 * g + 4])
                v.tensor_copy(wg[:, :, 4:5], allv[:, :, 16 + g:17 + g])
                link(v.tensor_copy(wg[:, :, 5:6], allv[:, :, 20 + g:21 + g]), sstep, nss)
                dve.wait_ge(st_used, g + 1)
                dve.wait_ge(tails, FBS * (g + 1))
                if g:
                    dve.wait_ge(cs_done, g)

                def tap(i):
                    return wg[:, i, :].unsqueeze(2).to_broadcast([P, FBS, DEC])
                old = ps[:, 5, 0:24 * FBS].rearrange("p (f b j) -> p f b j", f=FBS, j=3)
                link(v.tensor_tensor(ct[:], tail[:, :, 3:11], tap(3), ALU.mult), sstep, nss)
                link(v.tensor_tensor(ct[:], ct[:], tap(4), ALU.add), sstep, nss)
                for i in range(3):
                    w8 = tmp[:, 0, 0, 0:FBS * DEC].rearrange("p (f b) -> p f b", f=FBS)
                    link(v.tensor_tensor(w8, old[:, :, :, i], tap(i), ALU.mult), sstep, nss)
                    ins = v.tensor_tensor(ct[:], ct[:], w8, ALU.add)
                    if i < 2:
                        link(ins, sstep, nss)
                    else:
                        ins.then_inc(cs_sum, 1)
                dve.wait_ge(cs_done, g + 1)
                hx = S.hx[:, 4 * g:4 * g + 4, :]
                link(v.tensor_tensor(xdt_s[:], cx[:, 0:4, :], hx[:, :, 8:16], ALU.mult), sstep, nss)
                for q in range(2):
                    h = 2 * g + q
                    dve.wait_ge(bc_ps, 2 * h + 2)
                    dve.wait_ge(s_dec, h + 1)
                    for b in range(0, 4, 2):
                        for i in (b, b + 1):
                            bb = ps[:, 6, P * i:P * i + P].unsqueeze(1).to_broadcast([P, 4, NST])
                            t = v.tensor_tensor(tmp[:, i % 2], bb,
                                                xdt_s[:, :, 4 * q + i].unsqueeze(2).to_broadcast([P, 4, NST]), ALU.mult)
                        link(t, sstep, nss)
                        t = v.tensor_tensor(stt[:, b:b + 2], stt[:, b:b + 2], tmp[:], ALU.add)
                        if b == 0:
                            link(t, sstep, nss)
                    t.then_inc(s_new, 1)
                    dve.wait_ge(s_new, h + 1)
                    for b in range(0, 4, 2):
                        for i in (b, b + 1):
                            cc = ps[:, 7, P * i:P * i + P].unsqueeze(1).to_broadcast([P, 4, NST])
                            t = v.tensor_tensor(tmp[:, i % 2], cc, stt[:, i], ALU.mult)
                        if b == 0:
                            link(t, sstep, nss)
                        else:
                            t.then_inc(bc_used, 1)
                            dve.wait_ge(bc_used, h + 1)
                        link(v.tensor_reduce(ysum[:, :, 4 * q + b:4 * q + b + 2].rearrange("p k b -> p b k"), tmp[:], AX.X,
                                             ALU.add), sstep, nss)
                link(v.tensor_tensor(xdt_s[:], cx[:, 0:4, :], hx[:, :, 16:17].to_broadcast([P, 4, DEC]), ALU.mult), sstep, nss)
                link(v.tensor_tensor(ysum[:], ysum[:], xdt_s[:], ALU.add), sstep, nss)
                dve.wait_ge(zs_done, g + 1)
                link(v.tensor_tensor(ysum[:], ysum[:], zs[:], ALU.mult), sstep, nss)
                v.tensor_tensor(ysq[:], ysum[:], ysum[:], ALU.mult).then_inc(ysq_done, 1)
                dve.wait_ge(yss_ps, g + 1)
                v.tensor_scalar(yrs[:], ps[:, 5, 0:DEC], 1.0 / GW, EPS, ALU.mult, ALU.add).then_inc(yroot, 1)
                dve.wait_ge(yrooted, g + 1)
                link(v.reciprocal(yrs[:], yrs[:]), sstep, nss)
                link(v.tensor_tensor(ysum[:], ysum[:], yrs[:].unsqueeze(1).to_broadcast([P, 4, DEC]), ALU.mult), sstep, nss)
                ng = K.vecs[:, 136 + 4 * g:140 + 4 * g].unsqueeze(2).to_broadcast([P, 4, DEC])
                link(v.tensor_tensor(S.ysT[:, 4 * g:4 * g + 4, :], ysum[:], ng, ALU.mult), sstep, nss)

                def heads(vec):
                    return vec.unsqueeze(2).to_broadcast([P, GH, HD])

                def front(c):
                    n = TT * g + c
                    dve.wait_ge(bcb_ps, n + 1)
                    if n >= 2:
                        dve.wait_ge(sp_ps, n - 1)
                    v.tensor_tensor(cbm[:, c % 2, :], ps[:, 0, 0:P], K.le[:], ALU.mult).then_inc(cb_done, 1)
                    v.tensor_copy(btok[:, c % 2, :], ps[:, 0, P:2 * P]).then_inc(cb_done, 1)
                    dve.wait_ge(xt_ps, n + 1)
                    dve.wait_ge(xt_done, n + 1)
                    if n >= 2:
                        dve.wait_ge(yd_ps, n - 1)
                    v.tensor_tensor(xdt[:, c % 2, :].rearrange("p (h d) -> p h d", d=HD),
                                    ps[:, 3, :].rearrange("p (h d) -> p h d", d=HD),
                                    heads(S.dt[:, c, GH * g:GH * g + GH]), ALU.mult).then_inc(xdt_done, 1)
                    dve.wait_ge(m_exp, n + 1)
                    dve.wait_ge(cb_done, 2 * n + 2)
                    v.tensor_tensor(m[:, c % 2], m[:, c % 2], cbm[:, c % 2, :].unsqueeze(1).to_broadcast([P, GH, P]),
                                    ALU.mult).then_inc(m_done, 1)

                def back(c):
                    n = TT * g + c
                    yc = y[:, c % 2, :]
                    yh = yc.rearrange("p (h d) -> p h d", d=HD)
                    dve.wait_ge(yd_ps, n + 1)
                    dve.wait_ge(xd_done, n + 1)
                    if n >= 2:
                        dve.wait_ge(yT_ps, n - 1)
                    v.tensor_tensor(yc, ps[:, 5, :], xd[:, c % 2, :], ALU.add).then_inc(yd_done, 2)
                    if c:
                        t = tmp[:, 0].rearrange("p k n -> p (k n)")
                        dve.wait_ge(yo_ps, n - g)
                        v.tensor_tensor(t.rearrange("p (h d) -> p h d", d=HD), ps[:, 4, :].rearrange("p (h d) -> p h d", d=HD),
                                        heads(S.e_acs[:, c, GH * g:GH * g + GH]), ALU.mult).then_inc(yo_done, 1)
                        dve.wait_ge(yo_done, n - g)
                        dve.wait_ge(yd_done, 2 * (n + 1))
                        link(v.tensor_tensor(yc, yc, t, ALU.add), ystep, ny)
                    else:
                        dve.wait_ge(yd_done, 2 * (n + 1))
                    v.tensor_tensor(yc, yc, z[:, c, :], ALU.mult).then_inc(ygated, 1)
                    dve.wait_ge(sp_ps, n + 1)
                    if c == 0:
                        if g:
                            dve.wait_ge(fin_ps, g)
                        v.tensor_copy(state[:], ps[:, 3, :]).then_inc(s_done, 1)
                    else:
                        sh = state[:].rearrange("p (h d) -> p h d", d=HD)
                        dve.wait_ge(s_done, n)
                        v.tensor_tensor(sh, sh, heads(S.c_dec[:, c, GH * g:GH * g + GH]), ALU.mult).then_inc(s_scaled, 1)
                        dve.wait_ge(s_scaled, n - g)
                        v.tensor_tensor(state[:], state[:], ps[:, 3, :], ALU.add).then_inc(s_done, 1)
                    i = c % 2
                    dve.wait_ge(ysquared, n + 1)
                    v.tensor_scalar(stat[:, 1, i:i + 1], stat[:, 0, i:i + 1], 1.0 / GW, EPS, ALU.mult, ALU.add).then_inc(ymean, 1)

                def scale(c):
                    n = TT * g + c
                    i = c % 2
                    dve.wait_ge(yroot2, n + 1)
                    link(v.reciprocal(stat[:, 3, i:i + 1], stat[:, 2, i:i + 1]), ystep, ny)
                    v.tensor_scalar(y[:, i, :], y[:, i, :], stat[:, 3, i:i + 1], None, ALU.mult).then_inc(ynormed, 1)

                front(0)
                for c in range(TT):
                    if c + 1 < TT:
                        front(c + 1)
                    back(c)
                    scale(c)
                    if g + 1 < GROUPS:
                        for f in blocks_at[c]:
                            convolve(g + 1, f)



def second_slabs(A):
    slabs, span = [], {}

    def cols(w, k0, nk, c0, n):
        return w[0, P * k0:P * (k0 + nk), c0:c0 + n].rearrange("(k p) n -> p k n", p=P)

    def add(name, nk, *parts):
        span.setdefault(name, [len(slabs), 0])
        slabs.append((nk, parts))
        span[name][1] = len(slabs)

    for w, k0 in (("w_proj_ssm", 0), ("w_proj_ssm", KB), ("w_proj_attn", 0)):
        for i in range(4):
            add("merge", KB, (0, cols(A[w], k0, KB, 256 * i, 256)))
    for i in range(4):
        add("out", KB, (0, cols(A["w_out"], 0, KB, 256 * i, 256)))
    for f0, nf in ffn_parts():
        for f in range(f0, f0 + nf):
            add("ffn", KB, (0, cols(A["w_ffn_in"], 0, KB, P * f, P)), (P, cols(A["w_ffn_in"], 0, KB, FFN + P * f, P)))
        for h in range(2):
            add("ffn", nf, (0, cols(A["w_ffn_out"], f0, nf, 512 * h, 512)))
    return slabs, span


FPART = 4


def ffn_parts():
    return [(f, min(FPART, FB - f)) for f in range(0, FB, FPART)]


class SplitRing:

    def __init__(self, K, ctx, kept):
        nc = K.nc
        self.nc = nc
        self.slabs, self.span = second_slabs(K.A)
        self.raw = ctx.enter_context(nc.sbuf_tensor("w_raw", [P, 2, SLAB], F32))
        self.hi = ctx.enter_context(nc.sbuf_tensor("w_hi", [P, 2, SLAB], F32R))
        self.lo = ctx.enter_context(nc.sbuf_tensor("w_lo", [P, 2, SLAB], F32R))
        self.landed = [kept("raw_slab_landed0"), kept("raw_slab_landed1")]
        self.hi_done, self.split = kept("w_hi_done"), kept("w_split")

    def load(self, eng, n):
        if n >= len(self.slabs):
            return
        if n >= 2:
            eng.wait_ge(self.split, n - 1)
        nk, parts = self.slabs[n]
        for at, src in parts:
            dst = self.raw[:, n % 2, :].rearrange("p (k n) -> p k n", n=256 if nk == KB else 512)
            w = src.shape[2]
            eng.dma_start(dst[:, 0:nk, at:at + w], src).then_inc(self.landed[n % 2], 16)

    def load_stage(self, eng, stage):
        first, last = self.span[stage]
        for n in range(first + 3, last + 3):
            self.load(eng, n)

    def split_slab(self, pool, n, used=None):
        if n >= len(self.slabs):
            return
        pool.wait_ge(self.landed[n % 2], 16 * sum(len(self.slabs[m][1]) for m in range(n % 2, n + 1, 2)))
        if used:
            pool.wait_ge(*used)
        w = self.slabs[n][0] * (256 if self.slabs[n][0] == KB else 512)
        raw, hi, lo = (a[:, n % 2, 0:w] for a in (self.raw, self.hi, self.lo))
        self.nc.gpsimd.tensor_copy(hi, raw).then_inc(self.hi_done, 1)
        pool.wait_ge(self.hi_done, n + 1)
        self.nc.gpsimd.tensor_tensor(lo, raw, hi.bitcast(F32), ALU.subtract).then_inc(self.split, 1)

    def split_stage(self, pool, stage, used):
        first, last = self.span[stage]
        for n in range(first + 1, last + 1):
            self.split_slab(pool, n, used(n - 2 - first) if n - 2 >= first else None)

    def pair(self, n):
        nw = 256 if self.slabs[n][0] == KB else 512
        return [a[:, n % 2, :].rearrange("p (k n) -> p k n", n=nw) for a in (self.hi, self.lo)]


def product(nc, out, terms):
    for i, (ah, al, bh, bl) in enumerate(terms):
        nc.tensor.matmul(out, ah, bl, start=(i == 0), stop=False)
        nc.tensor.matmul(out, ah, bh, start=False, stop=False)
        mm = nc.tensor.matmul(out, al, bh, start=False, stop=(i == len(terms) - 1))
    return mm


def merge(K, W, merged):
    nc, A, ps = K.nc, K.A, K.ps
    first = W.span["merge"][0]
    PU = KB * TC
    NU = 3 * PU
    with ExitStack() as ctx:
        def sb(name, shape, dt=F32):
            return ctx.enter_context(nc.sbuf_tensor(name, shape, dt))
        raw = sb("m_raw", [P, 2, KB, CW])
        hi, lo = sb("m_hi", [P, 4, KB, CW], F32R), sb("m_lo", [P, 4, KB, CW], F32R)
        sig = sb("m_sig", [P, 2, NT])
        part = sb("m_part", [P, 2, CW])
        raw_in, sig_in = [K.sem(f"m_raw_in{i}") for i in range(2)], [K.sem(f"m_sig_in{i}") for i in range(2)]
        hi_done, split = K.sem("m_hi_done"), K.sem("m_split")
        gemm, freed, done = K.sem("m_sums"), K.sem("m_bank_free"), K.sem("m_done")
        block = ctx.enter_context(nc.Block())

        def sample_parts(q):
            return 2 if q % TC == TC - 1 and q // TC < 2 else 1

        @block.sync
        def _(sp):
            for n in range(3):
                W.load(sp, n)
            W.load_stage(sp, "merge")

        @block.gpsimd
        def _(pool):
            W.split_slab(pool, first)
            W.split_stage(pool, "merge", lambda i: (gemm, 2 * TC * (i + 1)))

        @block.scalar
        def _(act):
            def load(q):
                s, c = q // TC, q % TC
                if q >= 2:
                    act.wait_ge(split, q - 1)
                w = CW - (DEC if sample_parts(q) == 2 else 0)
                src = A["s_ssm"][KB * s:KB * s + KB] if s < 2 else A["s_att"]
                act.dma_start(raw[:, q % 2, :, 0:w], src.rearrange("k p n -> p k n")[:, :, CW * c:CW * c + w])\
                    .then_inc(raw_in[q % 2], 16)
                if w < CW:
                    act.dma_start(raw[:, q % 2, :, w:CW], K.ysT[:, KB * s:KB * s + KB, :]).then_inc(raw_in[q % 2], 16)

            def round_chunk(q):
                act.wait_ge(raw_in[q % 2], 16 * sum(sample_parts(m) for m in range(q % 2, q + 1, 2)))
                nc.scalar.copy(hi[:, q % 4].rearrange("p k n -> p (k n)"),
                               raw[:, q % 2].rearrange("p k n -> p (k n)")).then_inc(hi_done, 1)
                if q + 2 < 3 * TC:
                    load(q + 2)

            def load_sig(b):
                act.dma_start(sig[:, b % 2, :], A["s_sig"][b]).then_inc(sig_in[b % 2], 16)

            load(0)
            load(1)
            load_sig(0)
            load_sig(1)
            for q in range(4):
                round_chunk(q)
            for u in range(NU):
                s, b, c = u // PU, u // TC % KB, u % TC
                if b == KB - 1 and TC * s + c + 4 < 3 * TC:
                    act.wait_ge(gemm, u + 1)
                    round_chunk(TC * s + c + 4)
                if s and c == TC - 1 and KB * (s - 1) + b + 2 < 2 * KB:
                    act.wait_ge(done, u + 1 - PU)
                    load_sig(KB * (s - 1) + b + 2)

        @block.tensor
        def _(pe):
            for u in range(NU):
                s, b, c = u // PU, u // TC % KB, u % TC
                n, q = first + u // (2 * TC), TC * s + c
                if u % (2 * TC) == 0:
                    pe.wait_ge(W.split, n + 1)
                if b == 0:
                    pe.wait_ge(split, q + 1)
                if u >= 8:
                    pe.wait_ge(freed, u - 7)
                wh, wl = W.pair(n)
                cols = slice(P * (b % 2), P * (b % 2) + P)
                product(nc, ps[:, u % 8, 0:CW], [(wh[:, k, cols], wl[:, k, cols], hi[:, q % 4, k, :], lo[:, q % 4, k, :])
                                                 for k in range(KB)]).then_inc(gemm, 1)

        @block.vector
        def _(dve):
            v = nc.vector

            def rest(q):
                dve.wait_ge(hi_done, q + 1)
                flat = "p k n -> p (k n)"
                v.tensor_tensor(lo[:, q % 4].rearrange(flat), raw[:, q % 2].rearrange(flat),
                                hi[:, q % 4].rearrange(flat).bitcast(F32), ALU.subtract).then_inc(split, 1)

            for q in range(4):
                rest(q)
            for u in range(NU):
                s, b, c = u // PU, u // TC % KB, u % TC
                if u and (u - 1) // TC % KB == KB - 1:
                    q = TC * ((u - 1) // PU) + (u - 1) % TC + 4
                    if q < 3 * TC:
                        rest(q)
                cols = slice(CW * c, CW * c + CW)
                bank, to = ps[:, u % 8, 0:CW], merged[:, b, cols]
                dve.wait_ge(gemm, u + 1)
                if s == 0:
                    v.tensor_copy(to, bank).then_inc(freed, 1)
                    dve.wait_ge(freed, u + 1)
                    continue
                if c == 0:
                    dve.wait_ge(sig_in[b % 2], 16 * ((KB * (s - 1) + b) // 2 + 1))
                first_op, second_op = (ALU.add, ALU.mult) if s == 1 else (ALU.mult, ALU.add)
                other = sig[:, b % 2, cols]
                v.tensor_tensor(part[:, u % 2, :], bank, to if s == 1 else other, first_op).then_inc(freed, 1)
                dve.wait_ge(freed, u + 1)
                v.tensor_tensor(to, part[:, u % 2, :], other if s == 1 else to, second_op).then_inc(done, 1)


def project_out(K, W, merged, source):
    nc, A, ps = K.nc, K.A, K.ps
    first = W.span["out"][0]
    with ExitStack() as ctx:
        def sb(name, shape, dt=F32):
            return ctx.enter_context(nc.sbuf_tensor(name, shape, dt))
        hi, lo = sb("o_hi", [P, KB, NT], F32R), sb("o_lo", [P, KB, NT], F32R)
        x = sb("o_x", [P, 9, D])
        gate = sb("o_gate", [P, 2, D])
        part = sb("o_part", [P, 2, 256])
        x_in, gate_in, gemm = K.sem("o_x_in"), K.sem("o_gate_in"), K.sem("o_sums")
        hi_done, split = K.sem("o_hi_done"), K.sem("o_split")
        part_done, added, out = K.sem("o_part_done"), K.sem("o_added"), K.sem("o_stored")
        block = ctx.enter_context(nc.Block())

        def token_cols(t):
            return slice(P * t, P * t + rows_of(t))

        @block.sync
        def _(sp):
            for b in range(2):
                r = P if b == 0 else DEC
                sp.dma_start(gate[0:r, b, :], A["s_gates"][b, 0:r, :]).then_inc(gate_in, 16)
            for t in range(9):
                sp.dma_start(x[0:rows_of(t), t, :], source(t)).then_inc(x_in, 16)
            W.load_stage(sp, "out")

        @block.gpsimd
        def _(pool):
            W.split_stage(pool, "out", lambda i: (gemm, 9 * (i + 1)))

        @block.scalar
        def _(act):
            for t in range(9):
                nc.scalar.copy(hi[:, :, token_cols(t)], merged[:, :, token_cols(t)]).then_inc(hi_done, 1)
            for t in range(9):
                act.wait_ge(added, 27 + t + 1)
                act.dma_start(A["s_x1"][P * t:P * t + rows_of(t), :], x[0:rows_of(t), t, :]).then_inc(out, 16)
            act.wait_ge(out, 16 * 9)

        @block.tensor
        def _(pe):
            for s in range(4):
                wh, wl = W.pair(first + s)
                pe.wait_ge(W.split, first + s + 1)
                for t in range(9):
                    u, cols = 9 * s + t, token_cols(t)
                    if s == 0:
                        pe.wait_ge(split, t + 1)
                    if u >= 8:
                        pe.wait_ge(part_done, u - 7)
                    product(nc, ps[0:rows_of(t), u % 8, 0:256], [(hi[:, k, cols], lo[:, k, cols], wh[:, k, :], wl[:, k, :])
                                                                 for k in range(KB)]).then_inc(gemm, 1)

        @block.vector
        def _(dve):
            v = nc.vector

            def rest(t):
                cols = token_cols(t)
                dve.wait_ge(hi_done, t + 1)
                v.tensor_tensor(lo[:, :, cols], merged[:, :, cols], hi[:, :, cols].bitcast(F32), ALU.subtract).then_inc(split, 1)

            rest(0)
            rest(1)
            dve.wait_ge(gate_in, 32)
            dve.wait_ge(x_in, 16 * 9)
            for s in range(4):
                for t in range(9):
                    r, u = rows_of(t), 9 * s + t
                    cols = slice(256 * s, 256 * s + 256)
                    if s == 0 and t + 2 < 9:
                        rest(t + 2)
                    dve.wait_ge(gemm, u + 1)
                    v.tensor_tensor(part[0:r, u % 2, :], ps[0:r, u % 8, 0:256], gate[0:r, t // TT, cols], ALU.mult)\
                        .then_inc(part_done, 1)
                    dve.wait_ge(part_done, u + 1)
                    v.tensor_tensor(x[0:r, t, cols], x[0:r, t, cols], part[0:r, u % 2, :], ALU.add).then_inc(added, 1)


def second_norm(K, W, x, hi, lo):
    nc, A, ps = K.nc, K.A, K.ps
    shift, scale = K.modT[:, 2, :, :], K.modT[:, 3, :, :]
    with ExitStack() as ctx:
        def sb(name, shape):
            return ctx.enter_context(nc.sbuf_tensor("n2" + name, shape, F32))
        xn = sb("xn", [P, 2, D])
        full = sb("full", [P, 2, KB, P])
        sq = sb("sq", [P, D])
        stat = sb("stat", [P, 4, 9])
        x_in, x_in_s = K.sem("n2x_in"), K.sem("n2x_in_odd")
        squared, mean, root, inv = K.sem("n2squared"), K.sem("n2mean"), K.sem("n2root"), K.sem("n2inv")
        scaled, turned, moved = K.sem("n2scaled"), K.sem("n2turned"), K.sem("n2moved")
        hi_done, split, extra = K.sem("n2hi"), K.sem("n2split"), K.sem("n2sample_step")
        x_ins = [x_in, x_in_s]
        block = ctx.enter_context(nc.Block())

        @block.sync
        def _(sp):
            for t in range(9):
                if t >= 2:
                    sp.wait_ge(squared, t - 1)
                sp.dma_start(x[0:rows_of(t), t, :], A["s_x1"][P * t:P * t + rows_of(t), :]).then_inc(x_ins[t % 2], 16)

        @block.scalar
        def _(act):
            def square(t):
                r = rows_of(t)
                act.wait_ge(x_ins[t % 2], 16 * (t // 2 + 1))
                if t:
                    act.wait_ge(squared, t)
                nc.scalar.activation(sq[0:r, :], x[0:r, t, :], ACT.Square,
                                     accum_out=stat[0:r, 0, t:t + 1]).then_inc(squared, 1)
                act.wait_ge(mean, t + 1)
                nc.scalar.activation(stat[0:r, 2, t:t + 1], stat[0:r, 1, t:t + 1], ACT.Sqrt).then_inc(root, 1)

            square(0)
            for t in range(TT):
                square(t + 1)
                if t >= 2:
                    act.wait_ge(split, t - 1)
                for h in range(2):
                    act.wait_ge(turned, 2 * t + h + 1)
                    for j in range(4):
                        k = 4 * h + j
                        mv = nc.scalar.activation(full[:, t % 2, k, :], ps[:, 2 * (t % 2) + h, P * j:P * j + P],
                                                  ACT.Identity, bias=shift[:, k, 0:1], scale=scale[:, k, 0:1])
                    mv.then_inc(moved, 1)

        @block.vector
        def _(dve):
            v = nc.vector

            def divide(t):
                r = rows_of(t)
                dve.wait_ge(squared, t + 1)
                v.tensor_scalar(stat[0:r, 1, t:t + 1], stat[0:r, 0, t:t + 1], 1.0 / D, EPS, ALU.mult, ALU.add).then_inc(mean, 1)
                dve.wait_ge(root, t + 1)
                v.reciprocal(stat[0:r, 3, t:t + 1], stat[0:r, 2, t:t + 1]).then_inc(inv, 1)
                dve.wait_ge(inv, t + 1)
                if t >= 2:
                    dve.wait_ge(turned, 2 * (t - 1))
                v.tensor_scalar(xn[0:r, t % 2, :], x[0:r, t, :], stat[0:r, 3, t:t + 1], None, ALU.mult).then_inc(scaled, 1)

            def part(t):
                cols = slice(P * t, P * t + P)
                dve.wait_ge(moved, 2 * t + 2)
                v.tensor_copy(hi[:, :, cols], full[:, t % 2]).then_inc(hi_done, 1)
                dve.wait_ge(hi_done, t + 1)
                v.tensor_tensor(lo[:, :, cols], full[:, t % 2], hi[:, :, cols].bitcast(F32), ALU.subtract).then_inc(split, 1)

            divide(0)
            divide(1)
            for t in range(2, 9):
                divide(t)
                part(t - 2)
            part(TT - 1)
            dve.wait_ge(turned, 2 * TT + 1)
            dve.wait_ge(split, TT - 1)
            hs, cols = full[:, 0, :, 0:DEC], slice(SEQ, NT)
            v.tensor_tensor(hs, ps[:, 4, 0:64].rearrange("p (k s) -> p k s", k=KB), scale[:, :, 1:9], ALU.mult).then_inc(extra, 1)
            dve.wait_ge(extra, 1)
            v.tensor_tensor(hs, hs, shift[:, :, 1:9], ALU.add).then_inc(extra, 1)
            dve.wait_ge(extra, 2)
            v.tensor_copy(hi[:, :, cols], hs).then_inc(extra, 1)
            dve.wait_ge(extra, 3)
            v.tensor_tensor(lo[:, :, cols], hs, hi[:, :, cols].bitcast(F32), ALU.subtract)

        @block.tensor
        def _(pe):
            for t in range(9):
                pe.wait_ge(scaled, t + 1)
                if t == TT:
                    for k in range(KB):
                        mm = nc.tensor.transpose(ps[:, 4, 8 * k:8 * k + 8], xn[0:DEC, t % 2, P * k:P * k + P],
                                                 K.ident[0:DEC, 0:DEC])
                    mm.then_inc(turned, 1)
                    break
                for h in range(2):
                    if t >= 2:
                        pe.wait_ge(moved, 2 * (t - 2) + h + 1)
                    for j in range(4):
                        k = 4 * h + j
                        mm = nc.tensor.transpose(ps[:, 2 * (t % 2) + h, P * j:P * j + P],
                                                 xn[:, t % 2, P * k:P * k + P], K.ident[:])
                    mm.then_inc(turned, 1)


def ffn(K, W, x, h_hi, h_lo):
    nc, A, ps = K.nc, K.A, K.ps
    first = W.span["ffn"][0]
    parts = ffn_parts()
    with ExitStack() as ctx:
        def sb(name, shape, dt=F32):
            return ctx.enter_context(nc.sbuf_tensor(name, shape, dt))
        a_hi, a_lo = sb("a_hi", [P, FPART, NT], F32R), sb("a_lo", [P, FPART, NT], F32R)
        silu, prod = sb("f_silu", [P, 2, CW]), sb("f_prod", [P, 2, CW])
        gate = sb("f_gate", [P, 2, D])
        fg = sb("final_g", [P, D])
        scaled = sb("f_scaled", [P, 2, 512])
        stat = sb("f_stat", [P, 4, 9])
        gate_in, g_in = K.sem("gate2_in"), K.sem("final_g_in")
        up, silu_done, act_done = K.sem("hidden_sums"), K.sem("silu_done"), K.sem("hidden_done")
        hi_done, split = K.sem("hidden_hi"), K.sem("hidden_split")
        down, free, added = K.sem("down_sums"), K.sem("down_bank_free"), K.sem("down_added")
        squared, mean, root, inv, done = (K.sem(n) for n in ("squared2", "mean2", "root2", "inv2", "y_done"))
        out = K.store_sem("y_stored")
        block = ctx.enter_context(nc.Block())

        @block.sync
        def _(sp):
            for b in range(2):
                r = P if b == 0 else DEC
                sp.dma_start(gate[0:r, b, :], A["s_gates"][2 + b, 0:r, :]).then_inc(gate_in, 16)
            sp.dma_start(fg[:], A["final_g"].partition_broadcast(P)).then_inc(g_in, 16)
            W.load_stage(sp, "ffn")
            for t in range(9):
                sp.wait_ge(done, t + 1)
                dst = A["y_prompt"][0, P * t:P * t + P, :] if t < TT else A["y_sample"][:, 0, :]
                sp.dma_start(dst, x[0:rows_of(t), t, :]).then_inc(out, 16)
            sp.wait_ge(out, 16 * 9)

        @block.gpsimd
        def _(pool):
            used, ups, downs = [], 0, 0
            for f0, nf in parts:
                used += [(up, ups + TC * (f + 1)) for f in range(nf)] + [(down, downs + 9), (down, downs + 18)]
                ups, downs = ups + TC * nf, downs + 18
            W.split_stage(pool, "ffn", used.__getitem__)

        @block.tensor
        def _(pe):
            n, i, d = first, 0, 0
            for f0, nf in parts:
                for f in range(nf):
                    pe.wait_ge(W.split, n + 1)
                    wh, wl = W.pair(n)
                    for c in range(TC):
                        cols = slice(CW * c, CW * c + CW)
                        if i >= 3:
                            pe.wait_ge(act_done, i - 2)
                        for h in range(2):
                            w = slice(P * h, P * h + P)
                            mm = product(nc, ps[:, 2 * (i % 3) + h, 0:CW], [
                                (wh[:, k, w], wl[:, k, w], h_hi[:, k, cols], h_lo[:, k, cols]) for k in range(KB)])
                        mm.then_inc(up, 1)
                        i += 1
                    n += 1
                for h in range(2):
                    pe.wait_ge(W.split, n + 1)
                    wh, wl = W.pair(n)
                    for t in range(9):
                        r, cols = rows_of(t), slice(P * t, P * t + rows_of(t))
                        if h == 0 and t in (0, 2, 5):
                            pe.wait_ge(split, i - TC + {0: 1, 2: 2, 5: 3}[t])
                        if d >= 2:
                            pe.wait_ge(free, d - 1)
                        product(nc, ps[0:r, 6 + d % 2, :], [
                            (a_hi[:, k, cols], a_lo[:, k, cols], wh[:, k, :], wl[:, k, :]) for k in range(nf)]).then_inc(down, 1)
                        d += 1
                    n += 1

        @block.scalar
        def _(act):
            for i in range(TC * FB):
                act.wait_ge(up, i + 1)
                if i >= 2:
                    act.wait_ge(act_done, i - 1)
                nc.scalar.activation(silu[:, i % 2, :], ps[:, 2 * (i % 3), 0:CW], ACT.Silu).then_inc(silu_done, 1)
            for t in range(9):
                r = rows_of(t)
                act.wait_ge(added, 18 * len(parts) - 9 + t + 1)
                if t:
                    act.wait_ge(squared, t)
                nc.scalar.activation(ps[0:r, 4:6, :].rearrange("p a n -> p (a n)"), x[0:r, t, :], ACT.Square,
                                     accum_out=stat[0:r, 0, t:t + 1]).then_inc(squared, 1)
                act.wait_ge(mean, t + 1)
                nc.scalar.activation(stat[0:r, 2, t:t + 1], stat[0:r, 1, t:t + 1], ACT.Sqrt).then_inc(root, 1)

        @block.vector
        def _(dve):
            v = nc.vector

            def final(t):
                r = rows_of(t)
                dve.wait_ge(squared, t + 1)
                v.tensor_scalar(stat[0:r, 1, t:t + 1], stat[0:r, 0, t:t + 1], 1.0 / D, EPS, ALU.mult, ALU.add).then_inc(mean, 1)
                dve.wait_ge(root, t + 1)
                v.reciprocal(stat[0:r, 3, t:t + 1], stat[0:r, 2, t:t + 1]).then_inc(inv, 1)
                dve.wait_ge(inv, t + 1)
                v.scalar_tensor_tensor(x[0:r, t, :], x[0:r, t, :], stat[0:r, 3, t:t + 1], fg[0:r, :],
                                       ALU.mult, ALU.mult).then_inc(done, 1)

            dve.wait_ge(gate_in, 32)
            dve.wait_ge(g_in, 16)
            i = d = 0
            for f0, nf in parts:
                for f in range(nf):
                    for c in range(TC):
                        cols = slice(CW * c, CW * c + CW)
                        dve.wait_ge(silu_done, i + 1)
                        v.tensor_tensor(prod[:, i % 2, :], ps[:, 2 * (i % 3) + 1, 0:CW], silu[:, i % 2, :], ALU.mult).then_inc(act_done, 1)
                        dve.wait_ge(act_done, i + 1)
                        if f0 and f == 0 and c == 0:
                            dve.wait_ge(down, d)
                        v.tensor_copy(a_hi[:, f, cols], prod[:, i % 2, :]).then_inc(hi_done, 1)
                        dve.wait_ge(hi_done, i + 1)
                        v.tensor_tensor(a_lo[:, f, cols], prod[:, i % 2, :], a_hi[:, f, cols].bitcast(F32), ALU.subtract).then_inc(split, 1)
                        i += 1
                last = f0 + nf == FB
                for h in range(2):
                    for t in range(9):
                        r, cols = rows_of(t), slice(512 * h, 512 * h + 512)
                        dve.wait_ge(down, d + 1)
                        v.tensor_tensor(scaled[0:r, d % 2, :], ps[0:r, 6 + d % 2, :], gate[0:r, t // TT, cols], ALU.mult).then_inc(free, 1)
                        dve.wait_ge(free, d + 1)
                        if d >= 9:
                            dve.wait_ge(added, d - 8)
                        v.tensor_tensor(x[0:r, t, cols], x[0:r, t, cols], scaled[0:r, d % 2, :], ALU.add).then_inc(added, 1)
                        d += 1
                        if last and h and t:
                            final(t - 1)
            final(8)


def program(nc, A):
    K = Chip()
    K.nc, K.A = nc, A
    K.slabs, K.span = weight_slabs(A)
    A["s_sig"] = nc.dram_tensor("s_sig", (2 * KB, P, NT), F32, kind="Internal").ap()
    A["s_att"] = nc.dram_tensor("s_att", (KB, P, NT), F32, kind="Internal").ap()
    A["s_ssm"] = nc.dram_tensor("s_ssm", (2 * KB, P, SEQ), F32, kind="Internal").ap()
    A["s_x1"] = nc.dram_tensor("s_x1", (NT, D), F32, kind="Internal").ap()
    A["s_xbc"] = nc.dram_tensor("s_xbc", (6, P, NT), F32, kind="Internal").ap()
    A["s_mod"] = nc.dram_tensor("s_mod", (9, 4 * D), F32, kind="Internal").ap()
    A["s_gates"] = nc.dram_tensor("s_gates", (4, P, D), F32, kind="Internal").ap()
    with ExitStack() as ctx:
        def sb(name, shape, into=None):
            return (into or ctx).enter_context(nc.sbuf_tensor(name, shape, F32))
        K.lent = []
        kept = lambda name: ctx.enter_context(nc.semaphore(name))

        def lend(name):
            K.lent.append(nc.alloc_semaphore(name=name))
            return K.lent[-1]

        def retire():
            with nc.Block() as block:
                @block.sync
                def _(sp):
                    for s in K.lent:
                        sp.sem_clear(s)
            for s in reversed(K.lent):
                nc.release_semaphore(s)
            K.lent = []

        K.sem = lend
        stores = {n: kept(n) for n in (
            "ki_stored", "k_stored", "v_stored", "tail_rows_stored", "states_stored", "final_stored",
            "old_conv_rows_stored", "y_stored", "gate_out0", "gate_out1", "conv_state_in", "states_in",
            "ssm_yT_stored0", "ssm_yT_stored1",
            "mod_stored0", "mod_stored1")}
        K.store_sem = stores.__getitem__
        K.ps = ctx.enter_context(nc.psum_tensor("ps", [P, 8, 512], F32))
        K.landed = [kept(f"slab_landed{i}") for i in range(RING)]
        K.ident_in, K.const_in = kept("ident_in"), kept("const_in")
        K.ident = sb("ident", [P, P])
        K.vecs = sb("vecs", [P, 152])
        K.modT = sb("modT", [P, 4, KB, 9])
        K.cT = sb("cT", [P, KB, 9])
        K.ysT = sb("ysT", [P, INNER // P, DEC])
        xp, xs = A["x_prompt"][0], A["x_sample"][:, 0]

        def x_tile(t):
            return xp[P * t:P * t + P, :] if t < TT else xs

        with ExitStack() as first:
            K.ring = sb("ring", [P, RING, SLAB], first)
            K.le, K.gt, K.ones, K.diag_off = (sb(n, [P, P], first) for n in ("le", "gt", "ones", "diag_off"))
            K.heads_row, K.heads_col = sb("heads_row", [P, 3, HEADS], first), sb("heads_col", [HEADS, 3], first)
            K.dt_raw, K.dtT_raw = sb("dt_raw", [P, TT, HEADS], first), sb("dtT_raw", [HEADS, DEC], first)
            modulation(K)
            hT = sb("hT", [P, KB, NT], first)
            norm_stage(K, "n1", 0, hT, x_tile)
            with ExitStack() as att:
                T = Chip()
                T.qT = sb("qT", [P, KB, NT], att)
                T.v = sb("v", [P, TT + 1, KVH * HD], att)
                T.wi = sb("wi", [P, TT + 1, IH], att)
                T.q_s, T.k_s = sb("q_s", [DEC, D], att), sb("k_s", [DEC, KVH * HD], att)
                T.qi_s, T.ki_s = sb("qi_s", [DEC, IH * HD], att), sb("ki_s", [DEC, HD], att)
                T.dt_raw, T.dtT_raw = K.dt_raw, K.dtT_raw
                with ExitStack() as keys:
                    T.kT = sb("kT", [P, KVH, SEQ], keys)
                    T.bias = keys.enter_context(nc.sbuf_tensor("sel_bias", [P, BIAS_AT[TT]], BF16))
                    with ExitStack() as index:
                        T.kiT, T.qiT = sb("kiT", [P, SEQ], index), sb("qiT", [P, 2, SEQ], index)
                        with ExitStack() as rope:
                            K.cos, K.sin = (sb(n, [P, TT + 1, HD], rope) for n in ("cos", "sin"))
                            project(K, hT, T)
                        select(K, hT, T)
                    attend(K, T)
                attend_samples(K, T)
            retire()
            with ExitStack() as rec:
                S = Chip()
                S.dt, S.dta, S.ddt, S.e_acs, S.c_dec = (sb("s_" + n, [P, TT, HEADS], rec) for n in ("dt", "dta", "ddt", "e", "c"))
                S.hx = sb("s_hx", [P, INNER // P, 17], rec)
                S.ysT = K.ysT
                steps(K, S)
                ssm(K, hT, S)
            retire()
        with ExitStack() as second:
            W = SplitRing(K, second, lambda name: second.enter_context(nc.semaphore(name)))
            with ExitStack() as mix:
                merged = sb("merged", [P, KB, NT], mix)
                merge(K, W, merged)
                project_out(K, W, merged, x_tile)
            with ExitStack() as mlp:
                x1 = sb("x1", [P, 9, D], mlp)
                h_hi, h_lo = (mlp.enter_context(nc.sbuf_tensor(n, [P, KB, NT], F32R)) for n in ("h_hi", "h_lo"))
                second_norm(K, W, x1, h_hi, h_lo)
                ffn(K, W, x1, h_hi, h_lo)


_INS = ["x_prompt", "x_sample", "cache_k", "cache_v", "cache_kidx", "state_conv", "state_ssm", "page_table",
        "c_prompt", "c_sample", "w_ada", "b_ada", "norm1_g", "w_in", "conv_w", "conv_b", "dt_bias", "a_log",
        "d_skip", "ssm_norm_g", "w_proj_ssm", "w_proj_attn", "w_out", "norm2_g", "w_ffn_in", "w_ffn_out", "final_g"]
_OUTS = [("y_prompt", (1, SEQ, D)), ("y_sample", (DEC, 1, D)),
         ("k_prompt", (1, 1, SEQ, KVH, HD)), ("v_prompt", (1, 1, SEQ, KVH, HD)), ("kidx_prompt", (1, 1, SEQ, HD)),
         ("conv_prompt", (1, 1, CONV - 1, XBC)), ("ssm_prompt", (1, 1, HEADS, HD, NST)),
         ("k_sample", (1, DEC, 1, KVH, HD)), ("v_sample", (1, DEC, 1, KVH, HD)), ("kidx_sample", (1, DEC, 1, HD)),
         ("conv_sample", (1, DEC, CONV - 1, XBC)), ("ssm_sample", (1, DEC, HEADS, HD, NST))]


def shape_constants():
    import numpy as np
    i = np.arange(P)
    f = np.float32
    half = HD // 2
    inv = f(10000.0) ** (-np.arange(half, dtype=f) / f(half))
    pos = np.concatenate([np.arange(SEQ), np.full(P, PAST)]).astype(f)
    ang = (pos[:, None] * inv[None, :]).astype(f)
    cos, sin = np.cos(ang).astype(f), np.sin(ang).astype(f)
    tiled = lambda a: np.ascontiguousarray(a.reshape(TT + 1, P, HD).transpose(1, 0, 2))
    return {
        "k_ident": np.eye(P, dtype=f),
        "k_le": (i[:, None] <= i[None, :]).astype(f),
        "k_gt": (i[:, None] > i[None, :]).astype(f),
        "k_ones": np.ones((P, P), f),
        "k_diag_off": np.where(i[None, :] <= i[:, None], f(0), f(OFF)).astype(f),
        "k_diag_far": np.where(i[None, :] <= i[:, None], f(0), f(FAR)).astype(f),
        "k_cos": tiled(np.concatenate([cos, cos], 1)),
        "k_sin": tiled(np.concatenate([-sin, sin], 1)),
        "k_head": (np.arange(HEADS)[:, None] == np.arange(INNER)[None, :] // HD).astype(f),
        "k_who": (np.arange(DEC)[:, None] == i[None, :] // AH).astype(f),
    }


def kernel(**inputs):
    import numpy as _np
    import concourse.bacc as _bacc
    from concourse import mybir as _mybir
    from concourse.bass_utils import run_bass_kernel_spmd as _run

    nc = _bacc.Bacc("TRN2", target_bir_lowering=False, num_devices=1)
    arrays, A = {}, {}
    given = {n: _np.ascontiguousarray(inputs[n]) for n in _INS}
    given.update(shape_constants())
    for name, a in given.items():
        arrays[f"in_{name}"] = a
        A[name] = nc.dram_tensor(f"in_{name}", a.shape, _mybir.dt.from_np(a.dtype), kind="ExternalInput").ap()
    for name, shape in _OUTS:
        A[name] = nc.dram_tensor(f"out_{name}", shape, F32, kind="ExternalOutput").ap()
    program(nc, A)
    r = _run(nc, [arrays], core_ids=[0])
    return tuple(r.results[0][f"out_{name}"] for name, _ in _OUTS)
```
